# Optimizing a Trainium2 kernel written in Bass

```python
import math
import jax, jax.numpy as jnp
from jax import lax
import numpy as np

D_MODEL = 1024
BATCH = 1
SEQ = 512
DEPTH = 1
DEC_BATCH = 8
DEC_SEQ = 8
PAST_LEN = 4096
PAGE_SIZE = 128

MLA_HEADS = 16
QK_NOPE = 64
QK_ROPE = 32
QK_DIM = QK_NOPE + QK_ROPE
V_DIM = 64
Q_LORA = 384
KV_LORA = 256
ROPE_THETA = 10000.0
Q_BLOCK = 128
MLA_WIDTH = MLA_HEADS * V_DIM
SCALE = QK_DIM ** -0.5
RW_HEADS = 16
RW_HEAD = 64
RW_WIDTH = RW_HEADS * RW_HEAD
DECAY_LORA = 64
A_LORA = 64
N_SHIFT = 3 * RW_WIDTH + DECAY_LORA + A_LORA
RMS_EPS = 1e-6
GN_EPS = 64e-5
SPLITS = (Q_LORA, KV_LORA, QK_ROPE, MLA_WIDTH, N_SHIFT, RW_WIDTH, D_MODEL, D_MODEL)
N_IN = Q_LORA + KV_LORA + QK_ROPE + MLA_WIDTH + N_SHIFT + RW_WIDTH + 2 * D_MODEL

kernel_name = "mla_rwkv7_gated_hybrid_step"

def _rms(x):
    xf = x.astype(jnp.float32)
    return (xf * lax.rsqrt(jnp.mean(xf * xf, -1, keepdims=True) + RMS_EPS)).astype(x.dtype)

def _rope(x, pos):
    half = QK_ROPE // 2
    inv = ROPE_THETA ** (-jnp.arange(half, dtype=jnp.float32) / half)
    ang = pos.astype(jnp.float32)[:, None] * inv[None, :]
    shape = (1, ang.shape[0]) + (1,) * (x.ndim - 3) + (half,)
    cos = jnp.cos(ang).reshape(shape).astype(x.dtype)
    sin = jnp.sin(ang).reshape(shape).astype(x.dtype)
    x1, x2 = x[..., :half], x[..., half:]
    return jnp.concatenate([x1 * cos - x2 * sin, x1 * sin + x2 * cos], -1)

def _split(cols):
    out, i = [], 0
    for s in SPLITS:
        out.append(cols[..., i:i + s])
        i += s
    return out

def _front(x, c, w_ada, b_ada, g_norm, w_in):
    mod = jnp.dot(jax.nn.silu(c), w_ada) + b_ada
    shift, scale, gate = jnp.split(mod, 3, axis=-1)
    h = _rms(x) * g_norm * (1 + scale[:, None, :]) + shift[:, None, :]
    cols = jnp.einsum('btd,dn->btn', h, w_in)
    return _split(cols), gate

def _mla_query_latent(qa, kva, pos, g_qa, w_uq, g_kva, g_q):
    q = jnp.einsum('btr,rhd->bthd', _rms(qa) * g_qa, w_uq)
    q = _rms(q) * g_q
    q = jnp.concatenate([q[..., :QK_NOPE], _rope(q[..., QK_NOPE:], pos)], -1)
    c_lat = _rms(kva) * g_kva
    return q, c_lat

def _mla_keys(c_lat, kpe_raw, pos, w_uk, g_k):
    k_nope = jnp.einsum('btr,rhd->bthd', c_lat, w_uk)
    kn = k_nope.astype(jnp.float32)
    kp = kpe_raw.astype(jnp.float32)
    ms = (jnp.sum(kn * kn, -1) + jnp.sum(kp * kp, -1)[..., None]) / QK_DIM
    k_inv = lax.rsqrt(ms + RMS_EPS).astype(c_lat.dtype)
    k_pe = _rope(kpe_raw * g_k[QK_NOPE:], pos)
    return k_nope, k_pe, k_inv

def _prompt_attention(q, k, v):
    B, S, H, _ = q.shape
    nb = S // Q_BLOCK
    qb = jnp.moveaxis(q.reshape(B, nb, Q_BLOCK, H, QK_DIM), 1, 0)
    kpos = jnp.arange(S)

    def blk(args):
        qi, i = args
        s = jnp.einsum('bqhd,bkhd->bhqk', qi, k).astype(jnp.float32) * SCALE
        qpos = i * Q_BLOCK + jnp.arange(Q_BLOCK)
        s = jnp.where(kpos[None, :] <= qpos[:, None], s, -jnp.inf)
        p = jax.nn.softmax(s, axis=-1).astype(v.dtype)
        return jnp.einsum('bhqk,bkhd->bqhd', p, v)

    o = lax.map(blk, (qb, jnp.arange(nb)))
    return jnp.moveaxis(o, 0, 1).reshape(B, S, H * V_DIM)

def _sample_attention(q, c_new, kpe_new, kinv_new, cache_kv, cache_kpe, cache_kinv, page_table, w_uk, w_uv, g_k):
    Bd, T = q.shape[:2]
    L = page_table.shape[1] * PAGE_SIZE
    q_lat = jnp.einsum('bthd,rhd->bthr', q[..., :QK_NOPE] * g_k[:QK_NOPE], w_uk)
    q_pe = q[..., QK_NOPE:]
    allowed = jnp.concatenate([jnp.ones((T, L), bool), jnp.tril(jnp.ones((T, T), bool))], axis=1)

    def one(args):
        pt, ql, qp, cn, kn, sn = args
        c_all = jnp.concatenate([cache_kv[pt].reshape(L, KV_LORA).astype(cn.dtype), cn], 0)
        kp_all = jnp.concatenate([cache_kpe[pt].reshape(L, QK_ROPE).astype(kn.dtype), kn], 0)
        ki_all = jnp.concatenate([cache_kinv[pt].reshape(L, MLA_HEADS).astype(sn.dtype), sn], 0)
        s = (jnp.einsum('thr,kr->htk', ql, c_all) + jnp.einsum('thr,kr->htk', qp, kp_all)).astype(jnp.float32)
        s = s * ki_all.T[:, None, :].astype(jnp.float32) * SCALE
        s = jnp.where(allowed[None], s, -jnp.inf)
        p = jax.nn.softmax(s, axis=-1).astype(c_all.dtype)
        o_lat = jnp.einsum('htk,kr->thr', p, c_all)
        return jnp.einsum('thr,rhd->thd', o_lat, w_uv)

    o = lax.map(one, (page_table, q_lat, q_pe, c_new, kpe_new, kinv_new))
    return o.reshape(Bd, T, MLA_HEADS * V_DIM)

def _wkv_scan(S0, r, decay, k, v, kk, a):
    def step(S, inp):
        r_t, d_t, k_t, v_t, kk_t, a_t = inp
        Sk = jnp.einsum('bhij,bhj->bhi', S, kk_t)
        S = S * d_t[:, :, None, :] - Sk[..., None] * (kk_t * a_t)[:, :, None, :] + v_t[..., None] * k_t[:, :, None, :]
        return S, jnp.einsum('bhij,bhj->bhi', S, r_t)

    xs = tuple(jnp.moveaxis(t.astype(jnp.float32), 1, 0) for t in (r, decay, k, v, kk, a))
    S, o = lax.scan(step, S0.astype(jnp.float32), xs)
    return S, jnp.moveaxis(o, 0, 1)

def _rwkv(p, z, shift0, S0, mu_shift, w0, w_decay2, a0, w_a2, k_k, k_a, r_k, gn_g, gn_b):
    B, T, _ = p.shape
    prev = jnp.concatenate([shift0[:, None, :].astype(p.dtype), p[:, :-1]], axis=1)
    xs = p + (prev - p) * mu_shift
    o1 = RW_WIDTH
    o2 = o1 + DECAY_LORA
    o3 = o2 + RW_WIDTH
    o4 = o3 + RW_WIDTH
    r, wl, k, v, al = xs[..., :o1], xs[..., o1:o2], xs[..., o2:o3], xs[..., o3:o4], xs[..., o4:]
    w = -jax.nn.softplus(-(w0 + jnp.tanh(wl) @ w_decay2)) - 0.5
    decay = jnp.exp(-jnp.exp(w.astype(jnp.float32)))
    a = jax.nn.sigmoid(a0 + al @ w_a2)
    hs = lambda t: t.reshape(B, T, RW_HEADS, RW_HEAD)
    r, k, v, a, decay = hs(r), hs(k), hs(v), hs(a), hs(decay)
    kk = (k * k_k.reshape(RW_HEADS, RW_HEAD)).astype(jnp.float32)
    kk = kk * lax.rsqrt(jnp.maximum(jnp.sum(kk * kk, -1, keepdims=True), 1e-24))
    k = k * (1 + (a - 1) * k_a.reshape(RW_HEADS, RW_HEAD))
    S, o = _wkv_scan(S0, r, decay, k, v, kk, a)
    mean = jnp.mean(o, -1, keepdims=True)
    var = jnp.mean(jnp.square(o - mean), -1, keepdims=True)
    o = ((o - mean) * lax.rsqrt(var + GN_EPS)).astype(p.dtype)
    o = o * gn_g.reshape(RW_HEADS, RW_HEAD) + gn_b.reshape(RW_HEADS, RW_HEAD)
    o = o + jnp.sum(r * k * r_k, -1, keepdims=True) * v
    o = o.reshape(B, T, RW_WIDTH) * jax.nn.silu(z)
    return o, S, p[:, -1]

def _merge(x, gate, o_a, o_b, g_a, g_b, w_pa, w_pb, w_out):
    m = jax.nn.sigmoid(g_a) * (o_a @ w_pa) + jax.nn.sigmoid(g_b) * (o_b @ w_pb)
    return x + gate[:, None, :] * (m @ w_out)

def setup_inputs(seed: int = 0) -> dict:
    key = jax.random.key(seed)
    ks = list(jax.random.split(key, 40))
    nrm = lambda shape, s: jax.random.normal(ks.pop(), shape, jnp.float32) * s
    n_pages = PAST_LEN // PAGE_SIZE
    n_phys = (5 * DEC_BATCH * n_pages) // 4
    perm = jax.random.permutation(ks.pop(), n_phys)
    page_table = perm[:DEC_BATCH * n_pages].reshape(DEC_BATCH, n_pages).astype(jnp.int32)
    return {
        "x_prompt": nrm((BATCH, SEQ, D_MODEL), 1.0),
        "x_sample": nrm((DEC_BATCH, DEC_SEQ, D_MODEL), 1.0),
        "c_prompt": nrm((BATCH, D_MODEL), 1.0),
        "c_sample": nrm((DEC_BATCH, D_MODEL), 1.0),
        "cache_kv": nrm((n_phys, PAGE_SIZE, KV_LORA), 1.0),
        "cache_kpe": nrm((n_phys, PAGE_SIZE, QK_ROPE), 1.0),
        "cache_kinv": jax.random.uniform(ks.pop(), (n_phys, PAGE_SIZE, MLA_HEADS), jnp.float32, 0.7, 1.3),
        "state_wkv": nrm((DEC_BATCH, RW_HEADS, RW_HEAD, RW_HEAD), 0.3),
        "state_shift": nrm((DEC_BATCH, N_SHIFT), 1.0),
        "page_table": page_table,
        "w_ada": nrm((D_MODEL, 3 * D_MODEL), 0.5 * D_MODEL ** -0.5),
        "b_ada": nrm((3 * D_MODEL,), 0.01),
        "g_norm": 1.0 + nrm((D_MODEL,), 0.01),
        "w_in": nrm((D_MODEL, N_IN), D_MODEL ** -0.5),
        "g_qa": 1.0 + nrm((Q_LORA,), 0.01),
        "w_uq": nrm((Q_LORA, MLA_HEADS, QK_DIM), Q_LORA ** -0.5),
        "g_kva": 1.0 + nrm((KV_LORA,), 0.01),
        "w_uk": nrm((KV_LORA, MLA_HEADS, QK_NOPE), KV_LORA ** -0.5),
        "w_uv": nrm((KV_LORA, MLA_HEADS, V_DIM), KV_LORA ** -0.5),
        "g_q": 1.0 + nrm((QK_DIM,), 0.01),
        "g_k": 1.0 + nrm((QK_DIM,), 0.01),
        "w_pa": nrm((MLA_WIDTH, D_MODEL), MLA_WIDTH ** -0.5),
        "mu_shift": jax.random.uniform(ks.pop(), (N_SHIFT,), jnp.float32),
        "w0": jax.random.uniform(ks.pop(), (RW_WIDTH,), jnp.float32, -3.0, 1.0),
        "w_decay2": nrm((DECAY_LORA, RW_WIDTH), 0.1),
        "a0": nrm((RW_WIDTH,), 0.1),
        "w_a2": nrm((A_LORA, RW_WIDTH), 0.1),
        "k_k": 1.0 + nrm((RW_WIDTH,), 0.1),
        "k_a": 1.0 + nrm((RW_WIDTH,), 0.1),
        "r_k": nrm((RW_HEADS, RW_HEAD), 0.1),
        "gn_g": 1.0 + nrm((RW_WIDTH,), 0.01),
        "gn_b": nrm((RW_WIDTH,), 0.01),
        "w_pb": nrm((RW_WIDTH, D_MODEL), RW_WIDTH ** -0.5),
        "w_out": nrm((D_MODEL, D_MODEL), D_MODEL ** -0.5),
    }

def reference(x_prompt, x_sample, c_prompt, c_sample, cache_kv, cache_kpe, cache_kinv, state_wkv, state_shift,
              page_table, w_ada, b_ada, g_norm, w_in, g_qa, w_uq, g_kva, w_uk, w_uv, g_q, g_k, w_pa, mu_shift, w0,
              w_decay2, a0, w_a2, k_k, k_a, r_k, gn_g, gn_b, w_pb, w_out):
    B, S, _ = x_prompt.shape
    Bd, T, _ = x_sample.shape
    past = page_table.shape[1] * PAGE_SIZE

    pos_p = jnp.arange(S)
    (qa, kva, kpe_raw, z_a, p_sh, z_b, g_a, g_b), gate = _front(x_prompt, c_prompt, w_ada, b_ada, g_norm, w_in)
    q, kv_p = _mla_query_latent(qa, kva, pos_p, g_qa, w_uq, g_kva, g_q)
    k_nope, kpe_p, kinv_p = _mla_keys(kv_p, kpe_raw, pos_p, w_uk, g_k)
    keys = jnp.concatenate([k_nope * g_k[:QK_NOPE],
                            jnp.broadcast_to(kpe_p[:, :, None, :], (B, S, MLA_HEADS, QK_ROPE))], -1) * kinv_p[..., None]
    vals = jnp.einsum('btr,rhd->bthd', kv_p, w_uv)
    o_a = _prompt_attention(q, keys, vals) * jax.nn.silu(z_a)
    o_b, wkv_p, shift_p = _rwkv(p_sh, z_b, jnp.zeros((B, N_SHIFT), x_prompt.dtype),
                                jnp.zeros((B, RW_HEADS, RW_HEAD, RW_HEAD), jnp.float32),
                                mu_shift, w0, w_decay2, a0, w_a2, k_k, k_a, r_k, gn_g, gn_b)
    y_prompt = _merge(x_prompt, gate, o_a, o_b, g_a, g_b, w_pa, w_pb, w_out)

    pos_s = past + jnp.arange(T)
    (qa_s, kva_s, kpe_raw_s, z_a_s, p_sh_s, z_b_s, g_a_s, g_b_s), gate_s = _front(x_sample, c_sample, w_ada, b_ada,
                                                                                 g_norm, w_in)
    q_s, kv_s = _mla_query_latent(qa_s, kva_s, pos_s, g_qa, w_uq, g_kva, g_q)
    _, kpe_s, kinv_s = _mla_keys(kv_s, kpe_raw_s, pos_s, w_uk, g_k)
    o_a_s = _sample_attention(q_s, kv_s, kpe_s, kinv_s, cache_kv, cache_kpe, cache_kinv, page_table,
                              w_uk, w_uv, g_k) * jax.nn.silu(z_a_s)
    o_b_s, wkv_s, shift_s = _rwkv(p_sh_s, z_b_s, state_shift, state_wkv,
                                  mu_shift, w0, w_decay2, a0, w_a2, k_k, k_a, r_k, gn_g, gn_b)
    y_sample = _merge(x_sample, gate_s, o_a_s, o_b_s, g_a_s, g_b_s, w_pa, w_pb, w_out)

    return (y_prompt, y_sample, kv_p, kpe_p, kinv_p, wkv_p.astype(x_prompt.dtype), shift_p,
            kv_s, kpe_s, kinv_s, wkv_s.astype(x_sample.dtype), shift_s)


_drawn_inputs = setup_inputs


def setup_inputs(seed=0):
    import zlib

    import numpy as np

    out = dict(_drawn_inputs(seed))
    spreads = {}
    factors = {'cache_kv': 8.0,
     'cache_kpe': 8.0,
     'cache_kinv': 8.0,
     'g_norm': 4.614,
     'g_qa': 8.0,
     'w_uq': 4.769,
     'g_kva': 29.376,
     'g_q': 8.0,
     'g_k': 5.958,
     'gn_g': 64.0,
     'gn_b': 64.0}
    for name, (base, spread) in spreads.items():
        noise = np.random.default_rng([zlib.crc32(name.encode()), seed]).standard_normal(out[name].shape)
        drawn = base * np.exp(spread * noise) if base else spread * noise
        out[name] = __import__('jax').numpy.asarray(drawn.astype(out[name].dtype))
    for name, factor in factors.items():
        out[name] = (out[name] * factor).astype(out[name].dtype)
    return out
```

```python
import numpy as np
import concourse.bass as bass
from concourse import mybir
from contextlib import ExitStack

F32 = mybir.dt.float32
I32 = mybir.dt.int32
ALU = mybir.AluOpType
ACT = mybir.ActivationFunctionType
AX = mybir.AxisListType

P = 128
D = 1024
KT = D // P
SEQ = 512
PB = SEQ // P
NB = PB + 1
TOK = NB * P
BD = 8
TD = 8
SB = BD * TD
H = 16
NP = H // 2
NOPE, ROPE, QK = 64, 32, 96
VD = 64
QL, KL = 384, 256
MW = H * VD
RH = 64
NSH = 3 * 1024 + 64 + 64
PAGES = 32
PS = 128
SCALE = QK ** -0.5
EPS = 1e-6
GN_EPS = 64e-5
HALF = ROPE // 2
C_QA, C_KVA, C_KPE = 0, QL, QL + KL
C_ZA = QL + KL + ROPE
C_SH = C_ZA + MW
C_ZB = C_SH + NSH
C_GA = C_ZB + 1024
C_GB = C_GA + D
LAT = C_ZA
S_R, S_WL, S_K, S_V, S_AL = 0, 1024, 1088, 2112, 3136
NEG = -1e30
LD = -float(np.exp(-0.5))


def bc(ap, n, at):
    return ap.unsqueeze(at).to_broadcast(list(ap.shape[:at]) + [n] + list(ap.shape[at:]))


def adaln(nc, I, M):
    with ExitStack() as ctx:
        sb = lambda name, shape: ctx.enter_context(nc.sbuf_tensor("ad_" + name, shape, F32))
        ps = lambda name: ctx.enter_context(nc.psum_tensor("ad_" + name, [P, 512], F32))
        sem = lambda name: nc.alloc_semaphore(name)
        R = 1 + BD
        NT = 3 * D // 512
        crow, esil, cT = sb("crow", [R, D]), sb("esil", [R, D]), sb("cT", [P, KT, R])
        bada, gnorm, mod = sb("bada", [R, 3 * D]), sb("gnorm", [R, D]), sb("mod", [R, 3 * D])
        sel = sb("sel_ada", [R, 2 * P])
        wada = [sb(f"wada{i}", [P, KT, 512]) for i in range(2)]
        psC, psM = ps("psC"), [ps("psM0"), ps("psM1")]
        psS = [ps(f"psS{i}") for i in range(4)]
        small_in, c_exp, c_silu, c_tr, c_sb = sem("small_in"), sem("c_exp"), sem("c_silu"), sem("c_tr"), sem("c_sb")
        w_in_sb = [sem("wada_in0"), sem("wada_in1")]
        mm, ev, rows, spread, spread_sb = sem("mod_mm"), sem("mod_ev"), sem("mod_rows"), sem("spread"), sem("spread_sb")
        w_v = I["w_ada"].rearrange("(k p) n -> p k n", p=P)
        block = ctx.enter_context(nc.Block())

        @block.sync
        def _(sp):
            sp.dma_start(crow[0:1, :], I["c_prompt"]).then_inc(small_in, 16)
            sp.dma_start(crow[1:R, :], I["c_sample"]).then_inc(small_in, 16)
            sp.dma_start(bada[:, :], bc(I["b_ada"], R, 0)).then_inc(small_in, 16)
            sp.dma_start(gnorm[:, :], bc(I["g_norm"], R, 0)).then_inc(small_in, 16)
            sp.dma_start(sel[:, :], I["sel"]).then_inc(small_in, 16)
            sp.dma_start(M.ident[:, :], I["ident"]).then_inc(small_in, 16)
            for b in range(2):
                sp.dma_start(wada[b][:, :, :], w_v[:, :, b * 512:(b + 1) * 512]).then_inc(w_in_sb[b], 16)
            with sp.Fori(1, NT // 2) as i:
                for b in range(2):
                    sp.wait_ge(mm, 2 * i + b - 1)
                    sp.dma_start(wada[b][:, :, :], w_v[:, :, bass.ds(i * 1024 + b * 512, 512)]).then_inc(w_in_sb[b], 16)

        @block.gpsimd
        def _(pool):
            nc.gpsimd.memset(M.ones[:, :], 1.0)

        @block.scalar
        def _(act):
            act.wait_ge(small_in, 96)
            nc.scalar.activation(esil[:, :], crow[:, :], ACT.Exp, scale=-1.0).then_inc(c_exp, 1)
            for i in range(4):
                act.wait_ge(spread, 2 * (i + 1))
                dst = (M.G1, M.SH)[i % 2]
                nc.scalar.copy(dst[:, i // 2, 0:512], psS[2 * (i % 2)][:, :])
                nc.scalar.copy(dst[:, i // 2, 512:D], psS[2 * (i % 2) + 1][:, :]).then_inc(spread_sb, 1)

        @block.tensor
        def _(pe):
            pe.wait_ge(c_silu, 1)
            for k in range(KT):
                last = nc.tensor.transpose(psC[:, k * R:(k + 1) * R], crow[:, k * P:(k + 1) * P], M.ident[0:R, 0:R])
            last.then_inc(c_tr, 1)
            pe.wait_ge(c_sb, 1)
            with pe.Fori(0, NT // 2) as i:
                for b in range(2):
                    pe.wait_ge(w_in_sb[b], i * 16 + 16)
                    pe.wait_ge(ev, 2 * i)
                    for k in range(KT):
                        last = nc.tensor.matmul(psM[b][0:R, :], cT[:, k, :], wada[b][:, k, :], start=(k == 0), stop=(k == KT - 1))
                    last.then_inc(mm, 1)
            pe.wait_ge(rows, 1)
            for i in range(4):
                if i >= 2:
                    pe.wait_ge(spread_sb, i - 1)
                src = mod[:, D:2 * D] if i % 2 == 0 else mod[:, 0:D]
                for n in range(2):
                    nc.tensor.matmul(psS[2 * (i % 2) + n][:, :], sel[:, (i // 2) * P:(i // 2 + 1) * P],
                                     src[:, n * 512:(n + 1) * 512], start=True, stop=True).then_inc(spread, 1)

        @block.vector
        def _(dve):
            dve.wait_ge(c_exp, 1)
            nc.vector.tensor_scalar(esil[:, :], esil[:, :], 1.0, None, ALU.add)
            dve.drain()
            nc.vector.reciprocal(esil[:, :], esil[:, :])
            dve.drain()
            nc.vector.tensor_tensor(crow[:, :], crow[:, :], esil[:, :], ALU.mult).then_inc(c_silu, 1)
            dve.wait_ge(c_tr, 1)
            nc.vector.tensor_copy(cT[:, :, :], psC[:, 0:KT * R].rearrange("p (k r) -> p k r", r=R)).then_inc(c_sb, 1)
            with dve.Fori(0, NT // 2) as i:
                for b in range(2):
                    dve.wait_ge(mm, 2 * i + b + 1)
                    cols = bass.ds(i * 1024 + b * 512, 512)
                    nc.vector.tensor_tensor(mod[:, cols], psM[b][0:R, :], bada[:, cols], ALU.add).then_inc(ev, 1)
            dve.drain()
            nc.vector.tensor_copy(M.gate[:, :], mod[:, 2 * D:3 * D])
            nc.vector.scalar_tensor_tensor(mod[:, D:2 * D], mod[:, D:2 * D], 1.0, gnorm[:, :], ALU.add, ALU.mult).then_inc(rows, 1)


def front(nc, I, O, M):
    with ExitStack() as ctx:
        sb = lambda name, shape: ctx.enter_context(nc.sbuf_tensor("fr_" + name, shape, F32))
        ps = lambda name: ctx.enter_context(nc.psum_tensor("fr_" + name, [P, 512], F32))
        sem = lambda name: nc.alloc_semaphore(name)
        wl = sb("w_lat", [P, KT, LAT])
        wuq, wuk, wuv = sb("wuq", [P, 3, H * QK]), sb("wuk", [P, 2, MW]), sb("wuv", [P, 2, MW])
        gqa, gkva, gq, gk = sb("gqa", [P, QL]), sb("gkva", [P, KL]), sb("gq", [P, QK]), sb("gk", [P, QK])
        cos, sin = sb("cos", [P, NB, 2, HALF]), sb("sin", [P, NB, 2, HALF])
        xb, hb, hcur = sb("xb", [P, D]), sb("hb", [P, D]), sb("hcur", [P, KT, P])
        sqj = sb("sqj", [P, H * QK])
        lat, qan, clat, qcT = sb("lat", [P, LAT]), sb("qan", [P, QL]), sb("clat", [P, KL]), sb("qcT", [P, 5, P])
        st, st2 = sb("st", [P, 4]), sb("st2", [P, 2, H])
        q, kn = sb("q", [P, H, QK]), sb("kn", [P, H, NOPE])
        ra, rb = sb("ra", [P, H, ROPE]), sb("rb", [P, H, ROPE])
        kp, kpr, kpa, kpb = sb("kp", [P, ROPE]), sb("kpr", [P, ROPE]), sb("kpa", [P, ROPE]), sb("kpb", [P, ROPE])
        kinv, keys = sb("kinv", [P, H]), sb("keys", [P, H, QK])
        headsT, vs = sb("headsT", [QK, 8, 4, P]), sb("vs", [P, MW])
        psA = [ps(f"bankA{i}") for i in range(4)]
        psQ = [ps(f"bankQ{i}") for i in range(4)]
        names = ("vec_in", "x_in", "ssq", "ms", "rt", "h_done", "h_tr", "h_sb", "lat_mm", "lat_sb", "lat_ssq", "lat_ms",
                 "lat_rt", "lat_n", "lat_tr", "lat_T", "q_mm", "q_sb", "kn_mm", "kn_sb", "v_mm", "v_sb", "nrm", "nrm_rt",
                 "q_done", "k_done", "out_ready", "out_done", "tr_q", "tr_sb", "w_lat_in", "w_up_in", "hT_sb", "ones_", "sp_past", "spilled")
        s = {n: sem("f_" + n) for n in names}
        block = ctx.enter_context(nc.Block())
        blocks = lambda e, body: _prompt_blocks(e, body)

        @block.sync
        def _(sp):
            for dst, src in ((gqa, "g_qa"), (gkva, "g_kva"), (gq, "g_q"), (gk, "g_k")):
                sp.dma_start(dst[:, :], bc(I[src], P, 0)).then_inc(s["vec_in"], 16)
            sp.dma_start(cos[:, :, :, :], I["cos"]).then_inc(s["vec_in"], 16)
            sp.dma_start(sin[:, :, :, :], I["sin"]).then_inc(s["vec_in"], 16)
            sp.dma_start(xb[:, :], I["x_prompt"][0, 0:P, :]).then_inc(s["x_in"], 16)
            sp.dma_start(wl[:, :, :], I["w_in"].rearrange("(k p) n -> p k n", p=P)[:, :, 0:LAT]).then_inc(s["w_lat_in"], 16)
            sp.dma_start(wuq[:, :, :], I["w_uq"].rearrange("(k p) h d -> p k (h d)", p=P)).then_inc(s["w_up_in"], 16)
            sp.dma_start(wuk[:, :, :], I["w_uk"].rearrange("(k p) h d -> p k (h d)", p=P)).then_inc(s["w_up_in"], 16)
            sp.dma_start(wuv[:, :, :], I["w_uv"].rearrange("(k p) h d -> p k (h d)", p=P)).then_inc(s["w_up_in"], 16)

            def outputs(t, rows, kv, kpe, ki):
                sp.wait_ge(s["out_ready"], t + 1)
                sp.dma_start(kv, clat[0:rows, :]).then_inc(s["out_done"], 16)
                sp.dma_start(kpe, kpr[0:rows, :]).then_inc(s["out_done"], 16)
                sp.dma_start(ki, kinv[0:rows, :]).then_inc(s["out_done"], 16)

            def spill(t, tok):
                sp.wait_ge(s["v_sb"], t + 1)
                sp.dma_start(M.v_dram[tok, :], vs[:, :]).then_inc(s["spilled"], 16)
                for n in range(8):
                    sp.wait_ge(s["tr_sb"], t * 8 + n + 1)
                    sp.sem_inc(s["sp_past"], 1)
                    h = 4 * (n % 4)
                    dst = M.qk_dram[n // 4, h:h + 4, :, tok]
                    sp.dma_start(dst.rearrange("h d t -> d h t"), headsT[:, n, :, :]).then_inc(s["spilled"], 16)

            with sp.Fori(0, PB - 1) as t:
                sp.wait_ge(s["h_done"], t + 1)
                sp.dma_start(xb[:, :], I["x_prompt"][0, bass.ds(t * P + P, P), :]).then_inc(s["x_in"], 16)
                tok = bass.ds(t * P, P)
                outputs(t, P, O["kv_p"][0, tok, :], O["kpe_p"][0, tok, :], O["kinv_p"][0, tok, :])
                spill(t, tok)
            sp.wait_ge(s["h_done"], PB)
            sp.dma_start(xb[0:SB, :], I["x_sample"].rearrange("b t d -> (b t) d")).then_inc(s["x_in"], 16)
            tok = slice(SEQ - P, SEQ)
            outputs(PB - 1, P, O["kv_p"][0, tok, :], O["kpe_p"][0, tok, :], O["kinv_p"][0, tok, :])
            spill(PB - 1, tok)
            outputs(PB, SB, O["kv_s"].rearrange("b t d -> (b t) d"), O["kpe_s"].rearrange("b t d -> (b t) d"),
                    O["kinv_s"].rearrange("b t d -> (b t) d"))
            sp.wait_ge(s["out_done"], 48 * NB)
            sp.wait_ge(s["spilled"], 144 * PB)

        @block.scalar
        def _(act):
            act.wait_ge(s["vec_in"], 96)

            def body(t, sample):
                act.wait_ge(s["x_in"], 16 * (t + 1))
                nc.scalar.activation(sqj[:, 0:D], xb[:, :], ACT.Square, accum_out=st[:, 0:1]).then_inc(s["ssq"], 1)
                act.wait_ge(s["ms"], t + 1)
                nc.scalar.activation(st[:, 1:2], st[:, 0:1], ACT.Sqrt).then_inc(s["rt"], 1)
                act.wait_ge(s["h_tr"], t + 1)
                act.wait_ge(s["hT_sb"], t)
                for n in range(2):
                    last = nc.scalar.copy(hcur[:, 4 * n:4 * n + 4, :], psA[n][:, :].rearrange("p (k t) -> p k t", t=P))
                last.then_inc(s["h_sb"], 1)
                act.wait_ge(s["lat_mm"], t + 1)
                nc.scalar.copy(lat[:, 0:512], psA[2][:, :])
                nc.scalar.copy(lat[:, 512:LAT], psA[3][:, 0:LAT - 512]).then_inc(s["lat_sb"], 1)
                act.drain()
                nc.scalar.activation(sqj[:, 0:QL], lat[:, 0:QL], ACT.Square, scale=QL ** -0.5, accum_out=st[:, 0:1])
                nc.scalar.activation(sqj[:, 512:512 + KL], lat[:, QL:QL + KL], ACT.Square, scale=KL ** -0.5, accum_out=st[:, 1:2])
                nc.scalar.activation(sqj[:, 1024:1024 + ROPE], lat[:, QL + KL:LAT], ACT.Square, accum_out=st[:, 2:3]).then_inc(s["lat_ssq"], 1)
                act.wait_ge(s["lat_ms"], t + 1)
                nc.scalar.activation(st[:, 0:2], st[:, 0:2], ACT.Sqrt).then_inc(s["lat_rt"], 1)
                act.wait_ge(s["lat_tr"], t + 1)
                nc.scalar.copy(qcT[:, 0:4, :], psA[0][:, :].rearrange("p (k t) -> p k t", t=P))
                nc.scalar.copy(qcT[:, 4, :], psA[1][:, 0:P]).then_inc(s["lat_T"], 1)
                act.wait_ge(s["q_mm"], t + 1)
                qf = q[:, :, :].rearrange("p h d -> p (h d)")
                for n in range(3):
                    last = nc.scalar.copy(qf[:, n * 512:(n + 1) * 512], psQ[n][:, :])
                last.then_inc(s["q_sb"], 1)
                act.wait_ge(s["kn_mm"], t + 1)
                kf = kn[:, :, :].rearrange("p h d -> p (h d)")
                for n in range(2):
                    last = nc.scalar.copy(kf[:, n * 512:(n + 1) * 512], psA[2 + n][:, :])
                last.then_inc(s["kn_sb"], 1)
                if not sample:
                    act.wait_ge(s["v_mm"], t + 1)
                    act.wait_ge(s["spilled"], 144 * t)
                    for n in range(2):
                        last = nc.scalar.copy(vs[:, n * 512:(n + 1) * 512], psA[n][:, :])
                    last.then_inc(s["v_sb"], 1)
                act.wait_ge(s["nrm"], t + 1)
                nc.scalar.activation(st2[:, :, :], st2[:, :, :], ACT.Sqrt).then_inc(s["nrm_rt"], 1)
                if not sample:
                    for n in range(8):
                        act.wait_ge(s["tr_q"], t * 8 + n + 1)
                        nc.scalar.copy(headsT[:, n, :, :], psQ[n % 4][0:QK, :].rearrange("p (h t) -> p h t", t=P)).then_inc(s["tr_sb"], 1)

            blocks(act, body)

        @block.tensor
        def _(pe):
            def body(t, sample):
                pe.wait_ge(s["h_done"], t + 1)
                pe.wait_ge(s["v_sb"], t)
                for k in range(KT):
                    last = nc.tensor.transpose(psA[k // 4][:, (k % 4) * P:(k % 4 + 1) * P], hb[:, k * P:(k + 1) * P], M.ident[:, :])
                last.then_inc(s["h_tr"], 1)
                pe.wait_ge(s["h_sb"], t + 1)
                pe.wait_ge(s["w_lat_in"], 16)
                for n, (a, b) in enumerate(((0, 512), (512, LAT))):
                    for k in range(KT):
                        last = nc.tensor.matmul(psA[2 + n][:, 0:b - a], hcur[:, k, :], wl[:, k, a:b], start=(k == 0), stop=(k == KT - 1))
                last.then_inc(s["lat_mm"], 1)
                pe.wait_ge(s["lat_n"], t + 1)
                for k in range(3):
                    nc.tensor.transpose(psA[0][:, k * P:(k + 1) * P], qan[:, k * P:(k + 1) * P], M.ident[:, :])
                nc.tensor.transpose(psA[0][:, 3 * P:4 * P], clat[:, 0:P], M.ident[:, :])
                nc.tensor.transpose(psA[1][:, 0:P], clat[:, P:2 * P], M.ident[:, :]).then_inc(s["lat_tr"], 1)
                pe.wait_ge(s["lat_T"], t + 1)
                pe.wait_ge(s["w_up_in"], 48)
                pe.wait_ge(s["tr_sb"], t * 8)
                for n in range(3):
                    for k in range(3):
                        last = nc.tensor.matmul(psQ[n][:, :], qcT[:, k, :], wuq[:, k, n * 512:(n + 1) * 512], start=(k == 0), stop=(k == 2))
                last.then_inc(s["q_mm"], 1)
                for n in range(2):
                    for k in range(2):
                        last = nc.tensor.matmul(psA[2 + n][:, :], qcT[:, 3 + k, :], wuk[:, k, n * 512:(n + 1) * 512], start=(k == 0), stop=(k == 1))
                last.then_inc(s["kn_mm"], 1)
                if not sample:
                    for n in range(2):
                        for k in range(2):
                            last = nc.tensor.matmul(psA[n][:, :], qcT[:, 3 + k, :], wuv[:, k, n * 512:(n + 1) * 512], start=(k == 0), stop=(k == 1))
                    last.then_inc(s["v_mm"], 1)
                    for n in range(8):
                        src, ready = (q, s["q_done"]) if n < 4 else (keys, s["k_done"])
                        if n in (0, 4):
                            pe.wait_ge(ready, t + 1)
                        if n == 0:
                            pe.wait_ge(s["q_sb"], t + 1)
                        if n >= 4:
                            pe.wait_ge(s["tr_sb"], t * 8 + n - 3)
                        for h in range(4):
                            last = nc.tensor.transpose(psQ[n % 4][0:QK, h * P:(h + 1) * P], src[:, 4 * (n % 4) + h, :], M.ident[:, :])
                        last.then_inc(s["tr_q"], 1)

            blocks(pe, body)

        @block.gpsimd
        def _(pool):
            def body(t, sample):
                pool.wait_ge(s["h_sb"], t + 1)
                nc.gpsimd.tensor_copy(M.hT[:, :, bass.ds(t * P, P)], hcur[:, :, :]).then_inc(s["hT_sb"], 1)
                if sample:
                    pool.wait_ge(s["lat_T"], t + 1)
                    nc.gpsimd.tensor_copy(M.cnewT[:, :, :], qcT[:, 3:5, :])
                    nc.gpsimd.tensor_copy(M.cnew[:, 0:KL], clat[0:SB, :])
                    nc.gpsimd.memset(M.cnew[:, KL:KL + 1], 1.0).then_inc(s["ones_"], 1)

            blocks(pool, body)

        @block.vector
        def _(dve):
            v = nc.vector
            dve.wait_ge(s["vec_in"], 96)

            def rope(out, src, a, b, t, heads):
                table = lambda w: w[:, t, :, :].rearrange("p a c -> p (a c)")
                c_, s_ = table(cos), table(sin)
                if heads:
                    c_, s_ = bc(c_, H, 1), bc(s_, H, 1)
                v.tensor_tensor(a, src, c_, ALU.mult)
                v.tensor_tensor(b, src, s_, ALU.mult)
                dve.drain()
                v.tensor_tensor(out[..., 0:HALF], a[..., 0:HALF], b[..., HALF:ROPE], ALU.subtract)
                return v.tensor_tensor(out[..., HALF:ROPE], b[..., 0:HALF], a[..., HALF:ROPE], ALU.add)

            def body(t, sample):
                dve.wait_ge(s["ssq"], t + 1)
                v.tensor_scalar(st[:, 0:1], st[:, 0:1], 1.0 / D, EPS, ALU.mult, ALU.add).then_inc(s["ms"], 1)
                dve.wait_ge(s["rt"], t + 1)
                v.reciprocal(st[:, 3:4], st[:, 1:2])
                dve.drain()
                m = 1 if sample else 0
                v.scalar_tensor_tensor(hb[:, :], xb[:, :], st[:, 3:4], M.G1[:, m, :], ALU.mult, ALU.mult)
                dve.drain()
                v.tensor_tensor(hb[:, :], hb[:, :], M.SH[:, m, :], ALU.add).then_inc(s["h_done"], 1)
                dve.wait_ge(s["lat_ssq"], t + 1)
                v.tensor_scalar(st[:, 0:2], st[:, 0:2], EPS, None, ALU.add)
                dve.drain()
                v.tensor_copy(st[:, 3:4], st[:, 2:3]).then_inc(s["lat_ms"], 1)
                dve.wait_ge(s["lat_rt"], t + 1)
                v.reciprocal(st[:, 0:2], st[:, 0:2])
                dve.drain()
                dve.wait_ge(s["out_done"], t * 48)
                v.scalar_tensor_tensor(qan[:, :], lat[:, 0:QL], st[:, 0:1], gqa[:, :], ALU.mult, ALU.mult)
                v.scalar_tensor_tensor(clat[:, :], lat[:, QL:QL + KL], st[:, 1:2], gkva[:, :], ALU.mult, ALU.mult).then_inc(s["lat_n"], 1)
                v.tensor_tensor(kp[:, :], lat[:, QL + KL:LAT], gk[:, NOPE:QK], ALU.mult)
                dve.drain()
                rope(kpr[:, :], kp[:, :], kpa[:, :], kpb[:, :], t, False)
                dve.wait_ge(s["q_sb"], t + 1)
                sq = sqj[:, :].rearrange("p (h d) -> p h d", d=QK)
                v.tensor_tensor(sq, q[:, :, :], q[:, :, :], ALU.mult)
                dve.drain()
                v.tensor_reduce(st2[:, 0, :], sq, AX.X, ALU.add)
                dve.drain()
                dve.wait_ge(s["kn_sb"], t + 1)
                sk = sqj[:, 0:MW].rearrange("p (h d) -> p h d", d=NOPE)
                v.tensor_tensor(sk, kn[:, :, :], kn[:, :, :], ALU.mult)
                dve.drain()
                v.tensor_reduce(st2[:, 1, :], sk, AX.X, ALU.add)
                dve.drain()
                v.tensor_scalar(st2[:, 1, :], st2[:, 1, :], st[:, 3:4], None, ALU.add)
                dve.drain()
                v.tensor_scalar(st2[:, :, :], st2[:, :, :], 1.0 / QK, EPS, ALU.mult, ALU.add).then_inc(s["nrm"], 1)
                dve.wait_ge(s["nrm_rt"], t + 1)
                v.reciprocal(st2[:, :, :], st2[:, :, :])
                dve.drain()
                v.tensor_copy(kinv[:, :], st2[:, 1, :]).then_inc(s["out_ready"], 1)
                v.tensor_tensor(q[:, :, :], q[:, :, :], bc(st2[:, 0, :], QK, 2), ALU.mult)
                dve.drain()
                v.tensor_tensor(q[:, :, :], q[:, :, :], bc(gq[:, :], H, 1), ALU.mult)
                dve.drain()
                rope(q[:, :, NOPE:QK], q[:, :, NOPE:QK], ra[:, :, :], rb[:, :, :], t, True).then_inc(s["q_done"], 1)
                if not sample:
                    v.tensor_tensor(kn[:, :, :], kn[:, :, :], bc(gk[:, 0:NOPE], H, 1), ALU.mult)
                    dve.drain()
                    v.tensor_tensor(keys[:, :, 0:NOPE], kn[:, :, :], bc(kinv[:, :], NOPE, 2), ALU.mult)
                    v.tensor_tensor(keys[:, :, NOPE:QK], bc(kpr[:, :], H, 1), bc(kinv[:, :], ROPE, 2), ALU.mult).then_inc(s["k_done"], 1)
                else:
                    dve.drain()
                    v.tensor_tensor(M.qg[:, :, :], q[0:SB, :, 0:NOPE], bc(gk[0:SB, 0:NOPE], H, 1), ALU.mult)
                    v.tensor_copy(M.qpe[:, :, :], q[0:SB, :, NOPE:QK])
                    v.tensor_copy(M.kpenew[:, :], kpr[0:SB, :])
                    v.tensor_copy(M.kinvnew[:, :], kinv[0:SB, :])

            blocks(dve, body)


def _prompt_blocks(engine, body):
    with engine.Fori(0, PB) as t:
        body(t, False)
    body(PB, True)


def prompt(nc, I, M):
    with ExitStack() as ctx:
        sb = lambda name, shape: ctx.enter_context(nc.sbuf_tensor("pr_" + name, shape, F32))
        ps = lambda name: ctx.enter_context(nc.psum_tensor("pr_" + name, [P, 512], F32))
        sem = lambda name: nc.alloc_semaphore("p_" + name)
        wz = [sb(f"wz{i}", [P, KT, P]) for i in range(2)]
        tri = sb("tri", [P, P])
        qh = [sb(f"qh{i}", [QK, 2, SEQ]) for i in range(2)]
        kh = [sb(f"kh{i}", [QK, 2, SEQ]) for i in range(2)]
        vh = [sb(f"vh{i}", [P, PB, P]) for i in range(2)]
        pb, pT = sb("pb", [P, 2, SEQ]), sb("pT", [P, 2, SEQ])
        mx, nmx, rs, ri = sb("mx", [P, 8]), sb("nmx", [P, 8]), sb("rs", [P, 8]), sb("ri", [P, 8])
        ez, zs = sb("ez", [P, TOK]), sb("zs", [P, TOK])
        psS, psT = [ps("psS0"), ps("psS1")], [ps("psT0"), ps("psT1")]
        psO, psZ0, psZ1 = ps("psO"), ps("psZ0"), ps("psZ1")
        tri_in, wz_in = sem("tri_in"), [sem("wz_in0"), sem("wz_in1")]
        heads_in = [sem("heads_in0"), sem("heads_in1")]
        scores, maxed, exped, normed, tr, tr_sb, pv, o_sb, z_mm, z_exp, z_sb = (
            sem(n) for n in ("scores", "maxed", "exped", "normed", "tr", "tr_sb", "pv", "o_sb", "z_mm", "z_exp", "z_sb"))
        w_v = I["w_in"].rearrange("(k p) n -> p k n", p=P)
        NU = 2 * PB
        block = ctx.enter_context(nc.Block())

        @block.sync
        def _(sp):
            sp.dma_start(tri[:, :], I["tri"]).then_inc(tri_in, 16)

            def load(b, hp):
                for which, dst in ((0, qh[b]), (1, kh[b])):
                    src = M.qk_dram[which, bass.ds(2 * hp, 2), :, :]
                    sp.dma_start(dst[:, :, :], src.rearrange("h d t -> d h t")).then_inc(heads_in[b], 16)
                sp.dma_start(vh[b][:, :, :], M.v_dram[:, bass.ds(hp * P, P)].rearrange("(b t) n -> t b n", t=P)).then_inc(heads_in[b], 16)
                sp.dma_start(wz[b][:, :, :], w_v[:, :, bass.ds(C_ZA + hp * P, P)]).then_inc(wz_in[b], 16)

            for b in range(2):
                load(b, b)
            with sp.Fori(1, NP // 2) as i:
                for b in range(2):
                    sp.wait_ge(pv, NU * (2 * i + b - 1))
                    load(b, 2 * i + b)

        @block.tensor
        def _(pe):
            pe.wait_ge(tri_in, 16)

            def score(hp, hp_b, u):
                hh, qb = u // PB, u % PB
                pe.wait_ge(exped, NU * hp + u - 1) if u >= 1 else pe.wait_ge(exped, NU * hp)
                nk = (qb + 1) * P
                nc.tensor.matmul(psS[u % 2][:, 0:nk], qh[hp_b][:, hh, qb * P:nk], kh[hp_b][:, hh, 0:nk],
                                 start=True, stop=True).then_inc(scores, 1)

            def pair(i, b):
                hp = 2 * i + b
                pe.wait_ge(heads_in[b], i * 48 + 48)
                pe.wait_ge(wz_in[b], i * 16 + 16)
                pe.wait_ge(o_sb, hp)
                score(hp, b, 0)
                for u in range(NU):
                    if u + 1 < NU:
                        score(hp, b, u + 1)
                    k = u
                    nc.tensor.matmul(psZ0[:, :], wz[b][:, k, :], M.hT[:, k, 0:SEQ], start=(k == 0), stop=(k == KT - 1))
                    last = nc.tensor.matmul(psZ1[:, 0:P], wz[b][:, k, :], M.hT[:, k, SEQ:TOK], start=(k == 0), stop=(k == KT - 1))
                    if k == KT - 1:
                        last.then_inc(z_mm, 1)
                    hh, qb = u // PB, u % PB
                    pe.wait_ge(normed, NU * hp + u + 1)
                    for kb in range(qb + 1):
                        last = nc.tensor.transpose(psT[u % 2][:, kb * P:(kb + 1) * P], pb[:, u % 2, kb * P:(kb + 1) * P], M.ident[:, :])
                    last.then_inc(tr, 1)
                    pe.wait_ge(tr_sb, NU * hp + u + 1)
                    for kb in range(qb + 1):
                        last = nc.tensor.matmul(psO[hh * VD:(hh + 1) * VD, qb * P:(qb + 1) * P], vh[b][:, kb, hh * VD:(hh + 1) * VD],
                                                pT[:, u % 2, kb * P:(kb + 1) * P], start=(kb == 0), stop=(kb == qb))
                    last.then_inc(pv, 1)

            with pe.Fori(0, NP // 2) as i:
                for b in range(2):
                    pair(i, b)

        @block.vector
        def _(dve):
            v = nc.vector
            dve.wait_ge(tri_in, 16)
            with dve.Fori(0, NP) as hp:
                def top(u):
                    qb = u % PB
                    nk = (qb + 1) * P
                    dve.wait_ge(scores, NU * hp + u + 1)
                    v.tensor_tensor(psS[u % 2][:, qb * P:nk], psS[u % 2][:, qb * P:nk], tri[:, :], ALU.add)
                    dve.drain()
                    v.tensor_reduce(mx[:, u:u + 1], psS[u % 2][:, 0:nk], AX.X, ALU.max)
                    dve.drain()
                    v.tensor_scalar(nmx[:, u:u + 1], mx[:, u:u + 1], -SCALE, None, ALU.mult).then_inc(maxed, 1)

                top(0)
                for u in range(NU):
                    if u + 1 < NU:
                        top(u + 1)
                    nk = (u % PB + 1) * P
                    dve.wait_ge(exped, NU * hp + u + 1)
                    v.reciprocal(ri[:, u:u + 1], rs[:, u:u + 1])
                    dve.drain()
                    v.tensor_scalar(pb[:, u % 2, 0:nk], pb[:, u % 2, 0:nk], ri[:, u:u + 1], None, ALU.mult).then_inc(normed, 1)
                dve.wait_ge(z_exp, hp + 1)
                v.tensor_scalar(ez[:, :], ez[:, :], 1.0, None, ALU.add)
                dve.drain()
                v.reciprocal(ez[:, :], ez[:, :])
                dve.drain()
                v.tensor_tensor(zs[:, :], zs[:, :], ez[:, :], ALU.mult)
                dve.drain()
                dve.wait_ge(pv, NU * (hp + 1))
                v.tensor_copy(M.zas[:, hp, :], zs[:, SEQ:SEQ + SB])
                v.tensor_tensor(M.oaT[:, hp, 0:SEQ], psO[:, :], zs[:, 0:SEQ], ALU.mult).then_inc(o_sb, 1)

        @block.scalar
        def _(act):
            def evac(hp, u):
                nk = (u % PB + 1) * P
                act.wait_ge(tr, NU * hp + u + 1)
                nc.scalar.copy(pT[:, u % 2, 0:nk], psT[u % 2][:, 0:nk]).then_inc(tr_sb, 1)

            with act.Fori(0, NP) as hp:
                for u in range(NU):
                    nk = (u % PB + 1) * P
                    act.wait_ge(maxed, NU * hp + u + 1)
                    act.wait_ge(tr, NU * hp + u - 1) if u >= 1 else act.wait_ge(tr, NU * hp)
                    nc.scalar.activation(pb[:, u % 2, 0:nk], psS[u % 2][:, 0:nk], ACT.Exp, bias=nmx[:, u:u + 1], scale=SCALE,
                                         accum_out=rs[:, u:u + 1]).then_inc(exped, 1)
                    if u >= 1:
                        evac(hp, u - 1)
                evac(hp, NU - 1)
                act.wait_ge(z_mm, hp + 1)
                act.wait_ge(o_sb, hp)
                nc.scalar.activation(ez[:, 0:SEQ], psZ0[:, :], ACT.Exp, scale=-1.0)
                nc.scalar.activation(ez[:, SEQ:TOK], psZ1[:, 0:P], ACT.Exp, scale=-1.0)
                nc.scalar.copy(zs[:, 0:SEQ], psZ0[:, :])
                nc.scalar.copy(zs[:, SEQ:TOK], psZ1[:, 0:P]).then_inc(z_exp, 1)


def absorb(nc, I, M):
    with ExitStack() as ctx:
        sb = lambda name, shape: ctx.enter_context(nc.sbuf_tensor("ab_" + name, shape, F32))
        ps = lambda name: ctx.enter_context(nc.psum_tensor("ab_" + name, [P, 512], F32))
        sem = lambda name: nc.alloc_semaphore("b_" + name)
        wuk, ukT, qgT = sb("wuk_b", [P, 2, MW]), sb("ukT", [P, NP, KL]), sb("qgT", [P, NP, SB])
        bk = [ps(f"bankB{i}") for i in range(6)]
        w_in_sb, tr, tr_sb, mm, ev = (sem(n) for n in ("w_in", "tr", "tr_sb", "mm", "ev"))
        block = ctx.enter_context(nc.Block())

        @block.sync
        def _(sp):
            sp.dma_start(wuk[:, :, :], I["w_uk"].rearrange("(k p) h d -> p k (h d)", p=P)).then_inc(w_in_sb, 16)
            sp.wait_ge(w_in_sb, 16)

        @block.tensor
        def _(pe):
            pe.wait_ge(w_in_sb, 16)
            for hp in range(NP):
                for k in range(2):
                    last = nc.tensor.transpose(bk[hp // 2][:, (hp % 2) * KL + k * P:(hp % 2) * KL + (k + 1) * P],
                                               wuk[:, k, hp * P:(hp + 1) * P], M.ident[:, :])
                nc.tensor.transpose(bk[4][:, hp * SB:(hp + 1) * SB],
                                    M.qg[:, :, :].rearrange("t h d -> t (h d)")[:, hp * P:(hp + 1) * P], M.ident[0:SB, 0:SB])
            nc.tensor.transpose(bk[5][0:ROPE, 8 * SB - SB:8 * SB], M.kpenew[:, :], M.ident[0:SB, 0:SB]).then_inc(tr, 1)
            pe.wait_ge(tr_sb, 1)
            for half in range(2):
                if half:
                    pe.wait_ge(ev, 3)
                for h in range(8):
                    last = nc.tensor.transpose(bk[5][0:ROPE, h * SB:(h + 1) * SB], M.qpe[:, 8 * half + h, :], M.ident[0:SB, 0:SB])
                last.then_inc(mm, 1)
                if half == 0:
                    for rt in range(2):
                        for h in range(H):
                            b = 64 * (h % 2)
                            last = nc.tensor.matmul(bk[2 * (h % 2) + rt][:, (h // 2) * SB:(h // 2 + 1) * SB], ukT[b:b + 64, h // 2, rt * P:(rt + 1) * P],
                                                    qgT[b:b + 64, h // 2, :], start=True, stop=True)
                        last.then_inc(mm, 1)

        @block.vector
        def _(dve):
            v = nc.vector
            dve.wait_ge(tr, 1)
            for n in range(4):
                v.tensor_copy(ukT[:, 2 * n:2 * n + 2, :], bk[n][:, :].rearrange("p (a r) -> p a r", r=KL))
            v.memset(M.kpenewT[:, SB:P], 0.0)
            v.tensor_copy(M.kpenewT[:, 0:SB], bk[5][0:ROPE, 7 * SB:8 * SB])
            v.tensor_copy(qgT[:, :, :], bk[4][:, :].rearrange("p (a t) -> p a t", t=SB)).then_inc(tr_sb, 1)

            def by_batch(dst, bank, heads):
                return v.tensor_copy(dst[:, :, heads, :], bank.rearrange("p (h b t) -> p b h t", h=8, t=TD))

            dve.wait_ge(mm, 1)
            by_batch(M.qpT, bk[5][0:ROPE, :], slice(0, 8)).then_inc(ev, 1)
            for rt in range(2):
                dve.wait_ge(mm, 2 + rt)
                by_batch(M.qlT[:, rt], bk[rt][:, :], slice(0, H, 2))
                by_batch(M.qlT[:, rt], bk[2 + rt][:, :], slice(1, H, 2)).then_inc(ev, 1)
            dve.wait_ge(mm, 4)
            by_batch(M.qpT, bk[5][0:ROPE, :], slice(8, H)).then_inc(ev, 1)


def sample(nc, I, M):
    with ExitStack() as ctx:
        sb = lambda name, shape: ctx.enter_context(nc.sbuf_tensor("sa_" + name, shape, F32))
        ps = lambda name: ctx.enter_context(nc.psum_tensor("sa_" + name, [P, 512], F32))
        sem = lambda name: nc.alloc_semaphore("s_" + name)
        G, GP = 8, 4
        ROW = H * TD
        C1 = KL + 1
        table = ctx.enter_context(nc.sbuf_tensor("table", [1, BD * PAGES], I32))
        pages = [sb(f"pages{i}", [P, PAGES, C1]) for i in range(2)]
        kpe, kinv = [sb(f"kpe{i}", [P, PAGES, ROPE]) for i in range(2)], [sb(f"kinvp{i}", [P, PAGES, H]) for i in range(2)]
        cT, kT = sb("cT_pages", [P, 2, 2, 512]), sb("kpeT_pages", [ROPE, 2, 512])
        ST = sb("ST", [P, PAGES + 1, ROW])
        own = sb("own_mask", [SB, BD, ROW])
        top4, top1, topr, topb, topB = sb("top4", [P, 512]), sb("top1", [P, ROW]), sb("topr", [ROW, 1]), sb("topb", [ROW, P]), sb("topB", [P, ROW])
        ri, ol, olT = sb("ri_s", [ROW, 1]), sb("ol", [ROW, KL]), sb("olT", [P, 2, H, SB])
        wuv = sb("wuv_s", [P, 2, MW])
        psA, psK, psS, psO, psM = [ps("psA0"), ps("psA1")], ps("psK"), [ps("psSs0"), ps("psSs1")], ps("psOs"), ps("psMs")
        table_in, fixed_in = sem("table_in"), sem("fixed_in")
        pages_in = [sem("pages_in0"), sem("pages_in1")]
        cT_tr, cT_sb, scored, weighted, topped, top_tr, top_row, top_bc, centred, exped, pv, o_sb, o_tr, o_T, up, ones, gated, stored, sp_past = (
            sem(n) for n in ("cT_tr", "cT_sb", "scored", "weighted", "topped", "top_tr", "top_row", "top_bc",
                             "centred", "exped", "pv", "o_sb", "o_tr", "o_T", "up", "ones", "gated", "stored", "sp_past"))
        block = ctx.enter_context(nc.Block())

        @block.sync
        def _(sp):
            sp.dma_start(table[:, :], I["page_table"].rearrange("(a b) n -> a (b n)", a=1)).then_inc(table_in, 16)
            sp.dma_start(own[:, :, :], I["own_mask"]).then_inc(fixed_in, 16)
            sp.dma_start(wuv[:, :, :], I["w_uv"].rearrange("(k p) h d -> p k (h d)", p=P)).then_inc(fixed_in, 16)
            sp.wait_ge(table_in, 16)
            sp.wait_ge(ones, 1)

            def load(b, s):
                with sp.Fori(0, PAGES) as j:
                    page = sp.value_load(table[0:1, bass.ds(s * PAGES + j, 1)], min_val=0, max_val=M.n_phys - 1)
                    at = bass.ds(page, 1)
                    for dst, src, w in ((pages[b], "cache_kv", KL), (kpe[b], "cache_kpe", ROPE), (kinv[b], "cache_kinv", H)):
                        sp.dma_start(dst[:, bass.ds(j, 1), 0:w], I[src][at, :, :].rearrange("a p n -> p a n")).then_inc(pages_in[b], 16)

            for b in range(2):
                load(b, b)
            with sp.Fori(1, BD // 2) as i:
                for b in range(2):
                    sp.wait_ge(pv, 2 * i + b - 1)
                    sp.sem_inc(sp_past, 1)
                    load(b, 2 * i + b)
            sp.wait_ge(gated, 1)
            sp.dma_start(M.oa_dram, M.oaT[:, :, :]).then_inc(stored, 16)
            sp.wait_ge(stored, 16)

        @block.tensor
        def _(pe):
            pe.wait_ge(fixed_in, 32)

            def transposes(i, b, g):
                s = 2 * i + b
                pe.wait_ge(cT_sb, G * s + g)
                for p in range(GP):
                    at = slice(p * P, (p + 1) * P)
                    for r in range(2):
                        nc.tensor.transpose(psA[r][:, at], pages[b][:, GP * g + p, r * P:(r + 1) * P], M.ident[:, :])
                    last = nc.tensor.transpose(psK[0:ROPE, at], kpe[b][:, GP * g + p, :], M.ident[:, :])
                last.then_inc(cT_tr, 1)

            def scores(i, b, g):
                s = 2 * i + b
                pe.wait_ge(cT_sb, G * s + g + 1)
                pe.wait_ge(weighted, G * s + g - 1) if g >= 1 else pe.wait_ge(weighted, G * s)
                for p in range(GP):
                    at, out = slice(p * P, (p + 1) * P), psS[g % 2][:, p * ROW:(p + 1) * ROW]
                    for r in range(2):
                        nc.tensor.matmul(out, cT[:, g % 2, r, at], M.qlT[:, r, s, :, :].rearrange("p h t -> p (h t)"), start=(r == 0), stop=False)
                    last = nc.tensor.matmul(out, kT[:, g % 2, at], M.qpT[:, s, :, :].rearrange("p h t -> p (h t)"), start=False, stop=True)
                last.then_inc(scored, 1)

            def one(i, b):
                s = 2 * i + b
                pe.wait_ge(pages_in[b], i * 48 * PAGES + 48 * PAGES)
                transposes(i, b, 0)
                for g in range(G):
                    if g + 1 < G:
                        transposes(i, b, g + 1)
                    scores(i, b, g)
                pe.wait_ge(o_sb, s)
                own_ps = psM[:, 0:ROW]
                for r in range(2):
                    nc.tensor.matmul(own_ps, M.cnewT[:, r, :], M.qlT[:, r, s, :, :].rearrange("p h t -> p (h t)"), start=(r == 0), stop=False)
                nc.tensor.matmul(own_ps, M.kpenewT[:, :], M.qpT[:, s, :, :].rearrange("p h t -> p (h t)"), start=False, stop=True).then_inc(scored, 1)
                pe.wait_ge(topped, s + 1)
                nc.tensor.transpose(psM[:, 128:256], top1[:, :], M.ident[:, :]).then_inc(top_tr, 1)
                pe.wait_ge(top_row, s + 1)
                nc.tensor.transpose(psM[:, 256:384], topb[:, :], M.ident[:, :]).then_inc(top_bc, 1)
                for j in range(PAGES):
                    if j % 8 == 0:
                        pe.wait_ge(exped, s * 5 + j // 8 + 1)
                    nc.tensor.matmul(psO[:, 0:C1], ST[:, j, :], pages[b][:, j, :], start=(j == 0), stop=False)
                pe.wait_ge(exped, s * 5 + 5)
                nc.tensor.matmul(psO[:, 0:C1], ST[0:SB, PAGES, :], M.cnew[:, :], start=False, stop=True).then_inc(pv, 1)
                pe.wait_ge(o_sb, s + 1)
                for r in range(2):
                    last = nc.tensor.transpose(psM[:, r * P:(r + 1) * P], ol[:, r * P:(r + 1) * P], M.ident[:, :])
                last.then_inc(o_tr, 1)

            with pe.Fori(0, BD // 2) as i:
                for b in range(2):
                    pe.wait_ge(o_T, 2 * i + b)
                    one(i, b)
            pe.wait_ge(o_T, BD)
            for h in range(H):
                o = psK[VD * (h % 2):VD * (h % 2) + VD, (h // 2) * SB:(h // 2 + 1) * SB]
                for r in range(2):
                    last = nc.tensor.matmul(o, wuv[:, r, h * VD:(h + 1) * VD], olT[:, r, h, :], start=(r == 0), stop=(r == 1))
            last.then_inc(up, 1)

        @block.scalar
        def _(act):
            for b in range(2):
                nc.scalar.activation(pages[b][:, :, KL:C1], M.ones[:, 0:PAGES].unsqueeze(2), ACT.Copy)
            act.drain()
            act.nop().then_inc(ones, 1)

            with act.Fori(0, BD) as s:
                for g in range(G):
                    act.wait_ge(cT_tr, G * s + g + 1)
                    act.wait_ge(scored, (G + 1) * s + g - 1) if g >= 1 else act.wait_ge(scored, (G + 1) * s)
                    for r in range(2):
                        nc.scalar.copy(cT[:, g % 2, r, :], psA[r][:, :])
                    nc.scalar.copy(kT[:, g % 2, :], psK[0:ROPE, :]).then_inc(cT_sb, 1)
                for q in range(4):
                    act.wait_ge(centred, 5 * s + q + 1)
                    nc.scalar.activation(ST[:, 8 * q:8 * q + 8, :], ST[:, 8 * q:8 * q + 8, :], ACT.Exp, scale=SCALE).then_inc(exped, 1)
                act.wait_ge(centred, 5 * s + 5)
                nc.scalar.activation(ST[0:SB, PAGES, :], ST[0:SB, PAGES, :], ACT.Exp, scale=SCALE).then_inc(exped, 1)
                act.wait_ge(o_tr, s + 1)
                for r in range(2):
                    last = nc.scalar.copy(olT[:, r, :, bass.ds(s * TD, TD)], psM[:, r * P:(r + 1) * P].rearrange("p (h t) -> p h t", t=TD))
                last.then_inc(o_T, 1)

        @block.vector
        def _(dve):
            v = nc.vector
            dve.wait_ge(fixed_in, 32)

            def one(s, b):
                for g in range(G):
                    dve.wait_ge(scored, (G + 1) * s + g + 1)
                    if g == 0:
                        dve.wait_ge(pv, s)
                    group = ST[:, GP * g:GP * g + GP, :].rearrange("p a (h t) -> p (a h) t", t=TD)
                    ki = kinv[b][:, GP * g:GP * g + GP, :].rearrange("p a h -> p (a h)")
                    v.tensor_tensor(group, psS[g % 2][:, :].rearrange("p (r t) -> p r t", t=TD), bc(ki, TD, 2), ALU.mult).then_inc(weighted, 1)
                    dve.drain()
                    group = ST[:, GP * g:GP * g + GP, :].rearrange("p a r -> p (a r)")
                    if g == 0:
                        v.tensor_copy(top4[:, :], group)
                    else:
                        v.tensor_tensor(top4[:, :], top4[:, :], group, ALU.max)
                dve.wait_ge(scored, (G + 1) * s + G + 1)
                mine = ST[0:SB, PAGES, :]
                v.tensor_tensor(mine.rearrange("p (h t) -> p h t", t=TD), psM[0:SB, 0:ROW].rearrange("p (h t) -> p h t", t=TD),
                                bc(M.kinvnew[:, :], TD, 2), ALU.mult)
                dve.drain()
                v.tensor_tensor(mine, mine, own[:, s, :], ALU.add)
                dve.drain()
                v.tensor_tensor(top4[0:SB, 0:ROW], top4[0:SB, 0:ROW], mine, ALU.max)
                dve.drain()
                v.tensor_reduce(top1[:, :], top4[:, :].rearrange("p (a r) -> p r a", a=GP), AX.X, ALU.max).then_inc(topped, 1)
                dve.wait_ge(top_tr, s + 1)
                v.tensor_reduce(topr[:, :], psM[:, 128:256], AX.X, ALU.max)
                dve.drain()
                v.tensor_copy(topb[:, :], topr[:, 0:1].to_broadcast([ROW, P])).then_inc(top_row, 1)
                dve.wait_ge(top_bc, s + 1)
                v.tensor_copy(topB[:, :], psM[:, 256:384])
                dve.drain()
                for q in range(4):
                    part = ST[:, 8 * q:8 * q + 8, :]
                    v.tensor_tensor(part, part, bc(topB[:, :], 8, 1), ALU.subtract).then_inc(centred, 1)
                v.tensor_tensor(mine, mine, topB[0:SB, :], ALU.subtract).then_inc(centred, 1)
                dve.wait_ge(pv, s + 1)
                v.reciprocal(ri[:, :], psO[:, KL:C1])
                dve.drain()
                v.tensor_scalar(ol[:, :], psO[:, 0:KL], ri[:, 0:1], None, ALU.mult).then_inc(o_sb, 1)

            with dve.Fori(0, BD // 2) as i:
                for b in range(2):
                    one(2 * i + b, b)
            dve.wait_ge(up, 1)
            o = psK[:, :].rearrange("p (a t) -> p a t", t=SB)
            v.memset(M.oaT[:, :, SEQ + SB:TOK], 0.0)
            v.tensor_tensor(M.oaT[:, :, SEQ:SEQ + SB], o, M.zas[:, :, :], ALU.mult).then_inc(gated, 1)


V_MU, V_MULA, V_W0, V_A0, V_KK, V_KA, V_RK, V_GG, V_GB = 0, 24, 25, 33, 41, 49, 57, 65, 73
NVEC = 81
LEVELS = (2, 4, 8, 16, 32, 64)


def _load_vectors(sp, I, dst, sem):
    rows = lambda name, a, n: I[name][a:a + n * P].rearrange("(k p) -> k p", p=P)
    flat_rk = I["r_k"].rearrange("h d -> (h d)").rearrange("(k p) -> k p", p=P)
    parts = [(V_MU, 8, rows("mu_shift", S_R, 8)), (V_MU + 8, 8, rows("mu_shift", S_K, 8)), (V_MU + 16, 8, rows("mu_shift", S_V, 8)),
             (V_W0, 8, rows("w0", 0, 8)), (V_A0, 8, rows("a0", 0, 8)), (V_KK, 8, rows("k_k", 0, 8)), (V_KA, 8, rows("k_a", 0, 8)),
             (V_RK, 8, flat_rk), (V_GG, 8, rows("gn_g", 0, 8)), (V_GB, 8, rows("gn_b", 0, 8))]
    for at, n, src in parts:
        sp.dma_start(dst[at:at + n, :], src).then_inc(sem, 16)
    for half, at in enumerate((S_WL, S_AL)):
        sp.dma_start(dst[V_MULA:V_MULA + 1, 64 * half:64 * half + 64], I["mu_shift"][at:at + 64].rearrange("(a p) -> a p", a=1)).then_inc(sem, 16)
    return 16 * (len(parts) + 2)


def lora(nc, I, O, M):
    with ExitStack() as ctx:
        sb = lambda name, shape: ctx.enter_context(nc.sbuf_tensor("lo_" + name, shape, F32))
        ps = lambda name: ctx.enter_context(nc.psum_tensor("lo_" + name, [P, 512], F32))
        sem = lambda name: nc.alloc_semaphore("l_" + name)
        vec, ss = sb("vec", [NVEC, P]), sb("ss", [BD, 25, P])
        w = sb("w", [P, KT, P])
        px, pxs, d, ds_ = sb("px", [P, SEQ + 1]), sb("pxs", [P, BD, TD + 1]), sb("d", [P, SEQ]), sb("ds", [P, BD, TD])
        psV, psP, psQ = ps("psV"), ps("psP"), ps("psQ")
        vec_in, w_in_sb, tr, tr_sb, mm, ev, mixed, zeroed = (sem(n) for n in ("vec_in", "w_in", "tr", "tr_sb", "mm", "ev", "mixed", "zeroed"))
        block = ctx.enter_context(nc.Block())
        w_v = I["w_in"].rearrange("(k p) n -> p k n", p=P)
        ALL = 16 * (10 + 2) + 16 * 5

        @block.sync
        def _(sp):
            n = _load_vectors(sp, I, vec, vec_in)
            for i, at in enumerate((S_R, S_K, S_V)):
                sp.dma_start(ss[:, 8 * i:8 * i + 8, :], I["state_shift"][:, at:at + 1024].rearrange("b (k p) -> b k p", p=P)).then_inc(vec_in, 16)
            for half, at in enumerate((S_WL, S_AL)):
                sp.dma_start(ss[:, 24, 64 * half:64 * half + 64], I["state_shift"][:, at:at + 64]).then_inc(vec_in, 16)
                sp.dma_start(w[:, :, 64 * half:64 * half + 64], w_v[:, :, C_SH + at:C_SH + at + 64]).then_inc(w_in_sb, 16)
            assert n + 80 == ALL
            sp.dma_start(M.masks[:, :, :], I["chunk_masks"]).then_inc(M.masks_in, 16)
            sp.dma_start(M.see[:, :, :], I["see_masks"]).then_inc(M.masks_in, 16)
            sp.dma_start(M.seg[:, :], bc(I["segments"], P, 0)).then_inc(M.masks_in, 16)
            sp.dma_start(M.pick[:, :], I["pick"]).then_inc(M.masks_in, 16)
            sp.wait_ge(M.masks_in, 64)

        @block.tensor
        def _(pe):
            pe.wait_ge(vec_in, ALL)
            nc.tensor.transpose(psV[:, 0:NVEC], vec[:, :], M.ident[0:NVEC, 0:NVEC])
            for k in range(25):
                last = nc.tensor.transpose(psV[:, 128 + BD * k:128 + BD * k + BD], ss[:, k, :], M.ident[0:BD, 0:BD])
            last.then_inc(tr, 1)
            pe.wait_ge(w_in_sb, 32)
            for k in range(KT):
                nc.tensor.matmul(psP[:, :], w[:, k, :], M.hT[:, k, 0:SEQ], start=(k == 0), stop=(k == KT - 1))
            for k in range(KT):
                last = nc.tensor.matmul(psQ[:, 0:P], w[:, k, :], M.hT[:, k, SEQ:TOK], start=(k == 0), stop=(k == KT - 1))
            last.then_inc(mm, 1)

        @block.scalar
        def _(act):
            act.wait_ge(mixed, 1)
            nc.scalar.activation(M.la[0:64, :], M.la[0:64, :], ACT.Tanh)

        @block.vector
        def _(dve):
            v = nc.vector
            v.memset(px[:, 0:1], 0.0)
            v.memset(M.la[:, SEQ + SB:TOK], 0.0)
            dve.wait_ge(tr, 1)
            v.tensor_copy(M.vec[:, 0:NVEC], psV[:, 0:NVEC])
            v.tensor_copy(M.ss[:, :, :], psV[:, 128:128 + 25 * BD].rearrange("p (k b) -> p k b", b=BD))
            dve.drain()
            v.tensor_scalar(M.nvec[:, :], M.vec[:, V_W0:V_KK], -1.0, None, ALU.mult)
            v.tensor_copy(pxs[:, :, 0], M.ss[:, 24, :])
            dve.wait_ge(mm, 1)
            v.tensor_copy(px[:, 1:SEQ + 1], psP[:, :])
            v.tensor_copy(pxs[:, :, 1:TD + 1], psQ[:, 0:SB].rearrange("p (b t) -> p b t", t=TD))
            dve.drain()
            v.tensor_copy(M.shc[:, 24, 0:1], px[:, SEQ:SEQ + 1])
            v.tensor_copy(M.shc[:, 24, 1:1 + BD], pxs[:, :, TD])
            v.tensor_tensor(d[:, :], px[:, 0:SEQ], px[:, 1:SEQ + 1], ALU.subtract)
            v.tensor_tensor(ds_[:, :, :], pxs[:, :, 0:TD], pxs[:, :, 1:TD + 1], ALU.subtract)
            dve.drain()
            mu = M.vec[:, V_MULA:V_MULA + 1]
            v.scalar_tensor_tensor(M.la[:, 0:SEQ], d[:, :], mu, px[:, 1:SEQ + 1], ALU.mult, ALU.add)
            v.scalar_tensor_tensor(M.la[:, SEQ:SEQ + SB].rearrange("p (b t) -> p b t", t=TD), ds_[:, :, :], mu, pxs[:, :, 1:TD + 1], ALU.mult, ALU.add).then_inc(mixed, 1)


def rwkv(nc, I, O, M):
    with ExitStack() as ctx:
        sb = lambda name, shape: ctx.enter_context(nc.sbuf_tensor("rw_" + name, shape, F32))
        NU, C5 = 2 * NB, NB
        w = sb("w", [P, 4, KT, P])
        wlo = sb("wlo", [P, 2, P])
        px, pxs = sb("px", [P, 3, SEQ + 1]), sb("pxs", [P, 3, BD, TD + 1])
        dx, xs = sb("dx", [P, 3, TOK]), sb("xs", [P, 3, TOK])
        sa = sb("sa", [P, 2, TOK])
        L, Lx = sb("L", [P, TOK]), sb("Lx", [P, TOK])
        cen, gx, g = sb("cen", [P, PB + 1]), sb("gx", [P, PB + BD]), sb("g", [P, PB + BD])
        kk, kf, rn = sb("kk", [P, TOK]), sb("kf", [P, TOK]), sb("rn", [P, TOK])
        ob = kf
        Z, R, B, K = (sb(n, [P, TOK]) for n in ("Z", "R", "B", "K"))
        ZR = sb("ZR", [P, 2, 2, TOK])
        bonus, zb = sb("bonus", [P, TOK]), sb("zb", [P, TOK])
        tm = sb("tm", [P, C5, 4, P])
        gram = sb("gram", [P, NU, 4, P])
        X, XT, W, Nb = (sb(n, [P, NU, P]) for n in ("X", "XT", "W", "Nb"))
        Zt = sb("Zt", [P, NU, RH])
        U0 = sb("U0", [P, C5, 2, RH])
        RT, Phi, Psi, S = sb("RT", [P, C5, P]), sb("Phi", [P, PB, P]), sb("Psi", [P, PB, P]), sb("S", [P, PB + 1, P])
        o, om = sb("o", [P, NU, RH]), sb("om", [P, 2, NU])
        osq = W[:, :, 0:RH]
        s_in = sb("s_in", [RH, BD, P])
        s0T, s0p = sb("s0T", [P, BD, RH]), sb("s0p", [P, 2, BD, RH])
        ZsT = sb("ZsT", [P, SB])
        selp = W[0:SB, 0:4, :].rearrange("p u (a i) -> p (u a) i", a=2)
        picked = sb("picked", [SB, 4, RH])
        bk2, bkT = sb("bk2", [P, P]), sb("bkT", [P, P])
        uv, uvm = sb("uv", [P, P]), XT[:, 0:BD, :]
        snT = Psi[:, :, :].rearrange("p c (a i) -> p (c a) i", a=2)
        s_out, sp_out = sb("s_out", [RH, BD, P]), sb("sp_out", [P, P])
        bank = [ctx.enter_context(nc.psum_tensor(f"rw_bank{i}", [P, 512], F32)) for i in range(8)]
        names = ["zeroed", "w_in", "s_in", "state_out", "stored", "out_sb", "ob_out", "lora_mm", "s0_tr", "proj",
                 "kk_sq", "proj_sb", "kk_sum", "rk_prod", "rk_sum", "zbk", "tm_tr", "zr", "bonus", "tm_sb", "gram_sb",
                 "gram", "x_first", "nb", "zkv", "zw", "y_mm", "y_sb", "rt_mm", "psi_mm", "zs_mm", "rt_sb", "s_next",
                 "phi_mm", "o_mm", "s0_sb", "seen", "bk2", "o_sb", "bk_tr", "on", "o_tr", "uvm", "sn_mm", "sn",
                 "sn_tr", "px", "sa", "cum", "expd", "z_in_nb", "zsT", "bkT", "mixed", "pxs0", "shc", "kk_max", "rn",
                 "var", "rstd", "dve_past", "pe_past", "pool_past"]
        names += [f"{n}{g}" for n in ("x_sb", "w_mm", "w_sb", "p_mm") for g in range(3)]
        E = {n: nc.alloc_semaphore("r_" + n) for n in names}
        ev = lambda name: E[name]

        w_v = I["w_in"].rearrange("(k p) n -> p k n", p=P)
        masks, see, pick = M.masks, M.see, M.pick
        I_, BLK, NBD = 0, 1, 2
        MB = 3
        LV = 4
        unit = lambda c, h: 2 * c + h
        chunk = lambda t, c: t[:, c * P:(c + 1) * P]
        H0, H1 = slice(0, RH), slice(RH, P)
        halves = (H0, H1)
        block = ctx.enter_context(nc.Block())

        @block.sync
        def _(sp):
            sp.wait_ge(ev("zeroed"), 1)

            def weights(hp):
                cols = lambda at: bass.ds(hp * P + at, P)
                for n, at in enumerate((C_SH + S_R, C_SH + S_K, C_SH + S_V, C_ZB)):
                    sp.dma_start(w[:, n, :, :], w_v[:, :, cols(at)]).then_inc(ev("w_in"), 16)
                sp.dma_start(wlo[H0, 0, :], I["w_decay2"][:, cols(0)]).then_inc(ev("w_in"), 16)
                sp.dma_start(wlo[H1, 1, :], I["w_a2"][:, cols(0)]).then_inc(ev("w_in"), 16)

            def states_in(hp):
                for h in range(2):
                    src = I["state_wkv"][:, bass.ds(2 * hp + h, 1), :, :].rearrange("b h i j -> i (b h) j")
                    sp.dma_start(s_in[:, :, h * RH:(h + 1) * RH], src).then_inc(ev("s_in"), 16)

            def states_out(hp):
                sp.wait_ge(ev("state_out"), 2 * hp + 2)
                for h in range(2):
                    dst = O["wkv_s"][:, bass.ds(2 * hp + h, 1), :, :].rearrange("b h i j -> i (b h) j")
                    sp.dma_start(dst, s_out[:, :, h * RH:(h + 1) * RH]).then_inc(ev("stored"), 16)
                    dst = O["wkv_p"][0, bass.ds(2 * hp + h, 1), :, :].rearrange("h i j -> (h i) j")
                    sp.dma_start(dst, sp_out[halves[h], halves[h]]).then_inc(ev("stored"), 16)

            def branch_out(hp):
                sp.wait_ge(ev("out_sb"), hp + 1)
                sp.dma_start(M.ob_dram[:, bass.ds(hp, 1), :].rearrange("p k t -> p (k t)"), ob[:, :]).then_inc(ev("ob_out"), 16)

            weights(0)
            states_in(0)
            with sp.Fori(0, NP - 1) as hp:
                sp.wait_ge(ev("lora_mm"), hp + 1)
                weights(hp + 1)
                sp.wait_ge(ev("s0_tr"), hp + 1)
                states_in(hp + 1)
                branch_out(hp)
                states_out(hp)
            states_out(NP - 1)
            branch_out(NP - 1)
            sp.wait_ge(ev("stored"), 64 * NP)
            sp.wait_ge(ev("ob_out"), 16 * NP)

        @block.tensor
        def _(pe):
            mm, tr = nc.tensor.matmul, nc.tensor.transpose
            with pe.Fori(0, NP) as hp:
                once = lambda name: pe.wait_ge(ev(name), hp + 1)
                pe.wait_ge(ev("w_in"), hp * 96 + 96)
                pe.wait_ge(ev("out_sb"), hp)
                pe.wait_ge(ev("state_out"), 2 * hp)
                for n in range(4):
                    for k in range(KT):
                        last = mm(bank[3][:, n * P:(n + 1) * P], w[:, n, k, :], M.hT[:, k, SEQ:TOK], start=(k == 0), stop=(k == KT - 1))
                for n, b in enumerate((0, 1, 2, 4)):
                    for k in range(KT):
                        last = mm(bank[b][:, :], w[:, n, k, :], M.hT[:, k, 0:SEQ], start=(k == 0), stop=(k == KT - 1))
                    last.then_inc(ev("proj"), 1)
                for n in range(2):
                    mm(bank[5 + n][:, :], wlo[:, n, :], M.la[:, 0:SEQ], start=True, stop=True)
                    last = mm(bank[7][:, n * P:(n + 1) * P], wlo[:, n, :], M.la[:, SEQ:TOK], start=True, stop=True)
                last.then_inc(ev("lora_mm"), 1)
                once("kk_sq")
                pe.wait_ge(ev("proj_sb"), hp + 1)
                mm(bank[0][:, :], masks[:, BLK, :], Z[:, 0:SEQ], start=True, stop=True)
                mm(bank[3][:, 0:P], masks[:, BLK, :], Z[:, SEQ:TOK], start=True, stop=True).then_inc(ev("kk_sum"), 1)
                once("rk_prod")
                mm(bank[1][:, :], masks[:, BLK, :], rn[:, 0:SEQ], start=True, stop=True)
                mm(bank[2][:, 0:P], masks[:, BLK, :], rn[:, SEQ:TOK], start=True, stop=True).then_inc(ev("rk_sum"), 1)
                once("zbk")
                for c in range(C5):
                    b = (4, 5, 6, 7, 0)[c]
                    for n, src in enumerate((Z[:, :], B[:, :], K[:, :], xs[:, 2, :])):
                        last = tr(bank[b][:, n * P:(n + 1) * P], chunk(src, c), M.ident[:, :])
                    last.then_inc(ev("tm_tr"), 1)
                once("zr")
                once("bonus")
                for u in range(NU):
                    c, h = u // 2, u % 2
                    if u == 0:
                        pe.wait_ge(ev("tm_sb"), hp * C5 + 5)
                    if u >= 3:
                        pe.wait_ge(ev("gram_sb"), hp * NU + u - 2)
                    b = bank[u % 3]
                    mm(b[:, 0:256], chunk(K, c), ZR[:, h, :, c * P:(c + 1) * P], start=True, stop=True)
                    mm(b[:, 256:512], chunk(B, c), ZR[:, h, :, c * P:(c + 1) * P], start=True, stop=True).then_inc(ev("gram"), 1)
                once("x_first")
                for lv in range(len(LEVELS)):
                    groups = (0, 1, 2) if lv < 2 else (0, 1)
                    for gr in groups:
                        us = range(4 * gr, min(4 * gr + 4, NU))
                        pe.wait_ge(ev("nb"), hp * 6 + lv + 1)
                        pe.wait_ge(ev(f"x_sb{gr}"), hp * (3 if gr == 2 else 7) + lv + 1)
                        for j, u in enumerate(us):
                            last = mm(bank[gr][:, j * P:(j + 1) * P], Nb[:, u, :], XT[:, u, :], start=True, stop=True)
                        last.then_inc(ev(f"w_mm{gr}"), 1)
                    for gr in groups:
                        us = range(4 * gr, min(4 * gr + 4, NU))
                        pe.wait_ge(ev(f"w_sb{gr}"), hp * (2 if gr == 2 else 6) + lv + 1)
                        pX = (bank[3], bank[5], bank[7])[gr]
                        pT = (bank[4], bank[6], bank[7])[gr]
                        for j, u in enumerate(us):
                            last = mm(pX[:, j * P:(j + 1) * P], W[:, u, :], X[:, u, :], start=True, stop=True)
                        if lv == 4:
                            off = 256 if gr == 2 else 0
                            for j, u in enumerate(us):
                                last = mm(pT[:, off + j * P:off + (j + 1) * P], X[:, u, :], W[:, u, :], start=True, stop=True)
                        last.then_inc(ev(f"p_mm{gr}"), 1)
                for u in range(NU):
                    c, h = u // 2, u % 2
                    last = mm(bank[0 if u < 8 else 1][:, (u % 8) * RH:(u % 8 + 1) * RH], gram[:, u, 0, :], tm[:, c, 3, h * RH:(h + 1) * RH], start=True, stop=True)
                last.then_inc(ev("zkv"), 1)
                once("zw")
                for gr in range(3):
                    pe.wait_ge(ev(f"x_sb{gr}"), (hp + 1) * (3 if gr == 2 else 7))
                for u in range(NU):
                    last = mm(bank[2 + u // 4][:, (u % 4) * P:(u % 4 + 1) * P], X[:, u, :], Nb[:, u, :], start=True, stop=True)
                last.then_inc(ev("y_mm"), 1)
                once("y_sb")
                for c in range(C5):
                    b = bank[5 + c // 2]
                    at = (c % 2) * 256
                    for h in range(2):
                        u = unit(c, h)
                        mm(b[halves[h], at:at + P], Zt[:, u, :], gram[:, u, 3, :], start=True, stop=True)
                        last = mm(b[halves[h], at + P:at + 256], Zt[:, u, :], tm[:, c, 1, :], start=True, stop=True)
                last.then_inc(ev("rt_mm"), 1)
                for c in range(PB):
                    mm(bank[0][:, c * P:(c + 1) * P], tm[:, c, 1, :], U0[:, c, :, :].rearrange("p h i -> p (h i)"), start=True, stop=False)
                    last = mm(bank[0][:, c * P:(c + 1) * P], tm[:, c, 2, :], tm[:, c, 3, :], start=False, stop=True)
                last.then_inc(ev("psi_mm"), 1)
                pe.wait_ge(ev("s_in"), hp * 32 + 32)
                pe.sem_inc(ev("pe_past"), 1)
                for b in range(BD):
                    last = tr(bank[2][:, b * RH:(b + 1) * RH], s_in[:, b, :], M.ident[0:RH, 0:RH])
                last.then_inc(ev("s0_tr"), 1)
                for h in range(2):
                    last = mm(bank[3][halves[h], 0:SB], tm[:, PB, 0, h * RH:(h + 1) * RH], X[:, unit(PB, h), 0:SB], start=True, stop=True)
                last.then_inc(ev("zs_mm"), 1)
                once("rt_sb")
                for c in range(1, PB):
                    pe.wait_ge(ev("s_next"), hp * PB + c)
                    mm(bank[4][:, (c - 1) * P:c * P], Phi[:, c, :], S[:, c, :], start=True, stop=True).then_inc(ev("phi_mm"), 1)
                for c in range(C5):
                    b = bank[1] if c < PB else bank[5]
                    at = (c % PB) * P
                    for h in range(2):
                        u = unit(c, h)
                        out = b[:, at + h * RH:at + (h + 1) * RH]
                        mm(out, gram[:, u, 3, :], U0[:, c, h, :], start=True, stop=False)
                        last = mm(out, gram[:, u, 1, :], tm[:, c, 3, h * RH:(h + 1) * RH], start=False, stop=not 1 <= c < PB)
                        if 1 <= c < PB:
                            last = mm(out, RT[:, c, :], S[:, c, h * RH:(h + 1) * RH], start=False, stop=True)
                last.then_inc(ev("o_mm"), 1)
                once("s0_sb")
                for n in range(4):
                    q, h = n // 2, n % 2
                    b = bank[(6, 7, 2, 3)[n]]
                    lhs = ZsT[:, :] if q == 0 else RT[:, PB, 0:SB]
                    mm(b[0:SB, :], lhs, s0p[:, h, :, :].rearrange("p b i -> p (b i)"), start=True, stop=True).then_inc(ev("seen"), 1)
                pe.wait_ge(ev("s_next"), hp * PB + PB)
                once("bk2")
                once("o_sb")
                tr(bank[0][:, 0:P], S[:, PB, :], M.ident[:, :])
                tr(bank[0][:, P:2 * P], bk2[:, :], M.ident[:, :])
                tr(bank[4][:, 0:P], uv[:, :], M.ident[:, :]).then_inc(ev("bk_tr"), 1)
                once("on")
                for c in range(C5):
                    src = o[:, 2 * c:2 * c + 2, :].rearrange("p h i -> p (h i)")
                    last = tr(bank[1 if c < PB else 5][:, (c % PB) * P:(c % PB + 1) * P], src, M.ident[:, :])
                last.then_inc(ev("o_tr"), 1)
                once("uvm")
                for n in range(2):
                    last = mm(bank[2 + n][:, :], bkT[:, :], uvm[:, 4 * n:4 * n + 4, :].rearrange("p b i -> p (b i)"), start=True, stop=True)
                last.then_inc(ev("sn_mm"), 1)
                once("sn")
                pe.sem_inc(ev("pe_past"), 1)
                for b in range(BD):
                    last = tr(bank[6 + b // 4][0:RH, (b % 4) * P:(b % 4 + 1) * P], snT[:, b, :], M.ident[:, :])
                last.then_inc(ev("sn_tr"), 1)

        @block.scalar
        def _(act):
            a = nc.scalar
            with act.Fori(0, NP) as hp:
                once = lambda name: act.wait_ge(ev(name), hp + 1)
                vcol = lambda t, at: t[:, bass.ds(hp + at, 1)]
                for n in range(3):
                    act.wait_ge(ev("proj"), 4 * hp + n + 1)
                    a.copy(px[:, n, 1:SEQ + 1], bank[n][:, :])
                    a.copy(pxs[:, n, :, 1:TD + 1], bank[3][:, n * P:n * P + SB].rearrange("p (b t) -> p b t", t=TD)).then_inc(ev("px"), 1)
                act.wait_ge(ev("proj"), 4 * hp + 4)
                a.copy(zb[:, 0:SEQ], bank[4][:, :])
                a.copy(zb[:, SEQ:TOK], bank[3][:, 3 * P:4 * P])
                a.activation(bonus[:, 0:SEQ], bank[4][:, :], ACT.Exp, scale=-1.0)
                a.activation(bonus[:, SEQ:TOK], bank[3][:, 3 * P:4 * P], ACT.Exp, scale=-1.0).then_inc(ev("proj_sb"), 1)
                once("lora_mm")
                for n, at in enumerate((0, V_A0 - V_W0)):
                    a.activation(sa[:, n, 0:SEQ], bank[5 + n][:, :], ACT.Exp, bias=vcol(M.nvec, at), scale=-1.0)
                    last = a.activation(sa[:, n, SEQ:TOK], bank[7][:, n * P:(n + 1) * P], ACT.Exp, bias=vcol(M.nvec, at), scale=-1.0)
                last.then_inc(ev("sa"), 1)
                once("cum")
                a.activation(g[:, :], gx[:, :], ACT.Exp, scale=LD)
                a.activation(dx[:, 0, :], L[:, :], ACT.Exp, scale=LD)
                a.activation(dx[:, 1, :], Lx[:, :], ACT.Exp, scale=LD)
                a.activation(dx[:, 2, :], L[:, :], ACT.Exp, scale=-LD).then_inc(ev("expd"), 1)
                once("kk_max")
                a.activation(rn[:, :], rn[:, :], ACT.Sqrt).then_inc(ev("rn"), 1)
                for c in range(C5):
                    b = (4, 5, 6, 7, 0)[c]
                    act.wait_ge(ev("tm_tr"), hp * C5 + c + 1)
                    a.copy(tm[:, c, :, :], bank[b][:, :].rearrange("p (n t) -> p n t", t=P)).then_inc(ev("tm_sb"), 1)
                for lv in range(len(LEVELS)):
                    for gr in ((0, 1, 2) if lv < 2 else (0, 1)):
                        us = slice(4 * gr, min(4 * gr + 4, NU))
                        n = us.stop - us.start
                        act.wait_ge(ev(f"w_mm{gr}"), hp * (2 if gr == 2 else 6) + lv + 1)
                        a.copy(W[:, us, :], bank[gr][:, 0:n * P].rearrange("p (u t) -> p u t", t=P)).then_inc(ev(f"w_sb{gr}"), 1)
                once("zkv")
                once("z_in_nb")
                a.copy(Nb[:, 0:8, RH:P], bank[0][:, :].rearrange("p (u i) -> p u i", i=RH))
                a.copy(Nb[:, 8:NU, RH:P], bank[1][:, 0:2 * RH].rearrange("p (u i) -> p u i", i=RH)).then_inc(ev("zw"), 1)
                once("y_mm")
                for gr in range(3):
                    n = min(4, NU - 4 * gr)
                    y = bank[2 + gr][:, 0:n * P].rearrange("p (u a i) -> p u a i", a=2, i=RH)
                    a.copy(Zt[:, 4 * gr:4 * gr + n, :], y[:, :, 0, :])
                    last = a.mul(U0[:, 2 * gr:2 * gr + n // 2, :, :].rearrange("p c h i -> p (c h) i"), y[:, :, 1, :], -1.0)
                last.then_inc(ev("y_sb"), 1)
                once("zs_mm")
                a.copy(ZsT[:, :], bank[3][:, 0:SB]).then_inc(ev("zsT"), 1)
                once("o_mm")
                a.copy(o[:, 0:8, :], bank[1][:, :].rearrange("p (u i) -> p u i", i=RH))
                a.copy(o[:, 8:NU, :], bank[5][:, 0:P].rearrange("p (u i) -> p u i", i=RH)).then_inc(ev("o_sb"), 1)
                once("bk_tr")
                act.wait_ge(ev("stored"), 64 * hp)
                a.copy(sp_out[:, :], bank[0][:, 0:P]).then_inc(ev("state_out"), 1)
                a.copy(bkT[:, :], bank[0][:, P:2 * P]).then_inc(ev("bkT"), 1)
                once("sn_tr")
                for n in range(2):
                    last = a.copy(s_out[:, 4 * n:4 * n + 4, :], bank[6 + n][0:RH, :].rearrange("p (b t) -> p b t", t=P))
                last.then_inc(ev("state_out"), 1)

        @block.gpsimd
        def _(pool):
            p = nc.gpsimd
            p.memset(wlo[:, :, :], 0.0)
            p.memset(ZR[:, :, :, :], 0.0)
            p.memset(s0p[:, :, :, :], 0.0)
            p.memset(gram[:, :, :, :], 0.0)
            p.memset(xs[:, :, SEQ + SB:TOK], 0.0)
            p.memset(bk2[:, :], 0.0)
            p.memset(uv[:, :], 0.0)
            p.memset(M.mhalf[:, :], -0.5)
            p.memset(px[:, :, 0:1], 0.0).then_inc(ev("zeroed"), 1)
            with pool.Fori(0, NP) as hp:
                once = lambda name: pool.wait_ge(ev(name), hp + 1)
                pool.wait_ge(ev("mixed"), hp)
                p.tensor_copy(pxs[:, :, :, 0], M.ss[:, 0:24, :].rearrange("p (n k) b -> p n k b", k=NP)[:, :, bass.ds(hp, 1), :].rearrange("p n k b -> p n (k b)")).then_inc(ev("pxs0"), 1)
                pool.wait_ge(ev("px"), 3 * hp + 3)
                pool.sem_inc(ev("pool_past"), 1)
                shc = M.shc[:, 0:24, :].rearrange("p (n k) b -> p n k b", k=NP)[:, :, bass.ds(hp, 1), :].rearrange("p n k b -> p n (k b)")
                p.tensor_copy(shc[:, :, 0:1], px[:, :, SEQ:SEQ + 1])
                p.tensor_copy(shc[:, :, 1:1 + BD], pxs[:, :, :, TD]).then_inc(ev("shc"), 1)
                p.drain()
                once("zbk")
                pool.sem_inc(ev("pool_past"), 1)
                for h in range(2):
                    rows = halves[h]
                    p.tensor_copy(ZR[rows, h, 0, :], Z[rows, :])
                    last = p.tensor_copy(ZR[rows, h, 1, :], R[rows, :])
                last.then_inc(ev("zr"), 1)
                pool.wait_ge(ev("gram_sb"), hp * NU + NU)
                for lv in range(len(LEVELS)):
                    n = NU if lv < 2 else 8
                    if lv:
                        pool.wait_ge(ev("w_mm0"), hp * 6 + lv)
                        pool.wait_ge(ev("w_mm1"), hp * 6 + lv)
                        if lv <= 2:
                            pool.wait_ge(ev("w_mm2"), hp * 2 + lv)
                    p.tensor_tensor(Nb[:, 0:n, :], gram[:, 0:n, 2, :], bc(masks[:, LV + lv, :], n, 1), ALU.mult).then_inc(ev("nb"), 1)
                pool.wait_ge(ev("w_mm0"), hp * 6 + 6)
                pool.wait_ge(ev("w_mm1"), hp * 6 + 6)
                pool.sem_inc(ev("pool_past"), 1)
                p.tensor_copy(Nb[:, :, 0:RH].rearrange("p (c h) i -> p c h i", h=2), tm[:, :, 0, :].rearrange("p c (h i) -> p c h i", h=2)).then_inc(ev("z_in_nb"), 1)
                once("var")
                p.tensor_tensor(om[:, 1, :], om[:, 1, :], M.mhalf[:, 0:1].to_broadcast([P, NU]), ALU.pow).then_inc(ev("rstd"), 1)

        @block.vector
        def _(dve):
            v = nc.vector
            tt, ts, stt = v.tensor_tensor, v.tensor_scalar, v.scalar_tensor_tensor
            dr = dve.drain
            by_b = lambda t: t.rearrange("p (b t) -> p b t", t=TD)
            dve.wait_ge(ev("zeroed"), 1)
            with dve.Fori(0, NP) as hp:
                once = lambda name: dve.wait_ge(ev(name), hp + 1)
                vcol = lambda at: M.vec[:, bass.ds(hp + at, 1)]
                dve.wait_ge(ev("px"), 3 * hp + 3)
                once("pxs0")
                tt(dx[:, :, 0:SEQ], px[:, :, 0:SEQ], px[:, :, 1:SEQ + 1], ALU.subtract)
                for n in range(3):
                    tt(by_b(dx[:, n, SEQ:SEQ + SB]), pxs[:, n, :, 0:TD], pxs[:, n, :, 1:TD + 1], ALU.subtract)
                dr()
                for n in range(3):
                    stt(xs[:, n, 0:SEQ], dx[:, n, 0:SEQ], vcol(V_MU + 8 * n), px[:, n, 1:SEQ + 1], ALU.mult, ALU.add)
                    last = stt(by_b(xs[:, n, SEQ:SEQ + SB]), by_b(dx[:, n, SEQ:SEQ + SB]), vcol(V_MU + 8 * n), pxs[:, n, :, 1:TD + 1], ALU.mult, ALU.add)
                last.then_inc(ev("mixed"), 1)
                dr()
                ts(kk[:, :], xs[:, 1, :], vcol(V_KK), None, ALU.mult)
                dr()
                tt(Z[:, :], kk[:, :], kk[:, :], ALU.mult).then_inc(ev("kk_sq"), 1)
                once("proj_sb")
                ts(bonus[:, :], bonus[:, :], 1.0, None, ALU.add)
                dr()
                v.reciprocal(bonus[:, :], bonus[:, :])
                dr()
                tt(zb[:, :], zb[:, :], bonus[:, :], ALU.mult)
                once("sa")
                ts(sa[:, :, :], sa[:, :, :], 1.0, None, ALU.add)
                dr()
                v.reciprocal(sa[:, :, :], sa[:, :, :])
                dr()
                v.tensor_tensor_scan(L[:, :], M.seg[:, :], sa[:, 0, :], 0.0, ALU.mult, ALU.add)
                dr()
                Lp = L[:, 0:SEQ].rearrange("p (c t) -> p c t", t=P)
                v.tensor_copy(cen[:, 0:PB], Lp[:, :, P // 2 - 1])
                v.memset(cen[:, PB:PB + 1], 0.0)
                v.tensor_copy(gx[:, PB:PB + BD], by_b(L[:, SEQ:SEQ + SB])[:, :, TD - 1])
                dr()
                tt(gx[:, 0:PB], Lp[:, :, P - 1], cen[:, 0:PB], ALU.subtract)
                dr()
                tt(gx[:, 0:PB], gx[:, 0:PB], cen[:, 1:PB + 1], ALU.add)
                tt(Lp, Lp, bc(cen[:, 0:PB], P, 2), ALU.subtract)
                dr()
                tt(Lx[:, :], L[:, :], sa[:, 0, :], ALU.subtract).then_inc(ev("cum"), 1)
                once("kk_sum")
                ts(rn[:, 0:SEQ], bank[0][:, :], 1e-24, None, ALU.max)
                ts(rn[:, SEQ:TOK], bank[3][:, 0:P], 1e-24, None, ALU.max).then_inc(ev("kk_max"), 1)
                dve.wait_ge(ev("ob_out"), 16 * hp)
                ts(kf[:, :], sa[:, 1, :], 1.0, vcol(V_KA), ALU.subtract, ALU.mult)
                dr()
                stt(kf[:, :], kf[:, :], 1.0, xs[:, 1, :], ALU.add, ALU.mult)
                once("rn")
                v.reciprocal(rn[:, :], rn[:, :])
                dr()
                tt(kk[:, :], kk[:, :], rn[:, :], ALU.mult)
                dr()
                stt(rn[:, :], xs[:, 0, :], vcol(V_RK), kf[:, :], ALU.mult, ALU.mult).then_inc(ev("rk_prod"), 1)
                once("expd")
                tt(Z[:, :], kk[:, :], dx[:, 1, :], ALU.mult)
                tt(R[:, :], xs[:, 0, :], dx[:, 0, :], ALU.mult)
                tt(K[:, :], kf[:, :], dx[:, 2, :], ALU.mult)
                tt(B[:, :], kk[:, :], sa[:, 1, :], ALU.mult)
                dr()
                tt(B[:, :], B[:, :], dx[:, 2, :], ALU.mult).then_inc(ev("zbk"), 1)
                dr()
                v.tensor_copy(bk2[:, 0:SB], B[:, SEQ:SEQ + SB])
                v.tensor_copy(bk2[:, SB:2 * SB], K[:, SEQ:SEQ + SB])
                v.tensor_copy(uv[:, SB:2 * SB], xs[:, 2, SEQ:SEQ + SB]).then_inc(ev("bk2"), 1)
                once("rk_sum")
                tt(bonus[:, 0:SEQ], bank[1][:, :], xs[:, 2, 0:SEQ], ALU.mult)
                tt(bonus[:, SEQ:TOK], bank[2][:, 0:P], xs[:, 2, SEQ:TOK], ALU.mult).then_inc(ev("bonus"), 1)
                for u in range(NU):
                    m = 0 if u < 8 else 1
                    dve.wait_ge(ev("gram"), hp * NU + u + 1)
                    dve.sem_inc(ev("dve_past"), 1)
                    v.copy_predicated(gram[:, u, :, :].rearrange("p a t -> p (a t)"), see[:, m, :], bank[u % 3][:, :]).then_inc(ev("gram_sb"), 1)
                def transposed(us):
                    return v.transpose(XT[:, us, :].rearrange("p u t -> p (u t)"), X[:, us, :].rearrange("p u t -> p (u t)"))

                dr()
                one = bc(masks[:, I_, :], 4, 1)
                for gr in range(3):
                    n = min(4, NU - 4 * gr)
                    us = slice(4 * gr, 4 * gr + n)
                    tt(X[:, us, :], gram[:, us, 2, :], bc(masks[:, MB, :], n, 1), ALU.mult)
                    dr()
                    tt(X[:, us, :], one[:, 0:n, :], X[:, us, :], ALU.subtract)
                    dr()
                    transposed(us).then_inc(ev(f"x_sb{gr}"), 1)
                dve.nop().then_inc(ev("x_first"), 1)
                for lv in range(len(LEVELS)):
                    for gr in ((0, 1, 2) if lv < 2 else (0, 1)):
                        n = min(4, NU - 4 * gr)
                        us = slice(4 * gr, 4 * gr + n)
                        dve.wait_ge(ev(f"p_mm{gr}"), hp * (2 if gr == 2 else 6) + lv + 1)
                        pX = (bank[3], bank[5], bank[7])[gr][:, 0:n * P].rearrange("p (u t) -> p u t", t=P)
                        off = 256 if gr == 2 else 0
                        pT = (bank[4], bank[6], bank[7])[gr][:, off:off + n * P].rearrange("p (u t) -> p u t", t=P)
                        last = tt(X[:, us, :], X[:, us, :], pX, ALU.subtract)
                        if lv < 4:
                            dr()
                            last = transposed(us)
                        elif lv == 4:
                            last = tt(XT[:, us, :], XT[:, us, :], pT, ALU.subtract)
                        last.then_inc(ev(f"x_sb{gr}"), 1)
                    dr()
                once("rt_mm")
                for q in range(3):
                    n = min(2, C5 - 2 * q)
                    got = bank[5 + q][:, 0:n * 256].rearrange("p (c a t) -> p c a t", a=2, t=P)
                    tt(RT[:, 2 * q:2 * q + n, :], R[:, 2 * q * P:(2 * q + n) * P].rearrange("p (c t) -> p c t", t=P), got[:, :, 0, :], ALU.subtract)
                    if q < 2:
                        tt(Phi[:, 2 * q:2 * q + 2, :], got[:, :, 1, :], bc(masks[:, NBD, :], 2, 1), ALU.mult)
                dr()
                tt(Phi[:, :, :], Phi[:, :, :], bc(masks[:, I_, :], PB, 1), ALU.add).then_inc(ev("rt_sb"), 1)
                once("psi_mm")
                for c in range(PB):
                    stt((S[:, 1, :] if c == 0 else Psi[:, c, :]), bank[0][:, c * P:(c + 1) * P], g[:, c:c + 1], masks[:, BLK, :], ALU.mult, ALU.mult)
                dr()
                dve.nop().then_inc(ev("s_next"), 1)
                for c in range(1, PB):
                    dve.wait_ge(ev("phi_mm"), hp * (PB - 1) + c)
                    stt(S[:, c + 1, :], bank[4][:, (c - 1) * P:c * P], g[:, c:c + 1], Psi[:, c, :], ALU.mult, ALU.add).then_inc(ev("s_next"), 1)
                    if c == 1:
                        once("s0_tr")
                        v.tensor_copy(s0T[:, :, :], bank[2][:, :].rearrange("p (b i) -> p b i", i=RH))
                        for h in range(2):
                            v.tensor_copy(s0p[halves[h], h, :, :], bank[2][halves[h], :].rearrange("p (b i) -> p b i", i=RH))
                        once("zsT")
                        dve.nop().then_inc(ev("s0_sb"), 1)
                for n in range(4):
                    dve.wait_ge(ev("seen"), 4 * hp + n + 1)
                    tt(selp[:, :, :], bank[(6, 7, 2, 3)[n]][0:SB, :].rearrange("p (b i) -> p b i", i=RH), bc(pick[:, 0:BD][0:SB], RH, 2), ALU.mult)
                    dr()
                    v.tensor_reduce(picked[:, n, :], selp[:, :, :].rearrange("p b i -> p i b"), AX.X, ALU.add)
                    dr()
                once("bk_tr")
                tt(uv[0:SB, :].rearrange("p (h i) -> p h i", h=2), U0[0:SB, PB, :, :], picked[:, 0:2, :], ALU.subtract)
                v.tensor_copy(uv[SB:P, :], bank[4][SB:P, 0:P])
                dr()
                tt(uvm[:, :, :], bc(uv[:, :], BD, 1), bc(pick[:, 0:BD], P, 2), ALU.mult)
                dr()
                v.memset(uv[:, 0:SB], 0.0)
                once("bkT")
                dve.nop().then_inc(ev("uvm"), 1)
                once("o_sb")
                tt(o[0:SB, 8:NU, :], o[0:SB, 8:NU, :], picked[:, 2:4, :], ALU.add)
                dr()
                v.tensor_reduce(om[:, 0, :], o[:, :, :], AX.X, ALU.add)
                dr()
                ts(om[:, 0, :], om[:, 0, :], 1.0 / RH, None, ALU.mult)
                dr()
                tt(o[:, :, :], o[:, :, :], bc(om[:, 0, :], RH, 2), ALU.subtract)
                dr()
                tt(osq[:, :, :], o[:, :, :], o[:, :, :], ALU.mult)
                dr()
                v.tensor_reduce(om[:, 1, :], osq[:, :, :], AX.X, ALU.add)
                dr()
                ts(om[:, 1, :], om[:, 1, :], 1.0 / RH, GN_EPS, ALU.mult, ALU.add).then_inc(ev("var"), 1)
                once("rstd")
                tt(o[:, :, :], o[:, :, :], bc(om[:, 1, :], RH, 2), ALU.mult).then_inc(ev("on"), 1)
                once("o_tr")
                for cols, b, n in ((slice(0, SEQ), bank[1], SEQ), (slice(SEQ, TOK), bank[5], P)):
                    ts(ob[:, cols], b[:, 0:n], vcol(V_GG), vcol(V_GB), ALU.mult, ALU.add)
                dr()
                tt(ob[:, :], ob[:, :], bonus[:, :], ALU.add)
                dr()
                tt(ob[:, :], ob[:, :], zb[:, :], ALU.mult).then_inc(ev("out_sb"), 1)
                once("sn_mm")
                for n in range(2):
                    bs = slice(4 * n, 4 * n + 4)
                    for h in range(2):
                        rows = halves[h]
                        got = bank[2 + n][rows, :].rearrange("p (b h i) -> p b h i", b=4, h=2)[:, :, h, :]
                        tt(snT[rows, bs, :], s0T[rows, bs, :], got, ALU.add)
                dr()
                tt(snT[:, :, :], snT[:, :, :], bc(g[:, PB:PB + BD], RH, 2), ALU.mult).then_inc(ev("sn"), 1)


def store_shift(nc, O, M):
    with ExitStack() as ctx:
        shrow = ctx.enter_context(nc.sbuf_tensor("shrow", [1 + BD, 25, P], F32))
        bank = [ctx.enter_context(nc.psum_tensor(f"sh_bank{i}", [P, 512], F32)) for i in range(7)]
        tr, tr_sb, stored = (nc.alloc_semaphore("sh_" + n) for n in ("tr", "tr_sb", "stored"))
        block = ctx.enter_context(nc.Block())

        @block.tensor
        def _(pe):
            for k in range(25):
                last = nc.tensor.transpose(bank[k // 4][0:1 + BD, (k % 4) * P:(k % 4 + 1) * P], M.shc[:, k, :], M.ident[:, :])
            last.then_inc(tr, 1)

        @block.vector
        def _(dve):
            dve.wait_ge(tr, 1)
            for q in range(7):
                n = min(4, 25 - 4 * q)
                last = nc.vector.tensor_copy(shrow[:, 4 * q:4 * q + n, :], bank[q][0:1 + BD, 0:n * P].rearrange("p (k t) -> p k t", t=P))
            last.then_inc(tr_sb, 1)

        @block.sync
        def _(sp):
            sp.wait_ge(tr_sb, 1)
            n = 0
            for rows, dst in ((slice(0, 1), O["shift_p"]), (slice(1, 1 + BD), O["shift_s"])):
                for i, at in enumerate((S_R, S_K, S_V)):
                    sp.dma_start(dst[:, at:at + 1024].rearrange("b (k p) -> b k p", p=P), shrow[rows, 8 * i:8 * i + 8, :]).then_inc(stored, 16)
                for half, at in enumerate((S_WL, S_AL)):
                    sp.dma_start(dst[:, at:at + 64], shrow[rows, 24, 64 * half:64 * half + 64]).then_inc(stored, 16)
                n += 5
            sp.wait_ge(stored, 16 * n)


def merge(nc, I, O, M):
    with ExitStack() as ctx:
        sb = lambda name, shape: ctx.enter_context(nc.sbuf_tensor("me_" + name, shape, F32))
        ps = lambda name: ctx.enter_context(nc.psum_tensor("me_" + name, [P, 512], F32))
        sem = lambda name: ctx.enter_context(nc.semaphore("m_" + name))
        w = [sb(f"w{i}", [P, 4, KT, P]) for i in range(2)]
        wo = sb("wo", [P, KT, D])
        oaT, obT = sb("oaT", [P, KT, TOK]), sb("obT", [P, KT, TOK])
        mT, sg, t = sb("mT", [P, KT, TOK]), sb("sg", [P, 2, TOK]), sb("t", [P, 2, TOK])
        sel, gs = sb("sel", [1 + BD, 2 * P]), sb("gs", [P, 2, D])
        xb = [sb(f"xb{i}", [P, D]) for i in range(2)]
        big, small = [ps(f"big{i}") for i in range(4)], [ps("small0"), ps("small1")]
        psY = [ps("psY0"), ps("psY1")]
        w_in_sb, x_in, y_out = [sem("w_in0"), sem("w_in1")], [sem("x_in0"), sem("x_in1")], [sem("y_out0"), sem("y_out1")]
        branch_in = sem("branch_in")
        fixed_in, proj, gated, summed, m_done, spread, spread_sb, y_mm, y_sb = (
            sem(n) for n in ("fixed_in", "proj", "gated", "summed", "m_done", "spread", "spread_sb", "y_mm", "y_sb"))
        w_v = I["w_in"].rearrange("(k p) n -> p k n", p=P)
        pa_v, pb_v = (I[n].rearrange("(k p) n -> p k n", p=P) for n in ("w_pa", "w_pb"))
        rows = lambda b: P if b < PB else SB
        block = ctx.enter_context(nc.Block())

        @block.sync
        def _(sp):
            def load(b, j):
                for n, (src, at) in enumerate(((w_v, C_GA), (w_v, C_GB), (pa_v, 0), (pb_v, 0))):
                    sp.dma_start(w[b][:, n, :, :], src[:, :, bass.ds(j * P + at, P)]).then_inc(w_in_sb[b], 16)

            def x_of(b):
                src = I["x_prompt"][0, b * P:(b + 1) * P, :] if b < PB else I["x_sample"].rearrange("b t d -> (b t) d")
                sp.dma_start(xb[b % 2][0:rows(b), :], src).then_inc(x_in[b % 2], 16)

            load(0, 0)
            sp.dma_start(oaT[:, :, :], M.oa_dram).then_inc(branch_in, 16)
            sp.dma_start(obT[:, :, :], M.ob_dram).then_inc(branch_in, 16)
            load(1, 1)
            sp.dma_start(sel[:, :], I["sel"]).then_inc(fixed_in, 16)
            with sp.Fori(1, KT // 2) as i:
                for b in range(2):
                    sp.wait_ge(proj, 4 * (2 * i + b - 1))
                    load(b, 2 * i + b)
            sp.dma_start(wo[:, :, :], I["w_out"].rearrange("(k p) n -> p k n", p=P)).then_inc(fixed_in, 16)
            x_of(0)
            x_of(1)
            for b in range(NB):
                sp.wait_ge(y_sb, 2 * b + 2)
                dst = O["y_p"][0, b * P:(b + 1) * P, :] if b < PB else O["y_s"].rearrange("b t d -> (b t) d")
                sp.dma_start(dst, xb[b % 2][0:rows(b), :]).then_inc(y_out[b % 2], 16)
                if b + 2 < NB:
                    sp.wait_ge(y_out[b % 2], 16 * (b // 2 + 1))
                    x_of(b + 2)
            sp.wait_ge(y_out[0], 16 * ((NB + 1) // 2))
            sp.wait_ge(y_out[1], 16 * (NB // 2))

        @block.tensor
        def _(pe):
            with pe.Fori(0, KT // 2) as i:
                for b in range(2):
                    j = 2 * i + b
                    pe.wait_ge(w_in_sb[b], i * 64 + 64)
                    for n, src in enumerate((M.hT, M.hT, oaT, obT)):
                        if n == 0:
                            pe.wait_ge(gated, 2 * j)
                            pe.wait_ge(summed, 2 * i)
                        if n == 2:
                            pe.wait_ge(branch_in, 32)
                            pe.wait_ge(summed, j)
                        for k in range(KT):
                            nc.tensor.matmul(big[n][:, :], w[b][:, n, k, :], src[:, k, 0:SEQ], start=(k == 0), stop=(k == KT - 1))
                        for k in range(KT):
                            last = nc.tensor.matmul(small[b][:, n * P:(n + 1) * P], w[b][:, n, k, :], src[:, k, SEQ:TOK], start=(k == 0), stop=(k == KT - 1))
                        last.then_inc(proj, 1)
            pe.wait_ge(fixed_in, 32)
            for q in range(4):
                if q >= 2:
                    pe.wait_ge(spread_sb, q - 1)
                nc.tensor.matmul(psY[q % 2][:, :], sel[:, (q // 2) * P:(q // 2 + 1) * P], M.gate[:, (q % 2) * 512:(q % 2 + 1) * 512],
                                 start=True, stop=True).then_inc(spread, 1)
            pe.wait_ge(m_done, KT)
            pe.wait_ge(spread_sb, 4)
            for b in range(NB):
                for n in range(2):
                    u = 2 * b + n
                    if u >= 2:
                        pe.wait_ge(y_sb, u - 1)
                    for k in range(KT):
                        last = nc.tensor.matmul(psY[n][0:rows(b), :], mT[:, k, b * P:b * P + rows(b)], wo[:, k, n * 512:(n + 1) * 512],
                                                start=(k == 0), stop=(k == KT - 1))
                    last.then_inc(y_mm, 1)

        @block.scalar
        def _(act):
            with act.Fori(0, KT // 2) as i:
                for b in range(2):
                    j = 2 * i + b
                    act.wait_ge(m_done, j)
                    for n in range(2):
                        act.wait_ge(proj, 4 * j + n + 1)
                        nc.scalar.activation(sg[:, n, 0:SEQ], big[n][:, :], ACT.Exp, scale=-1.0)
                        if n == 1:
                            act.wait_ge(proj, 4 * j + 4)
                            nc.scalar.activation(sg[:, 0, SEQ:TOK], small[b][:, 0:P], ACT.Exp, scale=-1.0).then_inc(gated, 1)
                            nc.scalar.activation(sg[:, 1, SEQ:TOK], small[b][:, P:2 * P], ACT.Exp, scale=-1.0).then_inc(gated, 1)
            for q in range(4):
                act.wait_ge(spread, q + 1)
                nc.scalar.copy(gs[:, q // 2, (q % 2) * 512:(q % 2 + 1) * 512], psY[q % 2][:, :]).then_inc(spread_sb, 1)

        @block.vector
        def _(dve):
            v = nc.vector
            with dve.Fori(0, KT // 2) as i:
                for b in range(2):
                    j = 2 * i + b
                    dve.wait_ge(gated, 2 * j + 2)
                    v.tensor_scalar(sg[:, :, :], sg[:, :, :], 1.0, None, ALU.add)
                    dve.drain()
                    v.reciprocal(sg[:, :, :], sg[:, :, :])
                    dve.drain()
                    for n in range(2):
                        v.tensor_tensor(t[:, n, 0:SEQ], big[2 + n][:, :], sg[:, n, 0:SEQ], ALU.mult)
                        last = v.tensor_tensor(t[:, n, SEQ:TOK], small[b][:, (2 + n) * P:(3 + n) * P], sg[:, n, SEQ:TOK], ALU.mult)
                    last.then_inc(summed, 1)
                    dve.drain()
                    v.tensor_tensor(mT[:, j, :], t[:, 0, :], t[:, 1, :], ALU.add).then_inc(m_done, 1)
            dve.wait_ge(spread_sb, 4)
            for b in range(NB):
                r = rows(b)
                for n in range(2):
                    cols = slice(n * 512, (n + 1) * 512)
                    dve.wait_ge(y_mm, 2 * b + n + 1)
                    if n == 0:
                        dve.wait_ge(x_in[b % 2], 16 * (b // 2 + 1))
                    acc = t[:, :, :].rearrange("p a t -> p (a t)")[0:r, n * 512:(n + 1) * 512]
                    v.tensor_tensor(acc, psY[n][0:r, :], gs[0:r, b // PB, cols], ALU.mult)
                    dve.drain()
                    v.tensor_tensor(xb[b % 2][0:r, cols], xb[b % 2][0:r, cols], acc, ALU.add).then_inc(y_sb, 1)


def constants():
    c = {}
    i = np.arange(P)
    c["ident"] = np.eye(P, dtype=np.float32)
    c["tri"] = np.where(i[None, :] <= i[:, None], 0.0, NEG).astype(np.float32)
    tok = np.arange(2 * P)
    owner = np.where(tok < P, 0, np.where(tok - P < SB, 1 + (tok - P) // TD, -1))
    c["sel"] = (owner[None, :] == np.arange(1 + BD)[:, None]).astype(np.float32)
    pos = np.concatenate([np.arange(SEQ), PAGES * PS + np.arange(P) % TD]).astype(np.float32)
    inv = np.float32(10000.0) ** (-np.arange(HALF, dtype=np.float32) / np.float32(HALF))
    ang = (pos[:, None] * inv[None, :]).reshape(NB, P, 1, HALF).transpose(1, 0, 2, 3)
    ang = np.repeat(ang, 2, axis=2)
    c["cos"], c["sin"] = np.cos(ang).astype(np.float32), np.sin(ang).astype(np.float32)
    k = np.arange(SB)
    seen = (k[:, None, None] // TD == np.arange(BD)[None, :, None]) & (k[:, None, None] % TD <= (np.arange(H * TD) % TD)[None, None, :])
    c["own_mask"] = np.where(seen, 0.0, NEG).astype(np.float32)
    a, b = np.meshgrid(i, i, indexing="ij")
    level = lambda n: ((a // (2 * n) == b // (2 * n)) & (a // n % 2 == 0) & (b // n % 2 == 1)).astype(np.float32)
    same = (a // RH == b // RH).astype(np.float32)
    c["chunk_masks"] = np.stack([np.eye(P, dtype=np.float32), same, -same, level(1)] + [level(n) for n in LEVELS], axis=1)
    own = (a // TD == b // TD) & (a < SB) & (b < SB)
    see = [np.concatenate([(a < b) & m, (a <= b) & m] * 2, axis=1) for m in (np.ones((P, P), bool), own)]
    c["see_masks"] = np.stack(see, axis=1).astype(np.int32)
    tok = np.arange(TOK)
    c["segments"] = np.where(tok < SEQ, tok % P != 0, tok % TD != 0).astype(np.float32)
    c["pick"] = ((i[:, None] % SB) // TD == np.arange(BD)[None, :]).astype(np.float32)
    return c


class Shared:
    pass


def free_semaphores(nc, since):
    nc.clear_and_free_semaphores(nc.allocated_since(since))
    nc.all_engine_barrier()


def build(nc, I, O):
    M = Shared()
    M.n_phys = I["cache_kv"].shape[0]
    M.v_dram = nc.dram_tensor("v_scratch", [SEQ, MW], F32, kind="Internal").ap()
    M.qk_dram = nc.dram_tensor("qk_scratch", [2, H, QK, SEQ], F32, kind="Internal").ap()
    M.oa_dram, M.ob_dram = (nc.dram_tensor(n + "_scratch", [P, KT, TOK], F32, kind="Internal").ap() for n in ("oa", "ob"))
    early = nc.snapshot_sems()
    with ExitStack() as whole:
        def hold(stack, name, shape):
            return stack.enter_context(nc.sbuf_tensor(name, shape, F32))

        M.ident = hold(whole, "ident_sb", [P, P])
        M.ones = hold(whole, "ones_sb", [P, P])
        M.hT = hold(whole, "hT", [P, KT, TOK])
        M.gate = hold(whole, "gate", [1 + BD, D])
        with ExitStack() as att:
            M.oaT = hold(att, "oaT", [P, KT, TOK])
            M.cnew, M.cnewT = hold(att, "cnew", [SB, KL + 1]), hold(att, "cnewT", [P, 2, P])
            M.kpenew, M.kpenewT = hold(att, "kpenew", [SB, ROPE]), hold(att, "kpenewT", [ROPE, P])
            M.kinvnew = hold(att, "kinvnew", [SB, H])
            M.zas = hold(att, "zas", [P, NP, SB])
            M.qg, M.qpe = hold(att, "qg", [SB, H, NOPE]), hold(att, "qpe", [SB, H, ROPE])
            with ExitStack() as first:
                M.G1, M.SH = hold(first, "G1", [P, 2, D]), hold(first, "SH", [P, 2, D])
                adaln(nc, I, M)
                front(nc, I, O, M)
            prompt(nc, I, M)
            M.qlT, M.qpT = hold(att, "qlT", [P, 2, BD, H, TD]), hold(att, "qpT", [ROPE, BD, H, TD])
            absorb(nc, I, M)
            sample(nc, I, M)
        with ExitStack() as rw:
            M.masks, M.seg, M.pick = hold(rw, "masks", [P, 4 + len(LEVELS), P]), hold(rw, "seg", [P, TOK]), hold(rw, "pick", [P, BD])
            M.see = rw.enter_context(nc.sbuf_tensor("see", [P, 2, 512], I32))
            M.vec, M.nvec, M.ss = hold(rw, "vec", [P, NVEC]), hold(rw, "nvec", [P, V_KK - V_W0]), hold(rw, "ssT", [P, 25, BD])
            M.shc, M.la, M.mhalf = hold(rw, "shc", [P, 25, 1 + BD]), hold(rw, "la", [P, TOK]), hold(rw, "mhalf", [P, 1])
            free_semaphores(nc, early)
            M.masks_in = nc.alloc_semaphore("masks_in")
            lora(nc, I, O, M)
            rwkv(nc, I, O, M)
            store_shift(nc, O, M)
        free_semaphores(nc, early)
        merge(nc, I, O, M)


_INS = ["x_prompt", "x_sample", "c_prompt", "c_sample", "cache_kv", "cache_kpe", "cache_kinv", "state_wkv", "state_shift",
        "page_table", "w_ada", "b_ada", "g_norm", "w_in", "g_qa", "w_uq", "g_kva", "w_uk", "w_uv", "g_q", "g_k", "w_pa",
        "mu_shift", "w0", "w_decay2", "a0", "w_a2", "k_k", "k_a", "r_k", "gn_g", "gn_b", "w_pb", "w_out"]
_OUTS = {"y_p": (1, SEQ, D), "y_s": (BD, TD, D), "kv_p": (1, SEQ, KL), "kpe_p": (1, SEQ, ROPE), "kinv_p": (1, SEQ, H),
         "wkv_p": (1, H, RH, RH), "shift_p": (1, NSH), "kv_s": (BD, TD, KL), "kpe_s": (BD, TD, ROPE), "kinv_s": (BD, TD, H),
         "wkv_s": (BD, H, RH, RH), "shift_s": (BD, NSH)}


def kernel(**inputs):
    import concourse.bacc as bacc
    from concourse.bass_utils import run_bass_kernel_spmd

    nc = bacc.Bacc("TRN2", target_bir_lowering=False, num_devices=1)
    arrays = {f"in_{name}": np.ascontiguousarray(inputs[name]) for name in _INS}
    arrays.update({f"in_{name}": a for name, a in constants().items()})
    I = {name[3:]: nc.dram_tensor(name, a.shape, mybir.dt.from_np(a.dtype), kind="ExternalInput").ap() for name, a in arrays.items()}
    O = {name: nc.dram_tensor(f"out_{name}", shape, F32, kind="ExternalOutput").ap() for name, shape in _OUTS.items()}
    build(nc, I, O)
    r = run_bass_kernel_spmd(nc, [arrays], core_ids=[0])
    return tuple(r.results[0][f"out_{name}"] for name in _OUTS)
```

```python
import numpy as np
import concourse.bass as bass
from concourse import mybir
from contextlib import ExitStack

F32 = mybir.dt.float32
I32 = mybir.dt.int32
ALU = mybir.AluOpType
ACT = mybir.ActivationFunctionType
AX = mybir.AxisListType

P = 128
D = 1024
KT = D // P
SEQ = 512
PB = SEQ // P
NB = PB + 1
TOK = NB * P
BD = 8
TD = 8
SB = BD * TD
H = 16
NP = H // 2
NOPE, ROPE, QK = 64, 32, 96
VD = 64
QL, KL = 384, 256
MW = H * VD
RH = 64
NSH = 3 * 1024 + 64 + 64
PAGES = 32
PS = 128
SCALE = QK ** -0.5
EPS = 1e-6
GN_EPS = 64e-5
HALF = ROPE // 2
C_QA, C_KVA, C_KPE = 0, QL, QL + KL
C_ZA = QL + KL + ROPE
C_SH = C_ZA + MW
C_ZB = C_SH + NSH
C_GA = C_ZB + 1024
C_GB = C_GA + D
LAT = C_ZA
S_R, S_WL, S_K, S_V, S_AL = 0, 1024, 1088, 2112, 3136
NEG = -1e30
LD = -float(np.exp(-0.5))


def bc(ap, n, at):
    return ap.unsqueeze(at).to_broadcast(list(ap.shape[:at]) + [n] + list(ap.shape[at:]))


def adaln(nc, I, M):
    with ExitStack() as ctx:
        sb = lambda name, shape: ctx.enter_context(nc.sbuf_tensor("ad_" + name, shape, F32))
        ps = lambda name: ctx.enter_context(nc.psum_tensor("ad_" + name, [P, 512], F32))
        sem = lambda name: nc.alloc_semaphore(name)
        R = 1 + BD
        NT = 3 * D // 512
        crow, esil, cT = sb("crow", [R, D]), sb("esil", [R, D]), sb("cT", [P, KT, R])
        bada, gnorm, mod = sb("bada", [R, 3 * D]), sb("gnorm", [R, D]), sb("mod", [R, 3 * D])
        sel = sb("sel_ada", [R, 2 * P])
        wada = [sb(f"wada{i}", [P, KT, 512]) for i in range(2)]
        psC, psM = ps("psC"), [ps("psM0"), ps("psM1")]
        psS = [ps(f"psS{i}") for i in range(4)]
        small_in, c_exp, c_silu, c_tr, c_sb = sem("small_in"), sem("c_exp"), sem("c_silu"), sem("c_tr"), sem("c_sb")
        w_in_sb = [sem("wada_in0"), sem("wada_in1")]
        mm, ev, rows, spread, spread_sb = sem("mod_mm"), sem("mod_ev"), sem("mod_rows"), sem("spread"), sem("spread_sb")
        w_v = I["w_ada"].rearrange("(k p) n -> p k n", p=P)
        block = ctx.enter_context(nc.Block())

        @block.sync
        def _(sp):
            for counted in (ev,):
                sp.sem_inc(counted, 1)
            sp.dma_start(crow[0:1, :], I["c_prompt"]).then_inc(small_in, 16)
            sp.dma_start(crow[1:R, :], I["c_sample"]).then_inc(small_in, 16)
            sp.dma_start(bada[:, :], bc(I["b_ada"], R, 0)).then_inc(small_in, 16)
            sp.dma_start(gnorm[:, :], bc(I["g_norm"], R, 0)).then_inc(small_in, 16)
            sp.dma_start(sel[:, :], I["sel"]).then_inc(small_in, 16)
            sp.dma_start(M.ident[:, :], I["ident"]).then_inc(small_in, 16)
            for b in range(2):
                sp.dma_start(wada[b][:, :, :], w_v[:, :, b * 512:(b + 1) * 512]).then_inc(w_in_sb[b], 16)
            with sp.Fori(1, NT // 2) as i:
                for b in range(2):
                    sp.wait_ge(mm, 2 * i + b - 1)
                    sp.dma_start(wada[b][:, :, :], w_v[:, :, bass.ds(i * 1024 + b * 512, 512)]).then_inc(w_in_sb[b], 16)

        @block.gpsimd
        def _(pool):
            nc.gpsimd.memset(M.ones[:, :], 1.0)

        @block.scalar
        def _(act):
            act.wait_ge(small_in, 96)
            nc.scalar.activation(esil[:, :], crow[:, :], ACT.Exp, scale=-1.0).then_inc(c_exp, 1)
            for i in range(4):
                act.wait_ge(spread, 2 * (i + 1))
                dst = (M.G1, M.SH)[i % 2]
                nc.scalar.copy(dst[:, i // 2, 0:512], psS[2 * (i % 2)][:, :])
                nc.scalar.copy(dst[:, i // 2, 512:D], psS[2 * (i % 2) + 1][:, :]).then_inc(spread_sb, 1)

        @block.tensor
        def _(pe):
            pe.wait_ge(c_silu, 1)
            for k in range(KT):
                last = nc.tensor.transpose(psC[:, k * R:(k + 1) * R], crow[:, k * P:(k + 1) * P], M.ident[0:R, 0:R])
            last.then_inc(c_tr, 1)
            pe.wait_ge(c_sb, 1)
            with pe.Fori(0, NT // 2) as i:
                for b in range(2):
                    pe.wait_ge(w_in_sb[b], i * 16 + 16)
                    pe.wait_ge(ev, 1 + 2 * i)
                    for k in range(KT):
                        last = nc.tensor.matmul(psM[b][0:R, :], cT[:, k, :], wada[b][:, k, :], start=(k == 0), stop=(k == KT - 1))
                    last.then_inc(mm, 1)
            pe.wait_ge(rows, 1)
            for i in range(4):
                if i >= 2:
                    pe.wait_ge(spread_sb, i - 1)
                src = mod[:, D:2 * D] if i % 2 == 0 else mod[:, 0:D]
                for n in range(2):
                    nc.tensor.matmul(psS[2 * (i % 2) + n][:, :], sel[:, (i // 2) * P:(i // 2 + 1) * P],
                                     src[:, n * 512:(n + 1) * 512], start=True, stop=True).then_inc(spread, 1)

        @block.vector
        def _(dve):
            dve.wait_ge(c_exp, 1)
            nc.vector.tensor_scalar(esil[:, :], esil[:, :], 1.0, None, ALU.add)
            dve.drain()
            nc.vector.reciprocal(esil[:, :], esil[:, :])
            dve.drain()
            nc.vector.tensor_tensor(crow[:, :], crow[:, :], esil[:, :], ALU.mult).then_inc(c_silu, 1)
            dve.wait_ge(c_tr, 1)
            nc.vector.tensor_copy(cT[:, :, :], psC[:, 0:KT * R].rearrange("p (k r) -> p k r", r=R)).then_inc(c_sb, 1)
            with dve.Fori(0, NT // 2) as i:
                for b in range(2):
                    dve.wait_ge(mm, 2 * i + b + 1)
                    cols = bass.ds(i * 1024 + b * 512, 512)
                    nc.vector.tensor_tensor(mod[:, cols], psM[b][0:R, :], bada[:, cols], ALU.add).then_inc(ev, 1)
            dve.drain()
            nc.vector.tensor_copy(M.gate[:, :], mod[:, 2 * D:3 * D])
            nc.vector.scalar_tensor_tensor(mod[:, D:2 * D], mod[:, D:2 * D], 1.0, gnorm[:, :], ALU.add, ALU.mult).then_inc(rows, 1)


def front(nc, I, O, M):
    with ExitStack() as ctx:
        sb = lambda name, shape: ctx.enter_context(nc.sbuf_tensor("fr_" + name, shape, F32))
        ps = lambda name: ctx.enter_context(nc.psum_tensor("fr_" + name, [P, 512], F32))
        sem = lambda name: nc.alloc_semaphore(name)
        wl = sb("w_lat", [P, KT, LAT])
        wuq, wuk, wuv = sb("wuq", [P, 3, H * QK]), sb("wuk", [P, 2, MW]), sb("wuv", [P, 2, MW])
        gqa, gkva, gq, gk = sb("gqa", [P, QL]), sb("gkva", [P, KL]), sb("gq", [P, QK]), sb("gk", [P, QK])
        cos, sin = sb("cos", [P, NB, 2, HALF]), sb("sin", [P, NB, 2, HALF])
        xb, hb, hcur = sb("xb", [P, D]), sb("hb", [P, D]), sb("hcur", [P, KT, P])
        sqj, sqa = sb("sqj", [P, H * QK]), sb("sqa", [P, D])
        sx = sb("sx", [P, 3])
        lat, qan, clat, qcT = sb("lat", [P, LAT]), sb("qan", [P, QL]), sb("clat", [P, KL]), sb("qcT", [P, 5, P])
        st, st2 = sb("st", [P, 4]), sb("st2", [P, 2, H])
        q, kn = sb("q", [P, H, QK]), sb("kn", [P, H, NOPE])
        ra, rb = sb("ra", [P, H, ROPE]), sb("rb", [P, H, ROPE])
        kp, kpr, kpa, kpb = sb("kp", [P, ROPE]), sb("kpr", [P, ROPE]), sb("kpa", [P, ROPE]), sb("kpb", [P, ROPE])
        kinv, keys = sb("kinv", [P, H]), sb("keys", [P, H, QK])
        headsT, vs = sb("headsT", [QK, 8, 4, P]), sb("vs", [P, MW])
        psA = [ps(f"bankA{i}") for i in range(4)]
        psQ = [ps(f"bankQ{i}") for i in range(4)]
        names = ("vec_in", "x_in", "ssq", "ms", "rt", "h_done", "h_tr", "h_sb", "lat_mm", "lat_sb", "lat_ssq", "lat_ms",
                 "lat_rt", "lat_n", "lat_tr", "lat_T", "q_mm", "q_sb", "kn_mm", "kn_sb", "v_mm", "v_sb", "nrm", "nrm_rt",
                 "q_done", "k_done", "out_ready", "out_done", "tr_q", "tr_sb", "w_lat_in", "w_up_in", "hT_sb", "ones_", "sp_past", "spilled")
        s = {n: sem("f_" + n) for n in names}
        block = ctx.enter_context(nc.Block())

        @block.sync
        def _(sp):
            for counted in (s["kn_sb"], s["hT_sb"], s["spilled"], s["v_sb"], s["tr_sb"], s["out_done"],):
                sp.sem_inc(counted, 1)
            for dst, src in ((gqa, "g_qa"), (gkva, "g_kva"), (gq, "g_q"), (gk, "g_k")):
                sp.dma_start(dst[:, :], bc(I[src], P, 0)).then_inc(s["vec_in"], 16)
            sp.dma_start(cos[:, :, :, :], I["cos"]).then_inc(s["vec_in"], 16)
            sp.dma_start(sin[:, :, :, :], I["sin"]).then_inc(s["vec_in"], 16)
            sp.dma_start(xb[:, :], I["x_prompt"][0, 0:P, :]).then_inc(s["x_in"], 16)
            sp.dma_start(wl[:, :, :], I["w_in"].rearrange("(k p) n -> p k n", p=P)[:, :, 0:LAT]).then_inc(s["w_lat_in"], 16)
            sp.dma_start(wuq[:, :, :], I["w_uq"].rearrange("(k p) h d -> p k (h d)", p=P)).then_inc(s["w_up_in"], 16)
            sp.dma_start(wuk[:, :, :], I["w_uk"].rearrange("(k p) h d -> p k (h d)", p=P)).then_inc(s["w_up_in"], 16)
            sp.dma_start(wuv[:, :, :], I["w_uv"].rearrange("(k p) h d -> p k (h d)", p=P)).then_inc(s["w_up_in"], 16)

            def outputs(t, rows, kv, kpe, ki):
                sp.wait_ge(s["out_ready"], t + 1)
                sp.dma_start(kv, clat[0:rows, :]).then_inc(s["out_done"], 16)
                sp.dma_start(kpe, kpr[0:rows, :]).then_inc(s["out_done"], 16)
                sp.dma_start(ki, kinv[0:rows, :]).then_inc(s["out_done"], 16)

            def spill(t, tok):
                sp.wait_ge(s["v_sb"], 1 + t + 1)
                sp.dma_start(M.v_dram[tok, :], vs[:, :]).then_inc(s["spilled"], 16)
                for n in range(8):
                    sp.wait_ge(s["tr_sb"], 1 + t * 8 + n + 1)
                    sp.sem_inc(s["sp_past"], 1)
                    h = 4 * (n % 4)
                    dst = M.qk_dram[n // 4, h:h + 4, :, tok]
                    sp.dma_start(dst.rearrange("h d t -> d h t"), headsT[:, n, :, :]).then_inc(s["spilled"], 16)

            with sp.Fori(0, PB - 1) as t:
                sp.wait_ge(s["h_done"], t + 1)
                sp.dma_start(xb[:, :], I["x_prompt"][0, bass.ds(t * P + P, P), :]).then_inc(s["x_in"], 16)
                tok = bass.ds(t * P, P)
                outputs(t, P, O["kv_p"][0, tok, :], O["kpe_p"][0, tok, :], O["kinv_p"][0, tok, :])
                spill(t, tok)
            sp.wait_ge(s["h_done"], PB)
            sp.dma_start(xb[0:SB, :], I["x_sample"].rearrange("b t d -> (b t) d")).then_inc(s["x_in"], 16)
            tok = slice(SEQ - P, SEQ)
            outputs(PB - 1, P, O["kv_p"][0, tok, :], O["kpe_p"][0, tok, :], O["kinv_p"][0, tok, :])
            spill(PB - 1, tok)
            outputs(PB, SB, O["kv_s"].rearrange("b t d -> (b t) d"), O["kpe_s"].rearrange("b t d -> (b t) d"),
                    O["kinv_s"].rearrange("b t d -> (b t) d"))
            sp.wait_ge(s["out_done"], 1 + 48 * NB)
            sp.wait_ge(s["spilled"], 1 + 144 * PB)

        @block.scalar
        def _(act):
            act.wait_ge(s["vec_in"], 96)

            def norm_x(t, sample):
                act.wait_ge(s["x_in"], 16 * (t + 1))
                nc.scalar.activation(sqa[:, 0:D], xb[:, :], ACT.Square, accum_out=sx[:, 0:1]).then_inc(s["ssq"], 1)
                act.wait_ge(s["ms"], t + 1)
                nc.scalar.activation(sx[:, 1:2], sx[:, 0:1], ACT.Sqrt).then_inc(s["rt"], 1)

            def latents(t, sample):
                act.wait_ge(s["h_tr"], t + 1)
                act.wait_ge(s["hT_sb"], 1 + t)
                for n in range(2):
                    last = nc.scalar.copy(hcur[:, 4 * n:4 * n + 4, :], psA[n][:, :].rearrange("p (k t) -> p k t", t=P))
                last.then_inc(s["h_sb"], 1)
                act.wait_ge(s["lat_mm"], t + 1)
                nc.scalar.copy(lat[:, 0:512], psA[2][:, :])
                nc.scalar.copy(lat[:, 512:LAT], psA[3][:, 0:LAT - 512]).then_inc(s["lat_sb"], 1)
                act.drain()
                nc.scalar.activation(sqa[:, 0:QL], lat[:, 0:QL], ACT.Square, scale=QL ** -0.5, accum_out=st[:, 0:1])
                nc.scalar.activation(sqa[:, 512:512 + KL], lat[:, QL:QL + KL], ACT.Square, scale=KL ** -0.5, accum_out=st[:, 1:2])
                nc.scalar.activation(sqa[:, 768:768 + ROPE], lat[:, QL + KL:LAT], ACT.Square, accum_out=st[:, 2:3]).then_inc(s["lat_ssq"], 1)

            def products(t, sample):
                act.wait_ge(s["lat_ms"], t + 1)
                nc.scalar.activation(st[:, 0:2], st[:, 0:2], ACT.Sqrt).then_inc(s["lat_rt"], 1)
                act.wait_ge(s["lat_tr"], t + 1)
                nc.scalar.copy(qcT[:, 0:4, :], psA[0][:, :].rearrange("p (k t) -> p k t", t=P))
                nc.scalar.copy(qcT[:, 4, :], psA[1][:, 0:P]).then_inc(s["lat_T"], 1)

            def norms(t, sample):
                act.wait_ge(s["q_mm"], t + 1)
                qf = q[:, :, :].rearrange("p h d -> p (h d)")
                for n in range(3):
                    last = nc.scalar.copy(qf[:, n * 512:(n + 1) * 512], psQ[n][:, :])
                last.then_inc(s["q_sb"], 1)
                act.wait_ge(s["kn_mm"], t + 1)
                kf = kn[:, :, :].rearrange("p h d -> p (h d)")
                for n in range(2):
                    last = nc.scalar.copy(kf[:, n * 512:(n + 1) * 512], psA[2 + n][:, :])
                last.then_inc(s["kn_sb"], 1)
                if not sample:
                    act.wait_ge(s["v_mm"], t + 1)
                    act.wait_ge(s["spilled"], 1 + 144 * t)
                    for n in range(2):
                        last = nc.scalar.copy(vs[:, n * 512:(n + 1) * 512], psA[n][:, :])
                    last.then_inc(s["v_sb"], 1)
                act.wait_ge(s["nrm"], t + 1)
                nc.scalar.activation(st2[:, :, :], st2[:, :, :], ACT.Sqrt).then_inc(s["nrm_rt"], 1)

            def heads(t, sample):
                if not sample:
                    for n in range(8):
                        act.wait_ge(s["tr_q"], t * 8 + n + 1)
                        nc.scalar.copy(headsT[:, n, :, :], psQ[n % 4][0:QK, :].rearrange("p (h t) -> p h t", t=P)).then_inc(s["tr_sb"], 1)

            _front_blocks(act, norm_x, latents, products, norms, heads)

        @block.tensor
        def _(pe):
            def latents(t, sample):
                pe.wait_ge(s["h_done"], t + 1)
                pe.wait_ge(s["v_sb"], 1 + t)
                for k in range(KT):
                    last = nc.tensor.transpose(psA[k // 4][:, (k % 4) * P:(k % 4 + 1) * P], hb[:, k * P:(k + 1) * P], M.ident[:, :])
                last.then_inc(s["h_tr"], 1)
                pe.wait_ge(s["h_sb"], t + 1)
                pe.wait_ge(s["w_lat_in"], 16)
                pe.wait_ge(s["kn_sb"], 1 + t)
                for n, (a, b) in enumerate(((0, 512), (512, LAT))):
                    for k in range(KT):
                        last = nc.tensor.matmul(psA[2 + n][:, 0:b - a], hcur[:, k, :], wl[:, k, a:b], start=(k == 0), stop=(k == KT - 1))
                last.then_inc(s["lat_mm"], 1)

            def products(t, sample):
                pe.wait_ge(s["lat_n"], t + 1)
                for k in range(3):
                    nc.tensor.transpose(psA[0][:, k * P:(k + 1) * P], qan[:, k * P:(k + 1) * P], M.ident[:, :])
                nc.tensor.transpose(psA[0][:, 3 * P:4 * P], clat[:, 0:P], M.ident[:, :])
                nc.tensor.transpose(psA[1][:, 0:P], clat[:, P:2 * P], M.ident[:, :]).then_inc(s["lat_tr"], 1)
                pe.wait_ge(s["lat_T"], t + 1)
                pe.wait_ge(s["w_up_in"], 48)
                pe.wait_ge(s["tr_sb"], 1 + t * 8)
                for n in range(3):
                    for k in range(3):
                        last = nc.tensor.matmul(psQ[n][:, :], qcT[:, k, :], wuq[:, k, n * 512:(n + 1) * 512], start=(k == 0), stop=(k == 2))
                last.then_inc(s["q_mm"], 1)
                for n in range(2):
                    for k in range(2):
                        last = nc.tensor.matmul(psA[2 + n][:, :], qcT[:, 3 + k, :], wuk[:, k, n * 512:(n + 1) * 512], start=(k == 0), stop=(k == 1))
                last.then_inc(s["kn_mm"], 1)
                if not sample:
                    for n in range(2):
                        for k in range(2):
                            last = nc.tensor.matmul(psA[n][:, :], qcT[:, 3 + k, :], wuv[:, k, n * 512:(n + 1) * 512], start=(k == 0), stop=(k == 1))
                    last.then_inc(s["v_mm"], 1)

            def heads(t, sample):
                if not sample:
                    for n in range(8):
                        src, ready = (q, s["q_done"]) if n < 4 else (keys, s["k_done"])
                        if n in (0, 4):
                            pe.wait_ge(ready, t + 1)
                        if n == 0:
                            pe.wait_ge(s["q_sb"], t + 1)
                        if n >= 4:
                            pe.wait_ge(s["tr_sb"], 1 + t * 8 + n - 3)
                        for h in range(4):
                            last = nc.tensor.transpose(psQ[n % 4][0:QK, h * P:(h + 1) * P], src[:, 4 * (n % 4) + h, :], M.ident[:, :])
                        last.then_inc(s["tr_q"], 1)

            _front_blocks(pe, None, latents, products, None, heads)

        @block.gpsimd
        def _(pool):
            def body(t, sample):
                pool.wait_ge(s["h_sb"], t + 1)
                nc.gpsimd.tensor_copy(M.hT[:, :, bass.ds(t * P, P)], hcur[:, :, :]).then_inc(s["hT_sb"], 1)
                if sample:
                    pool.wait_ge(s["lat_T"], t + 1)
                    nc.gpsimd.tensor_copy(M.cnewT[:, :, :], qcT[:, 3:5, :])
                    nc.gpsimd.tensor_copy(M.cnew[:, 0:KL], clat[0:SB, :])
                    nc.gpsimd.memset(M.cnew[:, KL:KL + 1], 1.0).then_inc(s["ones_"], 1)

            _prompt_blocks(pool, body)

        @block.vector
        def _(dve):
            v = nc.vector
            dve.wait_ge(s["vec_in"], 96)

            def rope(out, src, a, b, t, heads):
                table = lambda w: w[:, t, :, :].rearrange("p a c -> p (a c)")
                c_, s_ = table(cos), table(sin)
                if heads:
                    c_, s_ = bc(c_, H, 1), bc(s_, H, 1)
                v.tensor_tensor(a, src, c_, ALU.mult)
                v.tensor_tensor(b, src, s_, ALU.mult)
                dve.drain()
                v.tensor_tensor(out[..., 0:HALF], a[..., 0:HALF], b[..., HALF:ROPE], ALU.subtract)
                return v.tensor_tensor(out[..., HALF:ROPE], b[..., 0:HALF], a[..., HALF:ROPE], ALU.add)

            def norm_x(t, sample):
                dve.wait_ge(s["ssq"], t + 1)
                v.tensor_scalar(sx[:, 0:1], sx[:, 0:1], 1.0 / D, EPS, ALU.mult, ALU.add).then_inc(s["ms"], 1)
                dve.wait_ge(s["rt"], t + 1)
                v.reciprocal(sx[:, 2:3], sx[:, 1:2])
                dve.drain()
                m = 1 if sample else 0
                v.scalar_tensor_tensor(hb[:, :], xb[:, :], sx[:, 2:3], M.G1[:, m, :], ALU.mult, ALU.mult)
                dve.drain()
                v.tensor_tensor(hb[:, :], hb[:, :], M.SH[:, m, :], ALU.add).then_inc(s["h_done"], 1)

            def products(t, sample):
                dve.wait_ge(s["lat_ssq"], t + 1)
                v.tensor_scalar(st[:, 0:2], st[:, 0:2], EPS, None, ALU.add)
                dve.drain()
                v.tensor_copy(st[:, 3:4], st[:, 2:3]).then_inc(s["lat_ms"], 1)
                dve.wait_ge(s["lat_rt"], t + 1)
                v.reciprocal(st[:, 0:2], st[:, 0:2])
                dve.drain()
                dve.wait_ge(s["out_done"], 1 + t * 48)
                v.scalar_tensor_tensor(qan[:, :], lat[:, 0:QL], st[:, 0:1], gqa[:, :], ALU.mult, ALU.mult)
                v.scalar_tensor_tensor(clat[:, :], lat[:, QL:QL + KL], st[:, 1:2], gkva[:, :], ALU.mult, ALU.mult).then_inc(s["lat_n"], 1)
                v.tensor_tensor(kp[:, :], lat[:, QL + KL:LAT], gk[:, NOPE:QK], ALU.mult)
                dve.drain()
                rope(kpr[:, :], kp[:, :], kpa[:, :], kpb[:, :], t, False)

            def norms(t, sample):
                dve.wait_ge(s["q_sb"], t + 1)
                sq = sqj[:, :].rearrange("p (h d) -> p h d", d=QK)
                v.tensor_tensor(sq, q[:, :, :], q[:, :, :], ALU.mult)
                dve.drain()
                v.tensor_reduce(st2[:, 0, :], sq, AX.X, ALU.add)
                dve.drain()
                dve.wait_ge(s["kn_sb"], 1 + t + 1)
                sk = sqj[:, 0:MW].rearrange("p (h d) -> p h d", d=NOPE)
                v.tensor_tensor(sk, kn[:, :, :], kn[:, :, :], ALU.mult)
                dve.drain()
                v.tensor_reduce(st2[:, 1, :], sk, AX.X, ALU.add)
                dve.drain()
                v.tensor_scalar(st2[:, 1, :], st2[:, 1, :], st[:, 3:4], None, ALU.add)
                dve.drain()
                v.tensor_scalar(st2[:, :, :], st2[:, :, :], 1.0 / QK, EPS, ALU.mult, ALU.add).then_inc(s["nrm"], 1)
                dve.wait_ge(s["nrm_rt"], t + 1)
                v.reciprocal(st2[:, :, :], st2[:, :, :])
                dve.drain()
                v.tensor_copy(kinv[:, :], st2[:, 1, :]).then_inc(s["out_ready"], 1)
                v.tensor_tensor(q[:, :, :], q[:, :, :], bc(st2[:, 0, :], QK, 2), ALU.mult)
                dve.drain()
                v.tensor_tensor(q[:, :, :], q[:, :, :], bc(gq[:, :], H, 1), ALU.mult)
                dve.drain()
                rope(q[:, :, NOPE:QK], q[:, :, NOPE:QK], ra[:, :, :], rb[:, :, :], t, True).then_inc(s["q_done"], 1)
                if not sample:
                    v.tensor_tensor(kn[:, :, :], kn[:, :, :], bc(gk[:, 0:NOPE], H, 1), ALU.mult)
                    dve.drain()
                    v.tensor_tensor(keys[:, :, 0:NOPE], kn[:, :, :], bc(kinv[:, :], NOPE, 2), ALU.mult)
                    v.tensor_tensor(keys[:, :, NOPE:QK], bc(kpr[:, :], H, 1), bc(kinv[:, :], ROPE, 2), ALU.mult).then_inc(s["k_done"], 1)
                else:
                    dve.drain()
                    v.tensor_tensor(M.qg[:, :, :], q[0:SB, :, 0:NOPE], bc(gk[0:SB, 0:NOPE], H, 1), ALU.mult)
                    v.tensor_copy(M.qpe[:, :, :], q[0:SB, :, NOPE:QK])
                    v.tensor_copy(M.kpenew[:, :], kpr[0:SB, :])
                    v.tensor_copy(M.kinvnew[:, :], kinv[0:SB, :])


            _front_blocks(dve, norm_x, None, products, norms, None)


def _prompt_blocks(engine, body):
    with engine.Fori(0, PB) as t:
        body(t, False)
    body(PB, True)


def _front_blocks(engine, norm_x, latents, products, norms, heads):
    part = lambda f, t: f(t, isinstance(t, int) and t == PB) if f else None

    def turn(t, following):
        part(products, t)
        if following is not None:
            part(norm_x, following)
        part(norms, t)
        if following is not None:
            part(latents, following)
        part(heads, t)

    part(norm_x, 0)
    part(latents, 0)
    with engine.Fori(0, PB - 1) as t:
        turn(t, t + 1)
    turn(PB - 1, PB)
    turn(PB, None)


def prompt(nc, I, M):
    with ExitStack() as ctx:
        sb = lambda name, shape: ctx.enter_context(nc.sbuf_tensor("pr_" + name, shape, F32))
        ps = lambda name: ctx.enter_context(nc.psum_tensor("pr_" + name, [P, 512], F32))
        sem = lambda name: nc.alloc_semaphore("p_" + name)
        wz = [sb(f"wz{i}", [P, KT, P]) for i in range(2)]
        tri = sb("tri", [P, P])
        qh = [sb(f"qh{i}", [QK, 2, SEQ]) for i in range(2)]
        kh = [sb(f"kh{i}", [QK, 2, SEQ]) for i in range(2)]
        vh = [sb(f"vh{i}", [P, PB, P]) for i in range(2)]
        pb, pT = sb("pb", [P, 2, SEQ]), sb("pT", [P, 2, SEQ])
        mx, nmx, rs, ri = sb("mx", [P, 8]), sb("nmx", [P, 8]), sb("rs", [P, 8]), sb("ri", [P, 8])
        ez, zs = sb("ez", [P, TOK]), sb("zs", [P, TOK])
        psS, psT = [ps(f"psS{i}") for i in range(3)], [ps("psT0"), ps("psT1")]
        psO, psZ0, psZ1 = ps("psO"), ps("psZ0"), ps("psZ1")
        tri_in, wz_in = sem("tri_in"), [sem("wz_in0"), sem("wz_in1")]
        heads_in = [sem("heads_in0"), sem("heads_in1")]
        scores, maxed, exped, normed, tr, tr_sb, pv, o_sb, z_mm, z_exp, z_sb = (
            sem(n) for n in ("scores", "maxed", "exped", "normed", "tr", "tr_sb", "pv", "o_sb", "z_mm", "z_exp", "z_sb"))
        w_v = I["w_in"].rearrange("(k p) n -> p k n", p=P)
        NU = 2 * PB
        ZU = 2
        block = ctx.enter_context(nc.Block())

        @block.sync
        def _(sp):
            for counted in (exped, o_sb, tr, z_sb,):
                sp.sem_inc(counted, 1)
            sp.dma_start(tri[:, :], I["tri"]).then_inc(tri_in, 16)

            def load(b, hp):
                for which, dst in ((0, qh[b]), (1, kh[b])):
                    src = M.qk_dram[which, bass.ds(2 * hp, 2), :, :]
                    sp.dma_start(dst[:, :, :], src.rearrange("h d t -> d h t")).then_inc(heads_in[b], 16)
                sp.dma_start(vh[b][:, :, :], M.v_dram[:, bass.ds(hp * P, P)].rearrange("(b t) n -> t b n", t=P)).then_inc(heads_in[b], 16)
                sp.dma_start(wz[b][:, :, :], w_v[:, :, bass.ds(C_ZA + hp * P, P)]).then_inc(wz_in[b], 16)

            for b in range(2):
                load(b, b)
            with sp.Fori(1, NP // 2) as i:
                for b in range(2):
                    sp.wait_ge(pv, NU * (2 * i + b - 1))
                    load(b, 2 * i + b)

        @block.tensor
        def _(pe):
            pe.wait_ge(tri_in, 16)

            def score(hp, hp_b, u):
                hh, qb = u // PB, u % PB
                pe.wait_ge(exped, 1 + NU * hp + (u - 2 if u >= 3 else 0))
                nk = (qb + 1) * P
                nc.tensor.matmul(psS[u % 3][:, 0:nk], qh[hp_b][:, hh, qb * P:nk], kh[hp_b][:, hh, 0:nk],
                                 start=True, stop=True).then_inc(scores, 1)

            def pair(i, b):
                hp = 2 * i + b
                pe.wait_ge(heads_in[b], i * 48 + 48)
                pe.wait_ge(wz_in[b], i * 16 + 16)
                pe.wait_ge(z_sb, 1 + hp)

                def transposes(u):
                    pe.wait_ge(normed, NU * hp + u + 1)
                    for kb in range(u % PB + 1):
                        last = nc.tensor.transpose(psT[u % 2][:, kb * P:(kb + 1) * P], pb[:, u % 2, kb * P:(kb + 1) * P], M.ident[:, :])
                    last.then_inc(tr, 1)

                for u in range(3):
                    score(hp, b, u)
                transposes(0)
                for u in range(NU):
                    if u + 3 < NU:
                        score(hp, b, u + 3)
                    for k in range(KT * u // ZU, KT * (u + 1) // ZU if u < ZU else 0):
                        nc.tensor.matmul(psZ0[:, :], wz[b][:, k, :], M.hT[:, k, 0:SEQ], start=(k == 0), stop=(k == KT - 1))
                        last = nc.tensor.matmul(psZ1[:, 0:P], wz[b][:, k, :], M.hT[:, k, SEQ:TOK], start=(k == 0), stop=(k == KT - 1))
                        if k == KT - 1:
                            last.then_inc(z_mm, 1)
                    if u + 1 < NU:
                        transposes(u + 1)
                    if u == 0:
                        pe.wait_ge(o_sb, 1 + hp)
                    hh, qb = u // PB, u % PB
                    pe.wait_ge(tr_sb, NU * hp + u + 1)
                    for kb in range(qb + 1):
                        last = nc.tensor.matmul(psO[hh * VD:(hh + 1) * VD, qb * P:(qb + 1) * P], vh[b][:, kb, hh * VD:(hh + 1) * VD],
                                                pT[:, u % 2, kb * P:(kb + 1) * P], start=(kb == 0), stop=(kb == qb))
                    last.then_inc(pv, 1)

            with pe.Fori(0, NP // 2) as i:
                for b in range(2):
                    pair(i, b)

        @block.vector
        def _(dve):
            v = nc.vector
            dve.wait_ge(tri_in, 16)

            def pair(hp, b):
                def top(u):
                    qb = u % PB
                    nk = (qb + 1) * P
                    dve.wait_ge(scores, NU * hp + u + 1)
                    v.tensor_tensor(psS[u % 3][:, qb * P:nk], psS[u % 3][:, qb * P:nk], tri[:, :], ALU.add)
                    dve.drain()
                    v.tensor_reduce(mx[:, u:u + 1], psS[u % 3][:, 0:nk], AX.X, ALU.max)
                    dve.drain()
                    v.tensor_scalar(nmx[:, u:u + 1], mx[:, u:u + 1], -SCALE, None, ALU.mult).then_inc(maxed, 1)

                top(0)
                for u in range(NU):
                    if u + 1 < NU:
                        top(u + 1)
                    nk = (u % PB + 1) * P
                    dve.wait_ge(exped, 1 + NU * hp + u + 1)
                    v.reciprocal(ri[:, u:u + 1], rs[:, u:u + 1])
                    dve.drain()
                    v.tensor_scalar(pb[:, u % 2, 0:nk], pb[:, u % 2, 0:nk], ri[:, u:u + 1], None, ALU.mult).then_inc(normed, 1)
                    if u >= NU - NB:
                        c = u - (NU - NB)
                        if c == 0:
                            dve.wait_ge(z_exp, hp + 1)
                        part = ez[:, c * P:(c + 1) * P]
                        v.tensor_scalar(part, part, 1.0, None, ALU.add)
                        dve.drain()
                        v.reciprocal(part, part)
                dve.drain()
                dve.wait_ge(z_sb, 1 + hp + 1)
                v.tensor_tensor(zs[:, :], zs[:, :], ez[:, :], ALU.mult)
                dve.drain()
                dve.wait_ge(pv, NU * (hp + 1))
                v.tensor_copy(M.zas[:, hp, :], zs[:, SEQ:SEQ + SB])
                v.tensor_tensor(M.oaT[:, hp, 0:SEQ], psO[:, :], zs[:, 0:SEQ], ALU.mult).then_inc(o_sb, 1)

            with dve.Fori(0, NP // 2) as i:
                for b in range(2):
                    pair(2 * i + b, b)

        @block.scalar
        def _(act):
            def evac(hp, u):
                nk = (u % PB + 1) * P
                act.wait_ge(tr, 1 + NU * hp + u + 1)
                nc.scalar.copy(pT[:, u % 2, 0:nk], psT[u % 2][:, 0:nk]).then_inc(tr_sb, 1)

            with act.Fori(0, NP) as hp:
                for u in range(NU):
                    nk = (u % PB + 1) * P
                    act.wait_ge(maxed, NU * hp + u + 1)
                    act.wait_ge(tr, 1 + NU * hp + u - 1) if u >= 1 else act.wait_ge(tr, 1 + NU * hp)
                    nc.scalar.activation(pb[:, u % 2, 0:nk], psS[u % 3][:, 0:nk], ACT.Exp, bias=nmx[:, u:u + 1], scale=SCALE,
                                         accum_out=rs[:, u:u + 1]).then_inc(exped, 1)
                    if u >= 1:
                        evac(hp, u - 1)
                    if u == ZU:
                        act.wait_ge(z_mm, hp + 1)
                        act.wait_ge(o_sb, 1 + hp)
                        nc.scalar.activation(ez[:, 0:SEQ], psZ0[:, :], ACT.Exp, scale=-1.0)
                        nc.scalar.activation(ez[:, SEQ:TOK], psZ1[:, 0:P], ACT.Exp, scale=-1.0).then_inc(z_exp, 1)
                    if u == ZU + 2:
                        nc.scalar.copy(zs[:, 0:SEQ], psZ0[:, :])
                        nc.scalar.copy(zs[:, SEQ:TOK], psZ1[:, 0:P]).then_inc(z_sb, 1)
                evac(hp, NU - 1)


def absorb(nc, I, M):
    with ExitStack() as ctx:
        sb = lambda name, shape: ctx.enter_context(nc.sbuf_tensor("ab_" + name, shape, F32))
        ps = lambda name: ctx.enter_context(nc.psum_tensor("ab_" + name, [P, 512], F32))
        sem = lambda name: nc.alloc_semaphore("b_" + name)
        wuk, ukT, qgT = sb("wuk_b", [P, 2, MW]), sb("ukT", [P, NP, KL]), sb("qgT", [P, NP, SB])
        bk = [ps(f"bankB{i}") for i in range(6)]
        w_in_sb, tr, tr_sb, mm, ev = (sem(n) for n in ("w_in", "tr", "tr_sb", "mm", "ev"))
        block = ctx.enter_context(nc.Block())

        @block.sync
        def _(sp):
            sp.dma_start(wuk[:, :, :], I["w_uk"].rearrange("(k p) h d -> p k (h d)", p=P)).then_inc(w_in_sb, 16)
            sp.wait_ge(w_in_sb, 16)

        @block.tensor
        def _(pe):
            pe.wait_ge(w_in_sb, 16)
            for hp in range(NP):
                for k in range(2):
                    last = nc.tensor.transpose(bk[hp // 2][:, (hp % 2) * KL + k * P:(hp % 2) * KL + (k + 1) * P],
                                               wuk[:, k, hp * P:(hp + 1) * P], M.ident[:, :])
                nc.tensor.transpose(bk[4][:, hp * SB:(hp + 1) * SB],
                                    M.qg[:, :, :].rearrange("t h d -> t (h d)")[:, hp * P:(hp + 1) * P], M.ident[0:SB, 0:SB])
            nc.tensor.transpose(bk[5][0:ROPE, 8 * SB - SB:8 * SB], M.kpenew[:, :], M.ident[0:SB, 0:SB]).then_inc(tr, 1)
            pe.wait_ge(tr_sb, 1)
            for half in range(2):
                if half:
                    pe.wait_ge(ev, 3)
                for h in range(8):
                    last = nc.tensor.transpose(bk[5][0:ROPE, h * SB:(h + 1) * SB], M.qpe[:, 8 * half + h, :], M.ident[0:SB, 0:SB])
                last.then_inc(mm, 1)
                if half == 0:
                    for rt in range(2):
                        for h in range(H):
                            b = 64 * (h % 2)
                            last = nc.tensor.matmul(bk[2 * (h % 2) + rt][:, (h // 2) * SB:(h // 2 + 1) * SB], ukT[b:b + 64, h // 2, rt * P:(rt + 1) * P],
                                                    qgT[b:b + 64, h // 2, :], start=True, stop=True)
                        last.then_inc(mm, 1)

        @block.vector
        def _(dve):
            v = nc.vector
            dve.wait_ge(tr, 1)
            for n in range(4):
                v.tensor_copy(ukT[:, 2 * n:2 * n + 2, :], bk[n][:, :].rearrange("p (a r) -> p a r", r=KL))
            v.memset(M.kpenewT[:, SB:P], 0.0)
            v.tensor_copy(M.kpenewT[:, 0:SB], bk[5][0:ROPE, 7 * SB:8 * SB])
            v.tensor_copy(qgT[:, :, :], bk[4][:, :].rearrange("p (a t) -> p a t", t=SB)).then_inc(tr_sb, 1)

            def by_batch(dst, bank, heads):
                return v.tensor_copy(dst[:, :, heads, :], bank.rearrange("p (h b t) -> p b h t", h=8, t=TD))

            dve.wait_ge(mm, 1)
            by_batch(M.qpT, bk[5][0:ROPE, :], slice(0, 8)).then_inc(ev, 1)
            for rt in range(2):
                dve.wait_ge(mm, 2 + rt)
                by_batch(M.qlT[:, rt], bk[rt][:, :], slice(0, H, 2))
                by_batch(M.qlT[:, rt], bk[2 + rt][:, :], slice(1, H, 2)).then_inc(ev, 1)
            dve.wait_ge(mm, 4)
            by_batch(M.qpT, bk[5][0:ROPE, :], slice(8, H)).then_inc(ev, 1)


def sample(nc, I, M):
    with ExitStack() as ctx:
        sb = lambda name, shape: ctx.enter_context(nc.sbuf_tensor("sa_" + name, shape, F32))
        ps = lambda name: ctx.enter_context(nc.psum_tensor("sa_" + name, [P, 512], F32))
        sem = lambda name: nc.alloc_semaphore("s_" + name)
        G, GP = 8, 4
        ROW = H * TD
        C1 = KL + 1
        table = ctx.enter_context(nc.sbuf_tensor("table", [1, BD * PAGES], I32))
        pages = [sb(f"pages{i}", [P, PAGES, C1]) for i in range(2)]
        kpe, kinv = [sb(f"kpe{i}", [P, PAGES, ROPE]) for i in range(2)], [sb(f"kinvp{i}", [P, PAGES, H]) for i in range(2)]
        cT, kT = sb("cT_pages", [P, 2, 2, 512]), sb("kpeT_pages", [ROPE, 2, 512])
        STs = [sb(f"ST{i}", [P, PAGES + 1, ROW]) for i in range(2)]
        own = sb("own_mask", [SB, BD, ROW])
        top4, top1, topr, topb, topB = sb("top4", [P, 512]), sb("top1", [P, ROW]), sb("topr", [ROW, 1]), sb("topb", [ROW, P]), sb("topB", [P, ROW])
        ri, ol, olT = sb("ri_s", [ROW, 1]), sb("ol", [ROW, KL]), sb("olT", [P, 2, H, SB])
        wuv = cT[:, :, :, :].rearrange("p a r k -> p a (r k)")
        psA, psK, psS, psO, psM = [ps("psA0"), ps("psA1")], ps("psK"), [ps("psSs0"), ps("psSs1")], ps("psOs"), ps("psMs")
        table_in, fixed_in, wuv_in = sem("table_in"), sem("fixed_in"), sem("wuv_in")
        NC, CP = 4, PAGES // 4
        pages_in, keys_in = ([[sem(f"{n}_in{b}{c}") for c in range(NC)] for b in range(2)] for n in ("pages", "keys"))
        cT_tr, cT_sb, scored, weighted, topped, top_tr, top_row, top_bc, centred, exped, pv, o_sb, o_tr, o_T, up, ones, gated, stored, sp_past, pool_past = (
            sem(n) for n in ("cT_tr", "cT_sb", "scored", "weighted", "topped", "top_tr", "top_row", "top_bc",
                             "centred", "exped", "pv", "o_sb", "o_tr", "o_T", "up", "ones", "gated", "stored", "sp_past", "pool_past"))
        block = ctx.enter_context(nc.Block())

        def load_pages(e, what, landed, freed, past):
            def load(b, s, c):
                with e.Fori(c * CP, (c + 1) * CP) as j:
                    page = e.value_load(table[0:1, bass.ds(s * PAGES + j, 1)], min_val=0, max_val=M.n_phys - 1)
                    at = bass.ds(page, 1)
                    for dst, src, w in what:
                        e.dma_start(dst[b][:, bass.ds(j, 1), 0:w], I[src][at, :, :].rearrange("a p n -> p a n")).then_inc(landed[b][c], 16)

            for b in range(2):
                for c in range(NC):
                    load(b, b, c)
            with e.Fori(1, BD // 2) as i:
                for b in range(2):
                    for c in range(NC):
                        done, count = freed(2 * i + b - 2, c)
                        e.wait_ge(done, count)
                        e.sem_inc(past, 1)
                        load(b, 2 * i + b, c)

        @block.gpsimd
        def _(pool):
            pool.wait_ge(table_in, 16)
            load_pages(pool, ((kpe, "cache_kpe", ROPE), (kinv, "cache_kinv", H)), keys_in, lambda s, c: (weighted, 1 + G * s + 2 * c + 2), pool_past)

        @block.sync
        def _(sp):
            for counted in (cT_sb, weighted, o_sb, o_T, centred, scored,):
                sp.sem_inc(counted, 1)
            sp.dma_start(table[:, :], I["page_table"].rearrange("(a b) n -> a (b n)", a=1)).then_inc(table_in, 16)
            sp.dma_start(own[:, :, :], I["own_mask"]).then_inc(fixed_in, 16)
            sp.wait_ge(table_in, 16)
            sp.wait_ge(ones, 1)

            load_pages(sp, ((pages, "cache_kv", KL),), pages_in, lambda s, c: (pv, NC * s + c + 1), sp_past)
            sp.wait_ge(scored, 1 + (G + 1) * BD)
            sp.dma_start(wuv[:, :, :], I["w_uv"].rearrange("(k p) h d -> p k (h d)", p=P)).then_inc(wuv_in, 16)
            sp.wait_ge(gated, 1)
            sp.dma_start(M.oa_dram, M.oaT[:, :, :]).then_inc(stored, 16)
            sp.wait_ge(stored, 16)

        @block.tensor
        def _(pe):
            pe.wait_ge(fixed_in, 16)

            def transposes(s, b, g):
                if g % 2 == 0:
                    pe.wait_ge(pages_in[b][g // 2], (s - b) * (8 * CP) + 16 * CP)
                    pe.wait_ge(keys_in[b][g // 2], (s - b) * (16 * CP) + 32 * CP)
                pe.wait_ge(cT_sb, 1 + G * s + g)
                for p in range(GP):
                    at = slice(p * P, (p + 1) * P)
                    for r in range(2):
                        nc.tensor.transpose(psA[r][:, at], pages[b][:, GP * g + p, r * P:(r + 1) * P], M.ident[:, :])
                    last = nc.tensor.transpose(psK[0:ROPE, at], kpe[b][:, GP * g + p, :], M.ident[:, :])
                last.then_inc(cT_tr, 1)

            def scores(s, b, g):
                pe.wait_ge(cT_sb, 1 + G * s + g + 1)
                pe.wait_ge(weighted, 1 + G * s + g - 1) if g >= 1 else pe.wait_ge(weighted, 1 + G * s)
                for p in range(GP):
                    at, out = slice(p * P, (p + 1) * P), psS[g % 2][:, p * ROW:(p + 1) * ROW]
                    for r in range(2):
                        nc.tensor.matmul(out, cT[:, g % 2, r, at], M.qlT[:, r, s, :, :].rearrange("p h t -> p (h t)"), start=(r == 0), stop=False)
                    last = nc.tensor.matmul(out, kT[:, g % 2, at], M.qpT[:, s, :, :].rearrange("p h t -> p (h t)"), start=False, stop=True)
                last.then_inc(scored, 1)

            def softmax(s, k):
                if k == 0:
                    pe.wait_ge(topped, s + 1)
                    pe.wait_ge(o_T, 1 + s)
                    nc.tensor.transpose(psM[:, 128:256], top1[:, :], M.ident[:, :]).then_inc(top_tr, 1)
                if k == 1:
                    pe.wait_ge(top_row, s + 1)
                    nc.tensor.transpose(psM[:, 256:384], topb[:, :], M.ident[:, :]).then_inc(top_bc, 1)

            def own_tokens(s):
                pe.wait_ge(centred, 1 + 5 * s)
                for r in range(2):
                    nc.tensor.matmul(psM[:, 0:ROW], M.cnewT[:, r, :], M.qlT[:, r, s, :, :].rearrange("p h t -> p (h t)"), start=(r == 0), stop=False)
                nc.tensor.matmul(psM[:, 0:ROW], M.kpenewT[:, :], M.qpT[:, s, :, :].rearrange("p h t -> p (h t)"), start=False, stop=True).then_inc(scored, 1)

            def weights_times_latents(s, b, more):
                pe.wait_ge(o_sb, 1 + s)
                for j in range(PAGES):
                    if j % CP == 0:
                        pe.wait_ge(exped, s * 5 + j // CP + 1)
                    last = nc.tensor.matmul(psO[:, 0:C1], STs[b][:, j, :], pages[b][:, j, :], start=(j == 0), stop=False)
                    if j % CP == CP - 1 and j < PAGES - 1:
                        last.then_inc(pv, 1)
                pe.wait_ge(exped, s * 5 + 5)
                nc.tensor.matmul(psO[:, 0:C1], STs[b][0:SB, PAGES, :], M.cnew[:, :], start=False, stop=True).then_inc(pv, 1)
                if more:
                    pe.wait_ge(topped, s + 2)
                pe.wait_ge(o_sb, 1 + s + 1)
                for r in range(2):
                    last = nc.tensor.transpose(psM[:, r * P:(r + 1) * P], ol[:, r * P:(r + 1) * P], M.ident[:, :])
                last.then_inc(o_tr, 1)

            def step(s, n, b):
                if n is not None:
                    transposes(n, b, 0)
                    for g in range(G):
                        if s is not None:
                            softmax(s, g)
                        if g + 1 < G:
                            transposes(n, b, g + 1)
                        scores(n, b, g)
                    own_tokens(n)
                elif s is not None:
                    softmax(s, 0)
                    softmax(s, 1)
                if s is not None:
                    weights_times_latents(s, 1 - b, n is not None)

            _samples(pe, step)
            pe.wait_ge(o_T, 1 + BD)
            pe.wait_ge(wuv_in, 16)
            for h in range(H):
                o = psK[VD * (h % 2):VD * (h % 2) + VD, (h // 2) * SB:(h // 2 + 1) * SB]
                for r in range(2):
                    last = nc.tensor.matmul(o, wuv[:, r, h * VD:(h + 1) * VD], olT[:, r, h, :], start=(r == 0), stop=(r == 1))
            last.then_inc(up, 1)

        @block.scalar
        def _(act):
            for b in range(2):
                nc.scalar.activation(pages[b][:, :, KL:C1], M.ones[:, 0:PAGES].unsqueeze(2), ACT.Copy)
            act.drain()
            act.nop().then_inc(ones, 1)

            def exponentials(s, b, q):
                part = STs[b][:, 8 * q:8 * q + 8, :] if q < 4 else STs[b][0:SB, PAGES, :]
                act.wait_ge(centred, 1 + 5 * s + q + 1)
                nc.scalar.activation(part, part, ACT.Exp, scale=SCALE).then_inc(exped, 1)

            def step(s, n, b):
                for g in range(G):
                    if n is not None:
                        act.wait_ge(cT_tr, G * n + g + 1)
                        act.wait_ge(scored, 1 + (G + 1) * n + g - 1) if g >= 1 else act.wait_ge(scored, 1 + (G + 1) * n)
                        for r in range(2):
                            nc.scalar.copy(cT[:, g % 2, r, :], psA[r][:, :])
                        nc.scalar.copy(kT[:, g % 2, :], psK[0:ROPE, :]).then_inc(cT_sb, 1)
                    if s is not None and g >= 3:
                        exponentials(s, 1 - b, g - 3)
                if s is None:
                    return
                act.wait_ge(o_tr, s + 1)
                for r in range(2):
                    last = nc.scalar.copy(olT[:, r, :, bass.ds(s * TD, TD)], psM[:, r * P:(r + 1) * P].rearrange("p (h t) -> p h t", t=TD))
                last.then_inc(o_T, 1)

            _samples(act, step)

        @block.vector
        def _(dve):
            v = nc.vector
            dve.wait_ge(fixed_in, 16)

            def weighted_scores(s, b):
                ST = STs[b]
                for g in range(G):
                    dve.wait_ge(scored, 1 + (G + 1) * s + g + 1)
                    group = ST[:, GP * g:GP * g + GP, :].rearrange("p a (h t) -> p (a h) t", t=TD)
                    ki = kinv[b][:, GP * g:GP * g + GP, :].rearrange("p a h -> p (a h)")
                    v.tensor_tensor(group, psS[g % 2][:, :].rearrange("p (r t) -> p r t", t=TD), bc(ki, TD, 2), ALU.mult).then_inc(weighted, 1)
                    dve.drain()
                    group = ST[:, GP * g:GP * g + GP, :].rearrange("p a r -> p (a r)")
                    if g == 0:
                        v.tensor_copy(top4[:, :], group)
                    else:
                        v.tensor_tensor(top4[:, :], top4[:, :], group, ALU.max)
                dve.wait_ge(scored, 1 + (G + 1) * s + G + 1)
                mine = ST[0:SB, PAGES, :]
                v.tensor_tensor(mine.rearrange("p (h t) -> p h t", t=TD), psM[0:SB, 0:ROW].rearrange("p (h t) -> p h t", t=TD),
                                bc(M.kinvnew[:, :], TD, 2), ALU.mult)
                dve.drain()
                v.tensor_tensor(mine, mine, own[:, s, :], ALU.add)
                dve.drain()
                v.tensor_tensor(top4[0:SB, 0:ROW], top4[0:SB, 0:ROW], mine, ALU.max)
                dve.drain()
                v.tensor_reduce(top1[:, :], top4[:, :].rearrange("p (a r) -> p r a", a=GP), AX.X, ALU.max).then_inc(topped, 1)

            def centre(s, b):
                ST = STs[b]
                dve.wait_ge(top_tr, s + 1)
                v.tensor_reduce(topr[:, :], psM[:, 128:256], AX.X, ALU.max)
                dve.drain()
                v.tensor_copy(topb[:, :], topr[:, 0:1].to_broadcast([ROW, P])).then_inc(top_row, 1)
                dve.wait_ge(top_bc, s + 1)
                v.tensor_copy(topB[:, :], psM[:, 256:384])
                dve.drain()
                for q in range(4):
                    part = ST[:, 8 * q:8 * q + 8, :]
                    v.tensor_tensor(part, part, bc(topB[:, :], 8, 1), ALU.subtract).then_inc(centred, 1)
                mine = ST[0:SB, PAGES, :]
                v.tensor_tensor(mine, mine, topB[0:SB, :], ALU.subtract).then_inc(centred, 1)

            def step(s, n, b):
                if s is not None:
                    centre(s, 1 - b)
                if n is not None:
                    weighted_scores(n, b)
                if s is not None:
                    dve.wait_ge(pv, NC * s + NC)
                    v.reciprocal(ri[:, :], psO[:, KL:C1])
                    dve.drain()
                    v.tensor_scalar(ol[:, :], psO[:, 0:KL], ri[:, 0:1], None, ALU.mult).then_inc(o_sb, 1)

            _samples(dve, step)
            dve.wait_ge(up, 1)
            o = psK[:, :].rearrange("p (a t) -> p a t", t=SB)
            v.memset(M.oaT[:, :, SEQ + SB:TOK], 0.0)
            v.tensor_tensor(M.oaT[:, :, SEQ:SEQ + SB], o, M.zas[:, :, :], ALU.mult).then_inc(gated, 1)


def _samples(engine, step):
    step(None, 0, 0)
    with engine.Fori(0, BD // 2 - 1) as i:
        step(2 * i, 2 * i + 1, 1)
        step(2 * i + 1, 2 * i + 2, 0)
    step(BD - 2, BD - 1, 1)
    step(BD - 1, None, 0)


V_MU, V_MULA, V_W0, V_A0, V_KK, V_KA, V_RK, V_GG, V_GB = 0, 24, 25, 33, 41, 49, 57, 65, 73
NVEC = 81
LEVELS = (2, 4, 8, 16, 32, 64)


def _load_vectors(sp, I, dst, sem):
    rows = lambda name, a, n: I[name][a:a + n * P].rearrange("(k p) -> k p", p=P)
    flat_rk = I["r_k"].rearrange("h d -> (h d)").rearrange("(k p) -> k p", p=P)
    parts = [(V_MU, 8, rows("mu_shift", S_R, 8)), (V_MU + 8, 8, rows("mu_shift", S_K, 8)), (V_MU + 16, 8, rows("mu_shift", S_V, 8)),
             (V_W0, 8, rows("w0", 0, 8)), (V_A0, 8, rows("a0", 0, 8)), (V_KK, 8, rows("k_k", 0, 8)), (V_KA, 8, rows("k_a", 0, 8)),
             (V_RK, 8, flat_rk), (V_GG, 8, rows("gn_g", 0, 8)), (V_GB, 8, rows("gn_b", 0, 8))]
    for at, n, src in parts:
        sp.dma_start(dst[at:at + n, :], src).then_inc(sem, 16)
    for half, at in enumerate((S_WL, S_AL)):
        sp.dma_start(dst[V_MULA:V_MULA + 1, 64 * half:64 * half + 64], I["mu_shift"][at:at + 64].rearrange("(a p) -> a p", a=1)).then_inc(sem, 16)
    return 16 * (len(parts) + 2)


def lora(nc, I, O, M):
    with ExitStack() as ctx:
        sb = lambda name, shape: ctx.enter_context(nc.sbuf_tensor("lo_" + name, shape, F32))
        ps = lambda name: ctx.enter_context(nc.psum_tensor("lo_" + name, [P, 512], F32))
        sem = lambda name: nc.alloc_semaphore("l_" + name)
        vec, ss = sb("vec", [NVEC, P]), sb("ss", [BD, 25, P])
        w = sb("w", [P, KT, P])
        px, pxs, d, ds_ = sb("px", [P, SEQ + 1]), sb("pxs", [P, BD, TD + 1]), sb("d", [P, SEQ]), sb("ds", [P, BD, TD])
        psV, psP, psQ = ps("psV"), ps("psP"), ps("psQ")
        vec_in, w_in_sb, tr, tr_sb, mm, ev, mixed, zeroed = (sem(n) for n in ("vec_in", "w_in", "tr", "tr_sb", "mm", "ev", "mixed", "zeroed"))
        block = ctx.enter_context(nc.Block())
        w_v = I["w_in"].rearrange("(k p) n -> p k n", p=P)
        ALL = 16 * (10 + 2) + 16 * 5

        @block.sync
        def _(sp):
            n = _load_vectors(sp, I, vec, vec_in)
            for i, at in enumerate((S_R, S_K, S_V)):
                sp.dma_start(ss[:, 8 * i:8 * i + 8, :], I["state_shift"][:, at:at + 1024].rearrange("b (k p) -> b k p", p=P)).then_inc(vec_in, 16)
            for half, at in enumerate((S_WL, S_AL)):
                sp.dma_start(ss[:, 24, 64 * half:64 * half + 64], I["state_shift"][:, at:at + 64]).then_inc(vec_in, 16)
                sp.dma_start(w[:, :, 64 * half:64 * half + 64], w_v[:, :, C_SH + at:C_SH + at + 64]).then_inc(w_in_sb, 16)
            assert n + 80 == ALL
            sp.dma_start(M.masks[:, :, :], I["chunk_masks"]).then_inc(M.masks_in, 16)
            sp.dma_start(M.see[:, :, :], I["see_masks"]).then_inc(M.masks_in, 16)
            sp.dma_start(M.seg[:, :], bc(I["segments"], P, 0)).then_inc(M.masks_in, 16)
            sp.dma_start(M.pick[:, :], I["pick"]).then_inc(M.masks_in, 16)
            sp.wait_ge(M.masks_in, 64)

        @block.tensor
        def _(pe):
            pe.wait_ge(vec_in, ALL)
            nc.tensor.transpose(psV[:, 0:NVEC], vec[:, :], M.ident[0:NVEC, 0:NVEC])
            for k in range(25):
                last = nc.tensor.transpose(psV[:, 128 + BD * k:128 + BD * k + BD], ss[:, k, :], M.ident[0:BD, 0:BD])
            last.then_inc(tr, 1)
            pe.wait_ge(w_in_sb, 32)
            for k in range(KT):
                nc.tensor.matmul(psP[:, :], w[:, k, :], M.hT[:, k, 0:SEQ], start=(k == 0), stop=(k == KT - 1))
            for k in range(KT):
                last = nc.tensor.matmul(psQ[:, 0:P], w[:, k, :], M.hT[:, k, SEQ:TOK], start=(k == 0), stop=(k == KT - 1))
            last.then_inc(mm, 1)

        @block.scalar
        def _(act):
            act.wait_ge(mixed, 1)
            nc.scalar.activation(M.la[0:64, :], M.la[0:64, :], ACT.Tanh)

        @block.vector
        def _(dve):
            v = nc.vector
            v.memset(px[:, 0:1], 0.0)
            v.memset(M.la[:, SEQ + SB:TOK], 0.0)
            dve.wait_ge(tr, 1)
            v.tensor_copy(M.vec[:, 0:NVEC], psV[:, 0:NVEC])
            v.tensor_copy(M.ss[:, :, :], psV[:, 128:128 + 25 * BD].rearrange("p (k b) -> p k b", b=BD))
            dve.drain()
            v.tensor_scalar(M.nvec[:, :], M.vec[:, V_W0:V_KK], -1.0, None, ALU.mult)
            v.tensor_copy(pxs[:, :, 0], M.ss[:, 24, :])
            dve.wait_ge(mm, 1)
            v.tensor_copy(px[:, 1:SEQ + 1], psP[:, :])
            v.tensor_copy(pxs[:, :, 1:TD + 1], psQ[:, 0:SB].rearrange("p (b t) -> p b t", t=TD))
            dve.drain()
            v.tensor_copy(M.shc[:, 24, 0:1], px[:, SEQ:SEQ + 1])
            v.tensor_copy(M.shc[:, 24, 1:1 + BD], pxs[:, :, TD])
            v.tensor_tensor(d[:, :], px[:, 0:SEQ], px[:, 1:SEQ + 1], ALU.subtract)
            v.tensor_tensor(ds_[:, :, :], pxs[:, :, 0:TD], pxs[:, :, 1:TD + 1], ALU.subtract)
            dve.drain()
            mu = M.vec[:, V_MULA:V_MULA + 1]
            v.scalar_tensor_tensor(M.la[:, 0:SEQ], d[:, :], mu, px[:, 1:SEQ + 1], ALU.mult, ALU.add)
            v.scalar_tensor_tensor(M.la[:, SEQ:SEQ + SB].rearrange("p (b t) -> p b t", t=TD), ds_[:, :, :], mu, pxs[:, :, 1:TD + 1], ALU.mult, ALU.add).then_inc(mixed, 1)


def rwkv(nc, I, O, M):
    with ExitStack() as ctx:
        sb = lambda name, shape: ctx.enter_context(nc.sbuf_tensor("rw_" + name, shape, F32))
        NU, C5 = 2 * NB, NB
        w = sb("w", [P, 4, KT, P])
        wlo = sb("wlo", [P, 2, P])
        px, pxs = sb("px", [P, 3, SEQ + 1]), sb("pxs", [P, 3, BD, TD + 1])
        dx, xs = sb("dx", [P, 3, TOK]), sb("xs", [P, 3, TOK])
        sa = sb("sa", [P, 2, TOK])
        L, Lx = sb("L", [P, TOK]), sb("Lx", [P, TOK])
        cen, gx, g = sb("cen", [P, PB + 1]), sb("gx", [P, PB + BD]), sb("g", [P, PB + BD])
        kk, kf, rn = sb("kk", [P, TOK]), sb("kf", [P, TOK]), sb("rn", [P, TOK])
        Z, R, B, K = (sb(n, [P, TOK]) for n in ("Z", "R", "B", "K"))
        ob = R
        ZR = sb("ZR", [P, 2, 2, TOK])
        bonus, zb = sb("bonus", [P, TOK]), sb("zb", [P, TOK])
        tm = sb("tm", [P, C5, 4, P])
        gram = sb("gram", [P, NU, 4, P])
        X, XT, W, Nb = (sb(n, [P, NU, P]) for n in ("X", "XT", "W", "Nb"))
        Zt = sb("Zt", [P, NU, RH])
        U0 = sb("U0", [P, C5, 2, RH])
        RT, Phi, Psi, S = sb("RT", [P, C5, P]), sb("Phi", [P, PB, P]), sb("Psi", [P, PB, P]), sb("S", [P, PB + 1, P])
        o, om = sb("o", [P, NU, RH]), sb("om", [P, 2, NU])
        z_raw, z_exp = sb("z_raw", [P, TOK]), sb("z_exp", [P, TOK])
        osq = W[:, :, 0:RH]
        s_in = sb("s_in", [RH, BD, P])
        s0T, s0p = sb("s0T", [P, BD, RH]), sb("s0p", [P, 2, BD, RH])
        ZsT = sb("ZsT", [P, SB])
        selp = W[0:SB, 0:4, :].rearrange("p u (a i) -> p (u a) i", a=2)
        picked = sb("picked", [SB, 4, RH])
        bk2, bkT = sb("bk2", [P, P]), sb("bkT", [P, P])
        uv, uvm = sb("uv", [P, P]), XT[:, 0:BD, :]
        snT = Psi[:, :, :].rearrange("p c (a i) -> p (c a) i", a=2)
        s_out, sp_out = X[0:RH, 0:BD, :], sb("sp_out", [P, P])
        bank = [ctx.enter_context(nc.psum_tensor(f"rw_bank{i}", [P, 512], F32)) for i in range(8)]
        names = ["zeroed", "wlo_zeroed", "w_in", "s_in", "state_out", "stored", "out_sb", "ob_out", "lora_mm", "s0_tr", "proj",
                 "kk_sq", "proj_sb", "kk_sum", "rk_prod", "rk_sum", "zbk", "tm_tr", "zr", "bonus", "tm_sb", "gram_sb",
                 "gram", "nb", "zkv", "zw", "y_mm", "y_sb", "rt_mm", "psi_mm", "zs_mm", "rt_sb", "s_next",
                 "phi_mm", "o_mm", "s0_sb", "seen", "bk2", "o_sb", "bk_tr", "on", "o_tr", "uvm", "sn_mm", "sn",
                 "sn_tr", "px", "sa", "cum", "expd", "z_in_nb", "zsT", "bkT", "mixed", "pxs0", "shc", "kk_max", "rn",
                 "var", "rstd", "dve_past", "pe_past", "pool_past"]
        names += [f"{n}{g}" for n in ("x_sb", "w_mm", "w_sb", "p_mm") for g in range(3)]
        E = {n: nc.alloc_semaphore("r_" + n) for n in names}
        ev = lambda name: E[name]

        w_v = I["w_in"].rearrange("(k p) n -> p k n", p=P)
        masks, see, pick = M.masks, M.see, M.pick
        I_, BLK, NBD = 0, 1, 2
        MB = 3
        LV = 4
        unit = lambda c, h: 2 * c + h
        chunk = lambda t, c: t[:, c * P:(c + 1) * P]
        H0, H1 = slice(0, RH), slice(RH, P)
        halves = (H0, H1)
        block = ctx.enter_context(nc.Block())

        @block.sync
        def _(sp):
            for counted in (ev("out_sb"), ev("state_out"), ev("stored"), ev("mixed"), ev("ob_out"),):
                sp.sem_inc(counted, 1)

            def weights(hp):
                cols = lambda at: bass.ds(hp * P + at, P)
                for n, at in enumerate((C_SH + S_R, C_SH + S_K, C_SH + S_V, C_ZB)):
                    sp.dma_start(w[:, n, :, :], w_v[:, :, cols(at)]).then_inc(ev("w_in"), 16)
                if isinstance(hp, int):
                    sp.wait_ge(ev("wlo_zeroed"), 1)
                sp.dma_start(wlo[H0, 0, :], I["w_decay2"][:, cols(0)]).then_inc(ev("w_in"), 16)
                sp.dma_start(wlo[H1, 1, :], I["w_a2"][:, cols(0)]).then_inc(ev("w_in"), 16)

            def states_in(hp):
                for h in range(2):
                    src = I["state_wkv"][:, bass.ds(2 * hp + h, 1), :, :].rearrange("b h i j -> i (b h) j")
                    sp.dma_start(s_in[:, :, h * RH:(h + 1) * RH], src).then_inc(ev("s_in"), 16)

            def states_out(hp):
                sp.wait_ge(ev("state_out"), 1 + 2 * hp + 2)
                for h in range(2):
                    dst = O["wkv_s"][:, bass.ds(2 * hp + h, 1), :, :].rearrange("b h i j -> i (b h) j")
                    sp.dma_start(dst, s_out[:, :, h * RH:(h + 1) * RH]).then_inc(ev("stored"), 16)
                    dst = O["wkv_p"][0, bass.ds(2 * hp + h, 1), :, :].rearrange("h i j -> (h i) j")
                    sp.dma_start(dst, sp_out[halves[h], halves[h]]).then_inc(ev("stored"), 16)

            def branch_out(hp):
                sp.wait_ge(ev("out_sb"), 1 + hp + 1)
                sp.dma_start(M.ob_dram[:, bass.ds(hp, 1), :].rearrange("p k t -> p (k t)"), ob[:, :]).then_inc(ev("ob_out"), 16)

            weights(0)
            states_in(0)
            with sp.Fori(0, NP - 1) as hp:
                sp.wait_ge(ev("proj"), 4 * hp + 4)
                weights(hp + 1)
                sp.wait_ge(ev("s0_tr"), hp + 1)
                states_in(hp + 1)
                branch_out(hp)
                states_out(hp)
            states_out(NP - 1)
            branch_out(NP - 1)
            sp.wait_ge(ev("stored"), 1 + 64 * NP)
            sp.wait_ge(ev("ob_out"), 1 + 16 * NP)

        @block.tensor
        def _(pe):
            mm, tr = nc.tensor.matmul, nc.tensor.transpose

            def begin(hp, first):
                pe.wait_ge(ev("w_in"), hp * 96 + 96)
                for n, b in enumerate((1, 5)):
                    mm(bank[b][:, :], wlo[:, n, :], M.la[:, 0:SEQ], start=True, stop=True)
                if not first:
                    pe.wait_ge(ev("bkT"), hp)
                for n in range(2):
                    last = mm(bank[0][:, n * P:(n + 1) * P], wlo[:, n, :], M.la[:, SEQ:TOK], start=True, stop=True)
                last.then_inc(ev("lora_mm"), 1)
                if not first:
                    pe.wait_ge(ev("uvm"), hp)
                for n in range(4):
                    for k in range(KT):
                        last = mm(bank[4][:, n * P:(n + 1) * P], w[:, n, k, :], M.hT[:, k, SEQ:TOK], start=(k == 0), stop=(k == KT - 1))
                pe.wait_ge(ev("sa"), hp + 1)
                for n, b in enumerate((1, 5, 2, 3)):
                    for k in range(KT):
                        last = mm(bank[b][:, :], w[:, n, k, :], M.hT[:, k, 0:SEQ], start=(k == 0), stop=(k == KT - 1))
                    last.then_inc(ev("proj"), 1)
                pe.wait_ge(ev("kk_sq"), hp + 1)
                mm(bank[0][:, :], masks[:, BLK, :], Z[:, 0:SEQ], start=True, stop=True)
                mm(bank[1][:, 0:P], masks[:, BLK, :], Z[:, SEQ:TOK], start=True, stop=True).then_inc(ev("kk_sum"), 1)

            def middle(hp):
                once = lambda name: pe.wait_ge(ev(name), hp + 1)
                pe.wait_ge(ev("out_sb"), 1 + hp)
                pe.wait_ge(ev("state_out"), 1 + 2 * hp)
                once("kk_max")
                once("rk_prod")
                mm(bank[1][:, :], masks[:, BLK, :], K[:, 0:SEQ], start=True, stop=True)
                mm(bank[2][:, 0:P], masks[:, BLK, :], K[:, SEQ:TOK], start=True, stop=True).then_inc(ev("rk_sum"), 1)
                once("zbk")
                for c in range(C5):
                    b = (4, 5, 6, 7, 3)[c]
                    for n, src in enumerate((Z[:, :], B[:, :], K[:, :], xs[:, 2, :])):
                        last = tr(bank[b][:, n * P:(n + 1) * P], chunk(src, c), M.ident[:, :])
                    last.then_inc(ev("tm_tr"), 1)
                once("zr")
                once("bonus")
                for u in range(NU):
                    c, h = u // 2, u % 2
                    if u >= 3:
                        pe.wait_ge(ev("gram_sb"), hp * NU + u - 2)
                    b = bank[u % 3]
                    mm(b[:, 0:256], chunk(K, c), ZR[:, h, :, c * P:(c + 1) * P], start=True, stop=True)
                    mm(b[:, 256:512], chunk(B, c), ZR[:, h, :, c * P:(c + 1) * P], start=True, stop=True).then_inc(ev("gram"), 1)
                pe.wait_ge(ev("gram_sb"), hp * NU + NU)
                for lv in range(len(LEVELS)):
                    groups = (0, 1, 2) if lv < 2 else (0, 1)
                    for gr in groups:
                        us = range(4 * gr, min(4 * gr + 4, NU))
                        pe.wait_ge(ev("nb"), hp * 6 + lv + 1)
                        pe.wait_ge(ev(f"x_sb{gr}"), hp * (3 if gr == 2 else 7) + lv + 1)
                        for j, u in enumerate(us):
                            last = mm(bank[gr][:, j * P:(j + 1) * P], Nb[:, u, :], XT[:, u, :], start=True, stop=True)
                        last.then_inc(ev(f"w_mm{gr}"), 1)
                    for gr in groups:
                        us = range(4 * gr, min(4 * gr + 4, NU))
                        pe.wait_ge(ev(f"w_sb{gr}"), hp * (2 if gr == 2 else 6) + lv + 1)
                        pX = (bank[3], bank[5], bank[7])[gr]
                        pT = (bank[4], bank[6], bank[7])[gr]
                        for j, u in enumerate(us):
                            last = mm(pX[:, j * P:(j + 1) * P], W[:, u, :], X[:, u, :], start=True, stop=True)
                        if lv == 4:
                            off = 256 if gr == 2 else 0
                            for j, u in enumerate(us):
                                last = mm(pT[:, off + j * P:off + (j + 1) * P], X[:, u, :], W[:, u, :], start=True, stop=True)
                        last.then_inc(ev(f"p_mm{gr}"), 1)
                for u in range(NU):
                    c, h = u // 2, u % 2
                    last = mm(bank[0 if u < 8 else 1][:, (u % 8) * RH:(u % 8 + 1) * RH], gram[:, u, 0, :], tm[:, c, 3, h * RH:(h + 1) * RH], start=True, stop=True)
                last.then_inc(ev("zkv"), 1)
                once("zw")
                for gr in range(3):
                    pe.wait_ge(ev(f"x_sb{gr}"), (hp + 1) * (3 if gr == 2 else 7))
                for u in range(NU):
                    last = mm(bank[2 + u // 4][:, (u % 4) * P:(u % 4 + 1) * P], X[:, u, :], Nb[:, u, :], start=True, stop=True)
                last.then_inc(ev("y_mm"), 1)
                once("y_sb")
                for c in range(C5):
                    b = bank[5 + c // 2]
                    at = (c % 2) * 256
                    for h in range(2):
                        u = unit(c, h)
                        mm(b[halves[h], at:at + P], Zt[:, u, :], gram[:, u, 3, :], start=True, stop=True)
                        last = mm(b[halves[h], at + P:at + 256], Zt[:, u, :], tm[:, c, 1, :], start=True, stop=True)
                last.then_inc(ev("rt_mm"), 1)
                for c in range(PB):
                    mm(bank[0][:, c * P:(c + 1) * P], tm[:, c, 1, :], U0[:, c, :, :].rearrange("p h i -> p (h i)"), start=True, stop=False)
                    last = mm(bank[0][:, c * P:(c + 1) * P], tm[:, c, 2, :], tm[:, c, 3, :], start=False, stop=True)
                last.then_inc(ev("psi_mm"), 1)
                pe.wait_ge(ev("s_in"), hp * 32 + 32)
                pe.sem_inc(ev("pe_past"), 1)
                for b in range(BD):
                    last = tr(bank[2][:, b * RH:(b + 1) * RH], s_in[:, b, :], M.ident[0:RH, 0:RH])
                last.then_inc(ev("s0_tr"), 1)
                for h in range(2):
                    last = mm(bank[3][halves[h], 0:SB], tm[:, PB, 0, h * RH:(h + 1) * RH], X[:, unit(PB, h), 0:SB], start=True, stop=True)
                last.then_inc(ev("zs_mm"), 1)
                once("rt_sb")
                for c in range(1, PB):
                    pe.wait_ge(ev("s_next"), hp * PB + c)
                    mm(bank[4][:, (c - 1) * P:c * P], Phi[:, c, :], S[:, c, :], start=True, stop=True).then_inc(ev("phi_mm"), 1)
                for c in range(C5):
                    b = bank[1] if c < PB else bank[5]
                    at = (c % PB) * P
                    for h in range(2):
                        u = unit(c, h)
                        out = b[:, at + h * RH:at + (h + 1) * RH]
                        mm(out, gram[:, u, 3, :], U0[:, c, h, :], start=True, stop=False)
                        last = mm(out, gram[:, u, 1, :], tm[:, c, 3, h * RH:(h + 1) * RH], start=False, stop=not 1 <= c < PB)
                        if 1 <= c < PB:
                            last = mm(out, RT[:, c, :], S[:, c, h * RH:(h + 1) * RH], start=False, stop=True)
                last.then_inc(ev("o_mm"), 1)
                once("s0_sb")
                for n in range(4):
                    q, h = n // 2, n % 2
                    b = bank[(6, 7, 2, 3)[n]]
                    lhs = ZsT[:, :] if q == 0 else RT[:, PB, 0:SB]
                    mm(b[0:SB, :], lhs, s0p[:, h, :, :].rearrange("p b i -> p (b i)"), start=True, stop=True).then_inc(ev("seen"), 1)
                pe.wait_ge(ev("s_next"), hp * PB + PB)
                once("bk2")
                once("o_sb")
                tr(bank[0][:, 0:P], S[:, PB, :], M.ident[:, :])
                tr(bank[0][:, P:2 * P], bk2[:, :], M.ident[:, :])
                tr(bank[4][:, 0:P], uv[:, :], M.ident[:, :]).then_inc(ev("bk_tr"), 1)

            def finish(hp, last_pair):
                once = lambda name: pe.wait_ge(ev(name), hp + 1)
                once("uvm")
                once("on")
                for c in range(C5):
                    src = o[:, 2 * c:2 * c + 2, :].rearrange("p h i -> p (h i)")
                    last = tr(bank[6 if c < PB else 7][:, (c % PB) * P:(c % PB + 1) * P], src, M.ident[:, :])
                last.then_inc(ev("o_tr"), 1)
                if not last_pair:
                    pe.wait_ge(ev("proj_sb"), hp + 2)
                    pe.wait_ge(ev("kk_max"), hp + 2)
                for n, b in enumerate((1, 5)):
                    last = mm(bank[b][:, :], bkT[:, :], uvm[:, 4 * n:4 * n + 4, :].rearrange("p b i -> p (b i)"), start=True, stop=True)
                last.then_inc(ev("sn_mm"), 1)
                once("sn")
                pe.sem_inc(ev("pe_past"), 1)
                for b in range(BD):
                    last = tr(bank[2 + b // 4][0:RH, (b % 4) * P:(b % 4 + 1) * P], snT[:, b, :], M.ident[:, :])
                last.then_inc(ev("sn_tr"), 1)

            _pairs(pe, begin, middle, finish)

        @block.scalar
        def _(act):
            a = nc.scalar
            vcol = lambda t, hp, at: t[:, bass.ds(hp + at, 1)]

            def begin(hp, first):
                act.wait_ge(ev("lora_mm"), hp + 1)
                for n, at in enumerate((0, V_A0 - V_W0)):
                    a.activation(sa[:, n, 0:SEQ], bank[(1, 5)[n]][:, :], ACT.Exp, bias=vcol(M.nvec, hp, at), scale=-1.0)
                    last = a.activation(sa[:, n, SEQ:TOK], bank[0][:, n * P:(n + 1) * P], ACT.Exp, bias=vcol(M.nvec, hp, at), scale=-1.0)
                last.then_inc(ev("sa"), 1)
                for n, b in enumerate((1, 5, 2)):
                    act.wait_ge(ev("proj"), 4 * hp + n + 1)
                    a.copy(px[:, n, 1:SEQ + 1], bank[b][:, :])
                    a.copy(pxs[:, n, :, 1:TD + 1], bank[4][:, n * P:n * P + SB].rearrange("p (b t) -> p b t", t=TD)).then_inc(ev("px"), 1)
                act.wait_ge(ev("proj"), 4 * hp + 4)
                a.copy(z_raw[:, 0:SEQ], bank[3][:, :])
                a.copy(z_raw[:, SEQ:TOK], bank[4][:, 3 * P:4 * P])
                a.activation(z_exp[:, 0:SEQ], bank[3][:, :], ACT.Exp, scale=-1.0)
                a.activation(z_exp[:, SEQ:TOK], bank[4][:, 3 * P:4 * P], ACT.Exp, scale=-1.0).then_inc(ev("proj_sb"), 1)
                act.wait_ge(ev("kk_max"), hp + 1)
                a.activation(rn[:, :], rn[:, :], ACT.Sqrt).then_inc(ev("rn"), 1)

            def middle(hp):
                once = lambda name: act.wait_ge(ev(name), hp + 1)
                act.wait_ge(ev("mixed"), 1 + hp + 1)
                once("cum")
                a.activation(g[:, :], gx[:, :], ACT.Exp, scale=LD)
                a.activation(dx[:, 0, :], L[:, :], ACT.Exp, scale=LD)
                a.activation(dx[:, 1, :], Lx[:, :], ACT.Exp, scale=LD)
                a.activation(dx[:, 2, :], L[:, :], ACT.Exp, scale=-LD).then_inc(ev("expd"), 1)
                once("zbk")
                for h in range(2):
                    rows = halves[h]
                    a.copy(ZR[rows, h, 0, :], Z[rows, :])
                    last = a.copy(ZR[rows, h, 1, :], R[rows, :])
                last.then_inc(ev("zr"), 1)
                for c in range(C5):
                    b = (4, 5, 6, 7, 3)[c]
                    act.wait_ge(ev("tm_tr"), hp * C5 + c + 1)
                    a.copy(tm[:, c, :, :], bank[b][:, :].rearrange("p (n t) -> p n t", t=P)).then_inc(ev("tm_sb"), 1)
                for lv in range(len(LEVELS)):
                    for gr in ((0, 1, 2) if lv < 2 else (0, 1)):
                        us = slice(4 * gr, min(4 * gr + 4, NU))
                        n = us.stop - us.start
                        act.wait_ge(ev(f"w_mm{gr}"), hp * (2 if gr == 2 else 6) + lv + 1)
                        a.copy(W[:, us, :], bank[gr][:, 0:n * P].rearrange("p (u t) -> p u t", t=P)).then_inc(ev(f"w_sb{gr}"), 1)
                once("zkv")
                once("z_in_nb")
                a.copy(Nb[:, 0:8, RH:P], bank[0][:, :].rearrange("p (u i) -> p u i", i=RH))
                a.copy(Nb[:, 8:NU, RH:P], bank[1][:, 0:2 * RH].rearrange("p (u i) -> p u i", i=RH)).then_inc(ev("zw"), 1)
                once("y_mm")
                for gr in range(3):
                    n = min(4, NU - 4 * gr)
                    y = bank[2 + gr][:, 0:n * P].rearrange("p (u a i) -> p u a i", a=2, i=RH)
                    a.copy(Zt[:, 4 * gr:4 * gr + n, :], y[:, :, 0, :])
                    last = a.mul(U0[:, 2 * gr:2 * gr + n // 2, :, :].rearrange("p c h i -> p (c h) i"), y[:, :, 1, :], -1.0)
                last.then_inc(ev("y_sb"), 1)
                once("zs_mm")
                a.copy(ZsT[:, :], bank[3][:, 0:SB]).then_inc(ev("zsT"), 1)
                once("o_mm")
                a.copy(o[:, 0:8, :], bank[1][:, :].rearrange("p (u i) -> p u i", i=RH))
                a.copy(o[:, 8:NU, :], bank[5][:, 0:P].rearrange("p (u i) -> p u i", i=RH)).then_inc(ev("o_sb"), 1)
                once("bk_tr")
                act.wait_ge(ev("stored"), 1 + 64 * hp)
                a.copy(sp_out[:, :], bank[0][:, 0:P]).then_inc(ev("state_out"), 1)
                a.copy(bkT[:, :], bank[0][:, P:2 * P]).then_inc(ev("bkT"), 1)

            def finish(hp, last_pair):
                act.wait_ge(ev("sn_tr"), hp + 1)
                for n in range(2):
                    last = a.copy(s_out[:, 4 * n:4 * n + 4, :], bank[2 + n][0:RH, :].rearrange("p (b t) -> p b t", t=P))
                last.then_inc(ev("state_out"), 1)

            _pairs(act, begin, middle, finish)

        @block.gpsimd
        def _(pool):
            p = nc.gpsimd
            p.memset(wlo[:, :, :], 0.0).then_inc(ev("wlo_zeroed"), 1)
            p.memset(ZR[:, :, :, :], 0.0)
            p.memset(s0p[:, :, :, :], 0.0)
            p.memset(xs[:, :, SEQ + SB:TOK], 0.0)
            p.memset(bk2[:, :], 0.0)
            p.memset(uv[:, :], 0.0)
            p.memset(M.mhalf[:, :], -0.5)
            p.memset(px[:, :, 0:1], 0.0).then_inc(ev("zeroed"), 1)
            with pool.Fori(0, NP) as hp:
                once = lambda name: pool.wait_ge(ev(name), hp + 1)
                pool.wait_ge(ev("mixed"), 1 + hp)
                p.tensor_copy(pxs[:, :, :, 0], M.ss[:, 0:24, :].rearrange("p (n k) b -> p n k b", k=NP)[:, :, bass.ds(hp, 1), :].rearrange("p n k b -> p n (k b)")).then_inc(ev("pxs0"), 1)
                pool.wait_ge(ev("px"), 3 * hp + 3)
                pool.sem_inc(ev("pool_past"), 1)
                shc = M.shc[:, 0:24, :].rearrange("p (n k) b -> p n k b", k=NP)[:, :, bass.ds(hp, 1), :].rearrange("p n k b -> p n (k b)")
                p.tensor_copy(shc[:, :, 0:1], px[:, :, SEQ:SEQ + 1])
                p.tensor_copy(shc[:, :, 1:1 + BD], pxs[:, :, :, TD]).then_inc(ev("shc"), 1)
                pool.wait_ge(ev("gram_sb"), hp * NU + NU)
                for lv in range(len(LEVELS)):
                    n = NU if lv < 2 else 8
                    if lv:
                        pool.wait_ge(ev("w_mm0"), hp * 6 + lv)
                        pool.wait_ge(ev("w_mm1"), hp * 6 + lv)
                        if lv <= 2:
                            pool.wait_ge(ev("w_mm2"), hp * 2 + lv)
                    p.tensor_tensor(Nb[:, 0:n, :], gram[:, 0:n, 2, :], bc(masks[:, LV + lv, :], n, 1), ALU.mult).then_inc(ev("nb"), 1)
                pool.wait_ge(ev("w_mm0"), hp * 6 + 6)
                pool.wait_ge(ev("w_mm1"), hp * 6 + 6)
                pool.sem_inc(ev("pool_past"), 1)
                p.tensor_copy(Nb[:, :, 0:RH].rearrange("p (c h) i -> p c h i", h=2), tm[:, :, 0, :].rearrange("p c (h i) -> p c h i", h=2)).then_inc(ev("z_in_nb"), 1)
                once("var")
                p.tensor_tensor(om[:, 1, :], om[:, 1, :], M.mhalf[:, 0:1].to_broadcast([P, NU]), ALU.pow).then_inc(ev("rstd"), 1)

        @block.vector
        def _(dve):
            v = nc.vector
            tt, ts, stt = v.tensor_tensor, v.tensor_scalar, v.scalar_tensor_tensor
            dr = dve.drain
            by_b = lambda t: t.rearrange("p (b t) -> p b t", t=TD)
            v.memset(gram[:, :, :, :], 0.0)
            dve.wait_ge(ev("zeroed"), 1)
            vec_at = lambda hp, at: M.vec[:, bass.ds(hp + at, 1)]

            def begin(hp, first):
                once = lambda name: dve.wait_ge(ev(name), hp + 1)
                vcol = lambda at: vec_at(hp, at)
                once("sa")
                ts(sa[:, :, :], sa[:, :, :], 1.0, None, ALU.add)
                dr()
                v.reciprocal(sa[:, :, :], sa[:, :, :])
                dr()
                v.tensor_tensor_scan(L[:, :], M.seg[:, :], sa[:, 0, :], 0.0, ALU.mult, ALU.add)
                dr()
                Lp = L[:, 0:SEQ].rearrange("p (c t) -> p c t", t=P)
                v.tensor_copy(cen[:, 0:PB], Lp[:, :, P // 2 - 1])
                v.memset(cen[:, PB:PB + 1], 0.0)
                v.tensor_copy(gx[:, PB:PB + BD], by_b(L[:, SEQ:SEQ + SB])[:, :, TD - 1])
                dr()
                tt(gx[:, 0:PB], Lp[:, :, P - 1], cen[:, 0:PB], ALU.subtract)
                dr()
                tt(gx[:, 0:PB], gx[:, 0:PB], cen[:, 1:PB + 1], ALU.add)
                tt(Lp, Lp, bc(cen[:, 0:PB], P, 2), ALU.subtract)
                dr()
                tt(Lx[:, :], L[:, :], sa[:, 0, :], ALU.subtract).then_inc(ev("cum"), 1)
                dve.wait_ge(ev("px"), 3 * hp + 3)
                once("pxs0")
                tt(dx[:, :, 0:SEQ], px[:, :, 0:SEQ], px[:, :, 1:SEQ + 1], ALU.subtract)
                for n in range(3):
                    tt(by_b(dx[:, n, SEQ:SEQ + SB]), pxs[:, n, :, 0:TD], pxs[:, n, :, 1:TD + 1], ALU.subtract)
                dr()
                for n in range(3):
                    stt(xs[:, n, 0:SEQ], dx[:, n, 0:SEQ], vcol(V_MU + 8 * n), px[:, n, 1:SEQ + 1], ALU.mult, ALU.add)
                    last = stt(by_b(xs[:, n, SEQ:SEQ + SB]), by_b(dx[:, n, SEQ:SEQ + SB]), vcol(V_MU + 8 * n), pxs[:, n, :, 1:TD + 1], ALU.mult, ALU.add)
                last.then_inc(ev("mixed"), 1)
                dr()
                ts(kk[:, :], xs[:, 1, :], vcol(V_KK), None, ALU.mult)
                dr()
                tt(Z[:, :], kk[:, :], kk[:, :], ALU.mult).then_inc(ev("kk_sq"), 1)
                ts(kf[:, :], sa[:, 1, :], 1.0, vcol(V_KA), ALU.subtract, ALU.mult)
                dr()
                stt(kf[:, :], kf[:, :], 1.0, xs[:, 1, :], ALU.add, ALU.mult)
                dr()
                stt(K[:, :], xs[:, 0, :], vcol(V_RK), kf[:, :], ALU.mult, ALU.mult).then_inc(ev("rk_prod"), 1)
                once("kk_sum")
                ts(rn[:, 0:SEQ], bank[0][:, :], 1e-24, None, ALU.max)
                ts(rn[:, SEQ:TOK], bank[1][:, 0:P], 1e-24, None, ALU.max).then_inc(ev("kk_max"), 1)

            def middle(hp):
                once = lambda name: dve.wait_ge(ev(name), hp + 1)
                vcol = lambda at: vec_at(hp, at)
                once("rn")
                v.reciprocal(rn[:, :], rn[:, :])
                dr()
                tt(kk[:, :], kk[:, :], rn[:, :], ALU.mult)
                dr()
                once("expd")
                dve.wait_ge(ev("ob_out"), 1 + 16 * hp)
                tt(Z[:, :], kk[:, :], dx[:, 1, :], ALU.mult)
                tt(R[:, :], xs[:, 0, :], dx[:, 0, :], ALU.mult)
                once("rk_sum")
                tt(K[:, :], kf[:, :], dx[:, 2, :], ALU.mult)
                tt(B[:, :], kk[:, :], sa[:, 1, :], ALU.mult)
                dr()
                tt(B[:, :], B[:, :], dx[:, 2, :], ALU.mult).then_inc(ev("zbk"), 1)
                dr()
                v.tensor_copy(bk2[:, 0:SB], B[:, SEQ:SEQ + SB])
                v.tensor_copy(bk2[:, SB:2 * SB], K[:, SEQ:SEQ + SB])
                v.tensor_copy(uv[:, SB:2 * SB], xs[:, 2, SEQ:SEQ + SB]).then_inc(ev("bk2"), 1)
                tt(bonus[:, 0:SEQ], bank[1][:, :], xs[:, 2, 0:SEQ], ALU.mult)
                tt(bonus[:, SEQ:TOK], bank[2][:, 0:P], xs[:, 2, SEQ:TOK], ALU.mult).then_inc(ev("bonus"), 1)
                for u in range(NU):
                    m = 0 if u < 8 else 1
                    dve.wait_ge(ev("gram"), hp * NU + u + 1)
                    dve.sem_inc(ev("dve_past"), 1)
                    v.copy_predicated(gram[:, u, :, :].rearrange("p a t -> p (a t)"), see[:, m, :], bank[u % 3][:, :]).then_inc(ev("gram_sb"), 1)
                def transposed(us):
                    return v.transpose(XT[:, us, :].rearrange("p u t -> p (u t)"), X[:, us, :].rearrange("p u t -> p (u t)"))

                dr()
                dve.wait_ge(ev("stored"), 1 + 64 * hp)
                one = bc(masks[:, I_, :], 4, 1)
                for gr in range(3):
                    n = min(4, NU - 4 * gr)
                    us = slice(4 * gr, 4 * gr + n)
                    tt(X[:, us, :], gram[:, us, 2, :], bc(masks[:, MB, :], n, 1), ALU.mult)
                    dr()
                    tt(X[:, us, :], one[:, 0:n, :], X[:, us, :], ALU.subtract)
                    dr()
                    transposed(us).then_inc(ev(f"x_sb{gr}"), 1)
                for lv in range(len(LEVELS)):
                    for gr in ((0, 1, 2) if lv < 2 else (0, 1)):
                        n = min(4, NU - 4 * gr)
                        us = slice(4 * gr, 4 * gr + n)
                        dve.wait_ge(ev(f"p_mm{gr}"), hp * (2 if gr == 2 else 6) + lv + 1)
                        pX = (bank[3], bank[5], bank[7])[gr][:, 0:n * P].rearrange("p (u t) -> p u t", t=P)
                        off = 256 if gr == 2 else 0
                        pT = (bank[4], bank[6], bank[7])[gr][:, off:off + n * P].rearrange("p (u t) -> p u t", t=P)
                        last = tt(X[:, us, :], X[:, us, :], pX, ALU.subtract)
                        if lv < 4:
                            dr()
                            last = transposed(us)
                        elif lv == 4:
                            last = tt(XT[:, us, :], XT[:, us, :], pT, ALU.subtract)
                        last.then_inc(ev(f"x_sb{gr}"), 1)
                    dr()
                once("rt_mm")
                for q in range(3):
                    n = min(2, C5 - 2 * q)
                    got = bank[5 + q][:, 0:n * 256].rearrange("p (c a t) -> p c a t", a=2, t=P)
                    tt(RT[:, 2 * q:2 * q + n, :], R[:, 2 * q * P:(2 * q + n) * P].rearrange("p (c t) -> p c t", t=P), got[:, :, 0, :], ALU.subtract)
                    if q < 2:
                        tt(Phi[:, 2 * q:2 * q + 2, :], got[:, :, 1, :], bc(masks[:, NBD, :], 2, 1), ALU.mult)
                dr()
                tt(Phi[:, :, :], Phi[:, :, :], bc(masks[:, I_, :], PB, 1), ALU.add).then_inc(ev("rt_sb"), 1)
                once("psi_mm")
                for c in range(PB):
                    stt((S[:, 1, :] if c == 0 else Psi[:, c, :]), bank[0][:, c * P:(c + 1) * P], g[:, c:c + 1], masks[:, BLK, :], ALU.mult, ALU.mult)
                dr()
                dve.nop().then_inc(ev("s_next"), 1)
                for c in range(1, PB):
                    dve.wait_ge(ev("phi_mm"), hp * (PB - 1) + c)
                    stt(S[:, c + 1, :], bank[4][:, (c - 1) * P:c * P], g[:, c:c + 1], Psi[:, c, :], ALU.mult, ALU.add).then_inc(ev("s_next"), 1)
                    if c == 1:
                        once("s0_tr")
                        v.tensor_copy(s0T[:, :, :], bank[2][:, :].rearrange("p (b i) -> p b i", i=RH))
                        for h in range(2):
                            v.tensor_copy(s0p[halves[h], h, :, :], bank[2][halves[h], :].rearrange("p (b i) -> p b i", i=RH))
                        once("zsT")
                        dve.nop().then_inc(ev("s0_sb"), 1)
                once("proj_sb")
                ts(z_exp[:, :], z_exp[:, :], 1.0, None, ALU.add)
                dr()
                v.reciprocal(z_exp[:, :], z_exp[:, :])
                dr()
                tt(zb[:, :], z_raw[:, :], z_exp[:, :], ALU.mult)
                dr()
                for n in range(4):
                    dve.wait_ge(ev("seen"), 4 * hp + n + 1)
                    tt(selp[:, :, :], bank[(6, 7, 2, 3)[n]][0:SB, :].rearrange("p (b i) -> p b i", i=RH), bc(pick[:, 0:BD][0:SB], RH, 2), ALU.mult)
                    dr()
                    v.tensor_reduce(picked[:, n, :], selp[:, :, :].rearrange("p b i -> p i b"), AX.X, ALU.add)
                    dr()
                once("bk_tr")
                tt(uv[0:SB, :].rearrange("p (h i) -> p h i", h=2), U0[0:SB, PB, :, :], picked[:, 0:2, :], ALU.subtract)
                v.tensor_copy(uv[SB:P, :], bank[4][SB:P, 0:P])
                dr()
                tt(uvm[:, :, :], bc(uv[:, :], BD, 1), bc(pick[:, 0:BD], P, 2), ALU.mult)
                dr()
                v.memset(uv[:, 0:SB], 0.0)
                once("bkT")
                dve.nop().then_inc(ev("uvm"), 1)
                once("o_sb")
                tt(o[0:SB, 8:NU, :], o[0:SB, 8:NU, :], picked[:, 2:4, :], ALU.add)
                dr()
                v.tensor_reduce(om[:, 0, :], o[:, :, :], AX.X, ALU.add)
                dr()
                ts(om[:, 0, :], om[:, 0, :], 1.0 / RH, None, ALU.mult)
                dr()
                tt(o[:, :, :], o[:, :, :], bc(om[:, 0, :], RH, 2), ALU.subtract)
                dr()
                tt(osq[:, :, :], o[:, :, :], o[:, :, :], ALU.mult)
                dr()
                v.tensor_reduce(om[:, 1, :], osq[:, :, :], AX.X, ALU.add)
                dr()
                ts(om[:, 1, :], om[:, 1, :], 1.0 / RH, GN_EPS, ALU.mult, ALU.add).then_inc(ev("var"), 1)
                once("rstd")
                tt(o[:, :, :], o[:, :, :], bc(om[:, 1, :], RH, 2), ALU.mult).then_inc(ev("on"), 1)

            def finish(hp, last_pair):
                once = lambda name: dve.wait_ge(ev(name), hp + 1)
                vcol = lambda at: vec_at(hp, at)
                once("o_tr")
                for cols, b, n in ((slice(0, SEQ), bank[6], SEQ), (slice(SEQ, TOK), bank[7], P)):
                    ts(ob[:, cols], b[:, 0:n], vcol(V_GG), vcol(V_GB), ALU.mult, ALU.add)
                dr()
                tt(ob[:, :], ob[:, :], bonus[:, :], ALU.add)
                dr()
                tt(ob[:, :], ob[:, :], zb[:, :], ALU.mult).then_inc(ev("out_sb"), 1)
                once("sn_mm")
                for n in range(2):
                    bs = slice(4 * n, 4 * n + 4)
                    for h in range(2):
                        rows = halves[h]
                        got = bank[(1, 5)[n]][rows, :].rearrange("p (b h i) -> p b h i", b=4, h=2)[:, :, h, :]
                        tt(snT[rows, bs, :], s0T[rows, bs, :], got, ALU.add)
                dr()
                tt(snT[:, :, :], snT[:, :, :], bc(g[:, PB:PB + BD], RH, 2), ALU.mult).then_inc(ev("sn"), 1)

            _pairs(dve, begin, middle, finish)


def _pairs(engine, begin, middle, finish):
    begin(0, True)
    with engine.Fori(0, NP - 1) as hp:
        middle(hp)
        begin(hp + 1, False)
        finish(hp, False)
    middle(NP - 1)
    finish(NP - 1, True)


def store_shift(nc, O, M):
    with ExitStack() as ctx:
        shrow = ctx.enter_context(nc.sbuf_tensor("shrow", [1 + BD, 25, P], F32))
        bank = [ctx.enter_context(nc.psum_tensor(f"sh_bank{i}", [P, 512], F32)) for i in range(7)]
        tr, tr_sb, stored = (nc.alloc_semaphore("sh_" + n) for n in ("tr", "tr_sb", "stored"))
        block = ctx.enter_context(nc.Block())

        @block.tensor
        def _(pe):
            for k in range(25):
                last = nc.tensor.transpose(bank[k // 4][0:1 + BD, (k % 4) * P:(k % 4 + 1) * P], M.shc[:, k, :], M.ident[:, :])
            last.then_inc(tr, 1)

        @block.vector
        def _(dve):
            dve.wait_ge(tr, 1)
            for q in range(7):
                n = min(4, 25 - 4 * q)
                last = nc.vector.tensor_copy(shrow[:, 4 * q:4 * q + n, :], bank[q][0:1 + BD, 0:n * P].rearrange("p (k t) -> p k t", t=P))
            last.then_inc(tr_sb, 1)

        @block.sync
        def _(sp):
            sp.wait_ge(tr_sb, 1)
            n = 0
            for rows, dst in ((slice(0, 1), O["shift_p"]), (slice(1, 1 + BD), O["shift_s"])):
                for i, at in enumerate((S_R, S_K, S_V)):
                    sp.dma_start(dst[:, at:at + 1024].rearrange("b (k p) -> b k p", p=P), shrow[rows, 8 * i:8 * i + 8, :]).then_inc(stored, 16)
                for half, at in enumerate((S_WL, S_AL)):
                    sp.dma_start(dst[:, at:at + 64], shrow[rows, 24, 64 * half:64 * half + 64]).then_inc(stored, 16)
                n += 5
            sp.wait_ge(stored, 16 * n)


def merge(nc, I, O, M):
    with ExitStack() as ctx:
        sb = lambda name, shape: ctx.enter_context(nc.sbuf_tensor("me_" + name, shape, F32))
        ps = lambda name: ctx.enter_context(nc.psum_tensor("me_" + name, [P, 512], F32))
        sem = lambda name: ctx.enter_context(nc.semaphore("m_" + name))
        w = [sb(f"w{i}", [P, 4, KT, P]) for i in range(2)]
        wo = sb("wo", [P, KT, D])
        oaT, obT = sb("oaT", [P, KT, TOK]), sb("obT", [P, KT, TOK])
        mT, sg, t = sb("mT", [P, KT, TOK]), sb("sg", [P, 2, TOK]), sb("t", [P, 2, TOK])
        sel, gs = sb("sel", [1 + BD, 2 * P]), sb("gs", [P, 2, D])
        xb = [sb(f"xb{i}", [P, D]) for i in range(2)]
        big, small = [ps(f"big{i}") for i in range(4)], [ps("small0"), ps("small1")]
        psY = [ps("psY0"), ps("psY1")]
        w_in_sb, x_in, y_out = [sem("w_in0"), sem("w_in1")], [sem("x_in0"), sem("x_in1")], [sem("y_out0"), sem("y_out1")]
        branch_in = sem("branch_in")
        fixed_in, proj, gated, summed, m_done, spread, spread_sb, y_mm, y_sb = (
            sem(n) for n in ("fixed_in", "proj", "gated", "summed", "m_done", "spread", "spread_sb", "y_mm", "y_sb"))
        w_v = I["w_in"].rearrange("(k p) n -> p k n", p=P)
        pa_v, pb_v = (I[n].rearrange("(k p) n -> p k n", p=P) for n in ("w_pa", "w_pb"))
        rows = lambda b: P if b < PB else SB
        block = ctx.enter_context(nc.Block())

        @block.sync
        def _(sp):
            for counted in (gated, summed, m_done,):
                sp.sem_inc(counted, 1)
            def load(b, j):
                for n, (src, at) in enumerate(((w_v, C_GA), (w_v, C_GB), (pa_v, 0), (pb_v, 0))):
                    sp.dma_start(w[b][:, n, :, :], src[:, :, bass.ds(j * P + at, P)]).then_inc(w_in_sb[b], 16)

            def x_of(b):
                src = I["x_prompt"][0, b * P:(b + 1) * P, :] if b < PB else I["x_sample"].rearrange("b t d -> (b t) d")
                sp.dma_start(xb[b % 2][0:rows(b), :], src).then_inc(x_in[b % 2], 16)

            load(0, 0)
            sp.dma_start(oaT[:, :, :], M.oa_dram).then_inc(branch_in, 16)
            sp.dma_start(obT[:, :, :], M.ob_dram).then_inc(branch_in, 16)
            load(1, 1)
            sp.dma_start(sel[:, :], I["sel"]).then_inc(fixed_in, 16)
            with sp.Fori(1, KT // 2) as i:
                for b in range(2):
                    sp.wait_ge(proj, 4 * (2 * i + b - 1))
                    load(b, 2 * i + b)
            sp.dma_start(wo[:, :, :], I["w_out"].rearrange("(k p) n -> p k n", p=P)).then_inc(fixed_in, 16)
            x_of(0)
            x_of(1)
            for b in range(NB):
                sp.wait_ge(y_sb, 2 * b + 2)
                dst = O["y_p"][0, b * P:(b + 1) * P, :] if b < PB else O["y_s"].rearrange("b t d -> (b t) d")
                sp.dma_start(dst, xb[b % 2][0:rows(b), :]).then_inc(y_out[b % 2], 16)
                if b + 2 < NB:
                    sp.wait_ge(y_out[b % 2], 16 * (b // 2 + 1))
                    x_of(b + 2)
            sp.wait_ge(y_out[0], 16 * ((NB + 1) // 2))
            sp.wait_ge(y_out[1], 16 * (NB // 2))

        @block.tensor
        def _(pe):
            with pe.Fori(0, KT // 2) as i:
                for b in range(2):
                    j = 2 * i + b
                    pe.wait_ge(w_in_sb[b], i * 64 + 64)
                    for n, src in enumerate((M.hT, M.hT, oaT, obT)):
                        if n == 0:
                            pe.wait_ge(gated, 1 + 2 * j)
                            pe.wait_ge(summed, 1 + 2 * i)
                        if n == 2:
                            pe.wait_ge(branch_in, 32)
                            pe.wait_ge(summed, 1 + j)
                        for k in range(KT):
                            nc.tensor.matmul(big[n][:, :], w[b][:, n, k, :], src[:, k, 0:SEQ], start=(k == 0), stop=(k == KT - 1))
                        for k in range(KT):
                            last = nc.tensor.matmul(small[b][:, n * P:(n + 1) * P], w[b][:, n, k, :], src[:, k, SEQ:TOK], start=(k == 0), stop=(k == KT - 1))
                        last.then_inc(proj, 1)
            pe.wait_ge(fixed_in, 32)
            for q in range(4):
                if q >= 2:
                    pe.wait_ge(spread_sb, q - 1)
                nc.tensor.matmul(psY[q % 2][:, :], sel[:, (q // 2) * P:(q // 2 + 1) * P], M.gate[:, (q % 2) * 512:(q % 2 + 1) * 512],
                                 start=True, stop=True).then_inc(spread, 1)
            pe.wait_ge(m_done, 1 + KT)
            pe.wait_ge(spread_sb, 4)
            for b in range(NB):
                for n in range(2):
                    u = 2 * b + n
                    if u >= 2:
                        pe.wait_ge(y_sb, u - 1)
                    for k in range(KT):
                        last = nc.tensor.matmul(psY[n][0:rows(b), :], mT[:, k, b * P:b * P + rows(b)], wo[:, k, n * 512:(n + 1) * 512],
                                                start=(k == 0), stop=(k == KT - 1))
                    last.then_inc(y_mm, 1)

        @block.scalar
        def _(act):
            with act.Fori(0, KT // 2) as i:
                for b in range(2):
                    j = 2 * i + b
                    act.wait_ge(m_done, 1 + j)
                    for n in range(2):
                        act.wait_ge(proj, 4 * j + n + 1)
                        nc.scalar.activation(sg[:, n, 0:SEQ], big[n][:, :], ACT.Exp, scale=-1.0)
                        if n == 1:
                            act.wait_ge(proj, 4 * j + 4)
                            nc.scalar.activation(sg[:, 0, SEQ:TOK], small[b][:, 0:P], ACT.Exp, scale=-1.0).then_inc(gated, 1)
                            nc.scalar.activation(sg[:, 1, SEQ:TOK], small[b][:, P:2 * P], ACT.Exp, scale=-1.0).then_inc(gated, 1)
            for q in range(4):
                act.wait_ge(spread, q + 1)
                nc.scalar.copy(gs[:, q // 2, (q % 2) * 512:(q % 2 + 1) * 512], psY[q % 2][:, :]).then_inc(spread_sb, 1)

        @block.vector
        def _(dve):
            v = nc.vector
            with dve.Fori(0, KT // 2) as i:
                for b in range(2):
                    j = 2 * i + b
                    dve.wait_ge(gated, 1 + 2 * j + 2)
                    v.tensor_scalar(sg[:, :, :], sg[:, :, :], 1.0, None, ALU.add)
                    dve.drain()
                    v.reciprocal(sg[:, :, :], sg[:, :, :])
                    dve.drain()
                    for n in range(2):
                        v.tensor_tensor(t[:, n, 0:SEQ], big[2 + n][:, :], sg[:, n, 0:SEQ], ALU.mult)
                        last = v.tensor_tensor(t[:, n, SEQ:TOK], small[b][:, (2 + n) * P:(3 + n) * P], sg[:, n, SEQ:TOK], ALU.mult)
                    last.then_inc(summed, 1)
                    dve.drain()
                    v.tensor_tensor(mT[:, j, :], t[:, 0, :], t[:, 1, :], ALU.add).then_inc(m_done, 1)
            dve.wait_ge(spread_sb, 4)
            for b in range(NB):
                r = rows(b)
                for n in range(2):
                    cols = slice(n * 512, (n + 1) * 512)
                    dve.wait_ge(y_mm, 2 * b + n + 1)
                    if n == 0:
                        dve.wait_ge(x_in[b % 2], 16 * (b // 2 + 1))
                    acc = t[:, :, :].rearrange("p a t -> p (a t)")[0:r, n * 512:(n + 1) * 512]
                    v.tensor_tensor(acc, psY[n][0:r, :], gs[0:r, b // PB, cols], ALU.mult)
                    dve.drain()
                    v.tensor_tensor(xb[b % 2][0:r, cols], xb[b % 2][0:r, cols], acc, ALU.add).then_inc(y_sb, 1)


def constants():
    c = {}
    i = np.arange(P)
    c["ident"] = np.eye(P, dtype=np.float32)
    c["tri"] = np.where(i[None, :] <= i[:, None], 0.0, NEG).astype(np.float32)
    tok = np.arange(2 * P)
    owner = np.where(tok < P, 0, np.where(tok - P < SB, 1 + (tok - P) // TD, -1))
    c["sel"] = (owner[None, :] == np.arange(1 + BD)[:, None]).astype(np.float32)
    pos = np.concatenate([np.arange(SEQ), PAGES * PS + np.arange(P) % TD]).astype(np.float32)
    inv = np.float32(10000.0) ** (-np.arange(HALF, dtype=np.float32) / np.float32(HALF))
    ang = (pos[:, None] * inv[None, :]).reshape(NB, P, 1, HALF).transpose(1, 0, 2, 3)
    ang = np.repeat(ang, 2, axis=2)
    c["cos"], c["sin"] = np.cos(ang).astype(np.float32), np.sin(ang).astype(np.float32)
    k = np.arange(SB)
    seen = (k[:, None, None] // TD == np.arange(BD)[None, :, None]) & (k[:, None, None] % TD <= (np.arange(H * TD) % TD)[None, None, :])
    c["own_mask"] = np.where(seen, 0.0, NEG).astype(np.float32)
    a, b = np.meshgrid(i, i, indexing="ij")
    level = lambda n: ((a // (2 * n) == b // (2 * n)) & (a // n % 2 == 0) & (b // n % 2 == 1)).astype(np.float32)
    same = (a // RH == b // RH).astype(np.float32)
    c["chunk_masks"] = np.stack([np.eye(P, dtype=np.float32), same, -same, level(1)] + [level(n) for n in LEVELS], axis=1)
    own = (a // TD == b // TD) & (a < SB) & (b < SB)
    see = [np.concatenate([(a < b) & m, (a <= b) & m] * 2, axis=1) for m in (np.ones((P, P), bool), own)]
    c["see_masks"] = np.stack(see, axis=1).astype(np.int32)
    tok = np.arange(TOK)
    c["segments"] = np.where(tok < SEQ, tok % P != 0, tok % TD != 0).astype(np.float32)
    c["pick"] = ((i[:, None] % SB) // TD == np.arange(BD)[None, :]).astype(np.float32)
    return c


class Shared:
    pass


def free_semaphores(nc, since):
    nc.clear_and_free_semaphores(nc.allocated_since(since))
    nc.all_engine_barrier()


def build(nc, I, O):
    M = Shared()
    M.n_phys = I["cache_kv"].shape[0]
    M.v_dram = nc.dram_tensor("v_scratch", [SEQ, MW], F32, kind="Internal").ap()
    M.qk_dram = nc.dram_tensor("qk_scratch", [2, H, QK, SEQ], F32, kind="Internal").ap()
    M.oa_dram, M.ob_dram = (nc.dram_tensor(n + "_scratch", [P, KT, TOK], F32, kind="Internal").ap() for n in ("oa", "ob"))
    early = nc.snapshot_sems()
    with ExitStack() as whole:
        def hold(stack, name, shape):
            return stack.enter_context(nc.sbuf_tensor(name, shape, F32))

        M.ident = hold(whole, "ident_sb", [P, P])
        M.ones = hold(whole, "ones_sb", [P, P])
        M.hT = hold(whole, "hT", [P, KT, TOK])
        M.gate = hold(whole, "gate", [1 + BD, D])
        with ExitStack() as att:
            M.oaT = hold(att, "oaT", [P, KT, TOK])
            M.cnew, M.cnewT = hold(att, "cnew", [SB, KL + 1]), hold(att, "cnewT", [P, 2, P])
            M.kpenew, M.kpenewT = hold(att, "kpenew", [SB, ROPE]), hold(att, "kpenewT", [ROPE, P])
            M.kinvnew = hold(att, "kinvnew", [SB, H])
            M.zas = hold(att, "zas", [P, NP, SB])
            M.qg, M.qpe = hold(att, "qg", [SB, H, NOPE]), hold(att, "qpe", [SB, H, ROPE])
            with ExitStack() as first:
                M.G1, M.SH = hold(first, "G1", [P, 2, D]), hold(first, "SH", [P, 2, D])
                adaln(nc, I, M)
                front(nc, I, O, M)
            prompt(nc, I, M)
            M.qlT, M.qpT = hold(att, "qlT", [P, 2, BD, H, TD]), hold(att, "qpT", [ROPE, BD, H, TD])
            absorb(nc, I, M)
            sample(nc, I, M)
        with ExitStack() as rw:
            M.masks, M.seg, M.pick = hold(rw, "masks", [P, 4 + len(LEVELS), P]), hold(rw, "seg", [P, TOK]), hold(rw, "pick", [P, BD])
            M.see = rw.enter_context(nc.sbuf_tensor("see", [P, 2, 512], I32))
            M.vec, M.nvec, M.ss = hold(rw, "vec", [P, NVEC]), hold(rw, "nvec", [P, V_KK - V_W0]), hold(rw, "ssT", [P, 25, BD])
            M.shc, M.la, M.mhalf = hold(rw, "shc", [P, 25, 1 + BD]), hold(rw, "la", [P, TOK]), hold(rw, "mhalf", [P, 1])
            free_semaphores(nc, early)
            M.masks_in = nc.alloc_semaphore("masks_in")
            lora(nc, I, O, M)
            rwkv(nc, I, O, M)
            store_shift(nc, O, M)
        free_semaphores(nc, early)
        merge(nc, I, O, M)


_INS = ["x_prompt", "x_sample", "c_prompt", "c_sample", "cache_kv", "cache_kpe", "cache_kinv", "state_wkv", "state_shift",
        "page_table", "w_ada", "b_ada", "g_norm", "w_in", "g_qa", "w_uq", "g_kva", "w_uk", "w_uv", "g_q", "g_k", "w_pa",
        "mu_shift", "w0", "w_decay2", "a0", "w_a2", "k_k", "k_a", "r_k", "gn_g", "gn_b", "w_pb", "w_out"]
_OUTS = {"y_p": (1, SEQ, D), "y_s": (BD, TD, D), "kv_p": (1, SEQ, KL), "kpe_p": (1, SEQ, ROPE), "kinv_p": (1, SEQ, H),
         "wkv_p": (1, H, RH, RH), "shift_p": (1, NSH), "kv_s": (BD, TD, KL), "kpe_s": (BD, TD, ROPE), "kinv_s": (BD, TD, H),
         "wkv_s": (BD, H, RH, RH), "shift_s": (BD, NSH)}


def kernel(**inputs):
    import concourse.bacc as bacc
    from concourse.bass_utils import run_bass_kernel_spmd

    nc = bacc.Bacc("TRN2", target_bir_lowering=False, num_devices=1)
    arrays = {f"in_{name}": np.ascontiguousarray(inputs[name]) for name in _INS}
    arrays.update({f"in_{name}": a for name, a in constants().items()})
    I = {name[3:]: nc.dram_tensor(name, a.shape, mybir.dt.from_np(a.dtype), kind="ExternalInput").ap() for name, a in arrays.items()}
    O = {name: nc.dram_tensor(f"out_{name}", shape, F32, kind="ExternalOutput").ap() for name, shape in _OUTS.items()}
    build(nc, I, O)
    r = run_bass_kernel_spmd(nc, [arrays], core_ids=[0])
    return tuple(r.results[0][f"out_{name}"] for name in _OUTS)
```
